# Optimizing a Trainium2 kernel written in Bass

```python
import jax
import jax.numpy as jnp
from jax import lax

D_MODEL = 1024
BATCH = 1
SEQ = 256
DEPTH = 2

N_A_LAYERS = DEPTH - DEPTH // 2
N_B_LAYERS = DEPTH // 2
N_DENSE = (DEPTH + 1) // 2
N_MOE = DEPTH // 2

HGRN_EXPAND = 128
HGRN_HEADS = D_MODEL // HGRN_EXPAND
HGRN_DV = D_MODEL // HGRN_HEADS
HGRN_CHUNK = 64

ATT_HEAD_DIM = 64
ATT_HEADS = D_MODEL // ATT_HEAD_DIM
DILATED_BRANCHES = ((128, 1), (512, 4), (2048, 16))
N_BRANCH = len(DILATED_BRANCHES)
BAND = DILATED_BRANCHES[0][0] // DILATED_BRANCHES[0][1]
ATT_SCALE = ATT_HEAD_DIM ** -0.5
ROPE_THETA = 10000.0

D_FF = 2816
N_EXPERTS = 8
TOP_K = 2
D_FF_EXPERT = 3584
EPS = 1e-6

kernel_name = "hgrn2_yoco_dilated_moe_trunk"

def rms_norm(x, g):
    xf = x.astype(jnp.float32)
    y = xf * lax.rsqrt(jnp.mean(xf * xf, axis=-1, keepdims=True) + EPS)
    return (y * g.astype(jnp.float32)).astype(x.dtype)

def rope(t, pos):
    half = t.shape[-1] // 2
    inv_freq = ROPE_THETA ** (-jnp.arange(half, dtype=jnp.float32) / half)
    ang = pos.astype(jnp.float32)[:, None] * inv_freq[None, :]
    cos = jnp.cos(ang)[None, :, None, :]
    sin = jnp.sin(ang)[None, :, None, :]
    tf = t.astype(jnp.float32)
    t1, t2 = tf[..., :half], tf[..., half:]
    return jnp.concatenate([t1 * cos - t2 * sin, t2 * cos + t1 * sin], axis=-1)

def swiglu(h, w_gate, w_up, w_down):
    return (jax.nn.silu(h @ w_gate) * (h @ w_up)) @ w_down

def hgrn2_mixer(h, w_in, lower_bound, out_norm, w_out):
    B, S, _ = h.shape
    H, DK, DV, C = HGRN_HEADS, HGRN_EXPAND, HGRN_DV, HGRN_CHUNK
    N = S // C
    q, f_logit, v, g = jnp.split(h @ w_in, 4, axis=-1)
    lb = lower_bound.astype(jnp.float32)
    f = lb + (1.0 - lb) * jax.nn.sigmoid(f_logit.astype(jnp.float32))
    k = 1.0 - f

    def chunks(t):
        return t.astype(jnp.float32).reshape(B, N, C, H, -1).transpose(0, 3, 1, 2, 4)

    q_c, k_c, v_c = chunks(q), chunks(k), chunks(v)
    b = jnp.cumsum(chunks(jnp.log(f)), axis=3)
    b_last = b[:, :, :, -1:, :]
    q_dec = q_c * jnp.exp(b)
    k_dec = k_c * jnp.exp(-b)
    k_end = k_c * jnp.exp(b_last - b)
    causal = jnp.tril(jnp.ones((C, C), dtype=bool))
    scores = jnp.where(causal, jnp.einsum("bhncd,bhnsd->bhncs", q_dec, k_dec), 0.0)
    o_intra = jnp.einsum("bhncs,bhnsv->bhncv", scores, v_c)
    kv_chunk = jnp.einsum("bhnsd,bhnsv->bhndv", k_end, v_c)
    decay = jnp.exp(b_last[:, :, :, 0, :])

    def step(state, inp):
        dcy, kv = inp
        return dcy[..., None] * state + kv, state

    state0 = jnp.zeros((B, H, DK, DV), jnp.float32)
    _, states = lax.scan(step, state0, (jnp.moveaxis(decay, 2, 0), jnp.moveaxis(kv_chunk, 2, 0)))
    o_inter = jnp.einsum("bhncd,nbhdv->bhncv", q_dec, states)
    o = (o_intra + o_inter).transpose(0, 2, 3, 1, 4).reshape(B, S, H, DV)
    o = rms_norm(o, out_norm) * jax.nn.silu(g.astype(jnp.float32)).reshape(B, S, H, DV)
    return o.reshape(B, S, D_MODEL).astype(h.dtype) @ w_out

def dilated_branch(q, k, v, dil):
    B, S, H, D = q.shape
    L = S // dil
    nb = -(-L // BAND)
    Lp = nb * BAND

    def to_blocks(t):
        t = t.reshape(B, L, dil, H, D).transpose(0, 2, 1, 3, 4)
        t = jnp.pad(t, ((0, 0), (0, 0), (0, Lp - L), (0, 0), (0, 0)))
        return t.reshape(B, dil, nb, BAND, H, D)

    def with_prev(t):
        prev = jnp.pad(t[:, :, :-1], ((0, 0), (0, 0), (1, 0), (0, 0), (0, 0), (0, 0)))
        return jnp.concatenate([prev, t], axis=3)

    qb = to_blocks(q)
    kb = with_prev(to_blocks(k))
    vb = with_prev(to_blocks(v))
    s = jnp.einsum("brnqhd,brnkhd->brnhqk", qb, kb)
    qi = jnp.arange(BAND)[:, None]
    ki = jnp.arange(2 * BAND)[None, :]
    dist = qi + BAND - ki
    band_ok = (dist >= 0) & (dist <= BAND)
    valid = band_ok[None] & ((jnp.arange(nb)[:, None, None] > 0) | (ki >= BAND)[None])
    s = jnp.where(valid[None, None, :, None], s, -jnp.inf)
    m = jnp.max(s, axis=-1)
    p = jnp.exp(s - m[..., None])
    l = jnp.sum(p, axis=-1)
    o = jnp.einsum("brnhqk,brnkhd->brnqhd", p, vb) / jnp.swapaxes(l, 3, 4)[..., None]
    lse = jnp.swapaxes(m + jnp.log(l), 3, 4)
    o = o.reshape(B, dil, Lp, H, D)[:, :, :L].transpose(0, 2, 1, 3, 4).reshape(B, S, H, D)
    lse = lse.reshape(B, dil, Lp, H)[:, :, :L].transpose(0, 2, 1, 3).reshape(B, S, H)
    return o, lse

def shared_kv(h, kv_norm, w_kv, pos):
    B, S, _ = h.shape
    kv = (rms_norm(h, kv_norm) @ w_kv).reshape(B, S, 2, N_BRANCH, ATT_HEADS, ATT_HEAD_DIM)
    keys = [rope(kv[:, :, 0, i], pos) for i in range(N_BRANCH)]
    values = [kv[:, :, 1, i].astype(jnp.float32) for i in range(N_BRANCH)]
    return keys, values

def dilated_mixer(h, w_q, w_out, keys, values, pos):
    B, S, _ = h.shape
    q = (h @ w_q).reshape(B, S, N_BRANCH, ATT_HEADS, ATT_HEAD_DIM)
    outs, lses = [], []
    for i, (_, dil) in enumerate(DILATED_BRANCHES):
        o_i, lse_i = dilated_branch(rope(q[:, :, i], pos) * ATT_SCALE, keys[i], values[i], dil)
        outs.append(o_i)
        lses.append(lse_i)
    wts = jax.nn.softmax(jnp.stack(lses, axis=0), axis=0)
    o = jnp.sum(wts[..., None] * jnp.stack(outs, axis=0), axis=0)
    return o.reshape(B, S, D_MODEL).astype(h.dtype) @ w_out

def moe_swiglu(h, w_router, w_gate, w_up, w_down):
    B, S, Dm = h.shape
    t = h.reshape(B * S, Dm)
    probs = jax.nn.softmax((t @ w_router).astype(jnp.float32), axis=-1)
    top_p, top_i = lax.top_k(probs, TOP_K)
    top_p = top_p / jnp.sum(top_p, axis=-1, keepdims=True)
    combine = jnp.sum(jax.nn.one_hot(top_i, N_EXPERTS, dtype=jnp.float32) * top_p[..., None], axis=1).astype(h.dtype)
    out = jnp.zeros_like(t)
    for e in range(N_EXPERTS):
        out = out + combine[:, e:e + 1] * swiglu(t, w_gate[e], w_up[e], w_down[e])
    return out.reshape(B, S, Dm)

def setup_inputs(seed: int = 0) -> dict:
    key = jax.random.key(seed)
    ks = jax.random.split(key, 20)
    f32 = jnp.float32

    def dense(k, shape, fan_in):
        return jax.random.normal(k, shape, f32) * fan_in ** -0.5

    def gain(k, shape):
        return 1.0 + 0.02 * jax.random.normal(k, shape, f32)

    att_w = ATT_HEADS * ATT_HEAD_DIM
    return {
        "x": jax.random.normal(ks[0], (BATCH, SEQ, D_MODEL), f32),
        "attn_norm": gain(ks[1], (DEPTH, D_MODEL)),
        "ffn_norm": gain(ks[2], (DEPTH, D_MODEL)),
        "hgrn_w_in": dense(ks[3], (N_A_LAYERS, D_MODEL, 4 * D_MODEL), D_MODEL),
        "hgrn_lower_bounds": 0.1 * jax.random.normal(ks[4], (N_A_LAYERS + 1, D_MODEL), f32),
        "hgrn_out_norm": gain(ks[5], (N_A_LAYERS, HGRN_DV)),
        "hgrn_w_out": dense(ks[6], (N_A_LAYERS, D_MODEL, D_MODEL), D_MODEL),
        "kv_norm": gain(ks[7], (D_MODEL,)),
        "w_kv": dense(ks[8], (D_MODEL, 2 * N_BRANCH * att_w), D_MODEL),
        "dil_w_q": dense(ks[9], (N_B_LAYERS, D_MODEL, N_BRANCH * att_w), D_MODEL),
        "dil_w_out": dense(ks[10], (N_B_LAYERS, att_w, D_MODEL), att_w),
        "ffn_w_gate": dense(ks[11], (N_DENSE, D_MODEL, D_FF), D_MODEL),
        "ffn_w_up": dense(ks[12], (N_DENSE, D_MODEL, D_FF), D_MODEL),
        "ffn_w_down": dense(ks[13], (N_DENSE, D_FF, D_MODEL), D_FF),
        "moe_w_router": dense(ks[14], (N_MOE, D_MODEL, N_EXPERTS), D_MODEL),
        "moe_w_gate": dense(ks[15], (N_MOE, N_EXPERTS, D_MODEL, D_FF_EXPERT), D_MODEL),
        "moe_w_up": dense(ks[16], (N_MOE, N_EXPERTS, D_MODEL, D_FF_EXPERT), D_MODEL),
        "moe_w_down": dense(ks[17], (N_MOE, N_EXPERTS, D_FF_EXPERT, D_MODEL), D_FF_EXPERT),
        "final_norm": gain(ks[18], (D_MODEL,)),
    }

def reference(x, attn_norm, ffn_norm, hgrn_w_in, hgrn_lower_bounds, hgrn_out_norm, hgrn_w_out,
              kv_norm, w_kv, dil_w_q, dil_w_out, ffn_w_gate, ffn_w_up, ffn_w_down,
              moe_w_router, moe_w_gate, moe_w_up, moe_w_down, final_norm):
    pos = jnp.arange(x.shape[1])
    lbs = jnp.cumsum(jax.nn.softmax(hgrn_lower_bounds.astype(jnp.float32), axis=0), axis=0)
    h = x
    keys, values = None, None
    for layer in range(DEPTH):
        if layer == N_A_LAYERS:
            keys, values = shared_kv(h, kv_norm, w_kv, pos)
        hn = rms_norm(h, attn_norm[layer])
        if layer < N_A_LAYERS:
            h = h + hgrn2_mixer(hn, hgrn_w_in[layer], lbs[layer], hgrn_out_norm[layer], hgrn_w_out[layer])
        else:
            j = layer - N_A_LAYERS
            h = h + dilated_mixer(hn, dil_w_q[j], dil_w_out[j], keys, values, pos)
        hn = rms_norm(h, ffn_norm[layer])
        if layer % 2 == 0:
            i = layer // 2
            h = h + swiglu(hn, ffn_w_gate[i], ffn_w_up[i], ffn_w_down[i])
        else:
            i = layer // 2
            h = h + moe_swiglu(hn, moe_w_router[i], moe_w_gate[i], moe_w_up[i], moe_w_down[i])
    return rms_norm(h, final_norm)


_drawn_inputs = setup_inputs


def setup_inputs(seed=0):
    import zlib

    import numpy as np

    out = dict(_drawn_inputs(seed))
    spreads = {}
    factors = {'kv_norm': 2.701, 'final_norm': 2.905}
    for name, (base, spread) in spreads.items():
        noise = np.random.default_rng([zlib.crc32(name.encode()), seed]).standard_normal(out[name].shape)
        drawn = base * np.exp(spread * noise) if base else spread * noise
        out[name] = jnp.asarray(drawn.astype(out[name].dtype))
    for name, factor in factors.items():
        out[name] = (out[name] * factor).astype(out[name].dtype)
    return out
```

```python
from contextlib import ExitStack

import numpy as np

import concourse.bass as bass
from concourse import mybir

ACT = mybir.ActivationFunctionType
ALU = mybir.AluOpType
AX = mybir.AxisListType
F32 = mybir.dt.float32
I32 = mybir.dt.int32
U32 = mybir.dt.uint32

P = 128
D = 1024
S = 256
KT = D // P
TT = S // P
CHUNK = 64
HEAD = 64
NBR = 3
DILS = (1, 4, 16)
BAND = 128
DFF = 2816
DEXP = 3584
NEXP = 8
CAP = 96
EXTRA = (2 * S) // (CAP + 1)
BLOCKS = -(-S // CAP) - 1
ITEMS = NEXP + EXTRA + 1
EPS = 1e-6
SCALE = HEAD ** -0.5
ABSENT = -1000.0
LNEXP_SET = 6
FF_PAIRS = DFF // 256
EXP_PAIRS = DEXP // 256
GROUPS = 4
UNITS = 8
SLOTS = 14
SLOT = 2048

HG_SLOTS = dict(f=0, q=1, v=2, g=3)
HG_OUT = (4, 5, 6, 7)
FF_SLOTS = dict(gate=8, up=9, down=10)
AT_SLOTS = (0, 1, 2, 3, 4, 5, 6, 7, 11)
AT_OUT = (8, 9, 10, 12)
MOE_ORDER = (13, 0, 1, 2, 3, 4, 5, 6, 7, 11, 8, 9, 10, 12)
BEFORE_ATT = {s: (4 if s < 4 else 1 if s < 8 else 0) for s in AT_SLOTS}
BEFORE_ATO = {8: FF_PAIRS, 9: FF_PAIRS, 10: FF_PAIRS, 12: 0}
BEFORE_MOE = {**{s: n + GROUPS for s, n in BEFORE_ATT.items()}, **{s: n + 1 for s, n in BEFORE_ATO.items()}, 13: 0}
ROUNDS = 3 * EXP_PAIRS // SLOTS

CONSTS = {}
_at = 0
for _name, _n in (("ident", P), ("ustrict", P), ("ones", P), ("hgmask", P), ("reset", 2 * S), ("places", CAP),
                  ("experts", NEXP), ("over_k", EXTRA * BLOCKS * NEXP), ("over_e", BLOCKS * NEXP),
                  ("over_base", BLOCKS * NEXP), ("eps", 1), ("cos", S), ("sin", S),
                  ("mask0", NBR * P), ("mask1", NBR * S)):
    CONSTS[_name] = (_at, _at + _n)
    _at += _n
NCONST = _at
PARAMS = {}
_at = 0
for _name, _n in (("attn_norm", 2 * KT), ("ffn_norm", 2 * KT), ("kv_norm", KT), ("bounds", 2 * KT),
                  ("router", KT * NEXP), ("out_norm", P), ("final_norm", D)):
    PARAMS[_name] = (_at, _at + _n)
    _at += _n
NPARAM = _at


def constants():
    c = np.zeros((P, NCONST), np.float32)

    def put(name, value):
        a, b = CONSTS[name]
        c[:, a:b] = np.broadcast_to(np.asarray(value, np.float32), (P, b - a))

    r = np.arange(P)
    put("ident", np.eye(P))
    put("ustrict", r[:, None] < r[None, :])
    put("ones", np.ones((P, P)))
    put("hgmask", (r[:, None] <= r[None, :]) & (r[:, None] // CHUNK == r[None, :] // CHUNK))
    put("reset", (np.arange(2 * S) % CHUNK != 0)[None])
    put("places", np.arange(CAP)[None])
    put("experts", np.arange(NEXP)[None])
    nj = BLOCKS * NEXP
    put("over_k", np.repeat(np.arange(EXTRA), nj)[None])
    put("over_e", np.tile(np.arange(NEXP) + 1, BLOCKS)[None])
    put("over_base", (CAP * (1 + np.repeat(np.arange(BLOCKS), NEXP)))[None])
    put("eps", np.full((P, 1), EPS))
    half = HEAD // 2
    inv = np.float32(10000.0) ** (-np.arange(half, dtype=np.float32) / np.float32(half))
    ang = np.arange(S, dtype=np.float32)[None, :] * inv[:, None].astype(np.float32)
    put("cos", np.tile(np.cos(ang), (4, 1)))
    put("sin", np.concatenate([np.sin(ang), -np.sin(ang)] * 2, 0))
    for tt, name in ((0, "mask0"), (1, "mask1")):
        q = tt * P + r[:, None]
        k = np.arange((tt + 1) * P)[None, :]
        ok = [(k <= q) & ((q - k) % dil == 0) & (q - k <= BAND * dil) for dil in DILS]
        put(name, np.concatenate([np.where(m, 0.0, -1e30) for m in ok], 1))
    return c


class Chain:

    def __init__(self, eng, sem):
        self.eng, self.sem, self.base, self.n, self.i, self.per = eng, sem, 0, 0, 0, 0

    def __call__(self, ins):
        self.n += 1
        ins.then_inc(self.sem, 1)
        self.eng.wait_ge(self.sem, self.i * self.per + (self.base + self.n))

    def enter(self, i, per):
        self.base, self.n, self.i, self.per = self.base + self.n, 0, i, per

    def leave(self, trips):
        assert self.n == self.per, (self.n, self.per)
        self.base, self.n, self.i, self.per = self.base + trips * self.per, 0, 0, 0


def trunk_kernel(nc, t, consts, params, out):
    with ExitStack() as ctx:
        def sb(name, shape, dt=F32):
            return ctx.enter_context(nc.sbuf_tensor(name, shape, dt))

        def sem(name):
            return ctx.enter_context(nc.semaphore(name))

        ring = sb("ring", [P, SLOTS, SLOT])
        cst = sb("cst", [P, NCONST])
        par = sb("par", [P, NPARAM])
        h = sb("h", [P, TT, D])
        hn = sb("hn", [P, TT, D])
        hT = sb("hT", [P, KT, S])
        mixed = sb("mixed", [P, TT, D])
        mixedT = sb("mixedT", [P, KT, S])
        ssq = sb("ssq", [P, TT])
        rstd = sb("rstd", [P, TT])
        arena_floats = 9472
        arena = sb("arena", [P, arena_floats])
        table = sb("table", [P, EXTRA + 2], I32)

        def carve():
            used = [0]

            def take(*shape):
                n = int(np.prod(shape))
                a = arena[:, used[0]:used[0] + n]
                used[0] += n
                assert used[0] <= arena_floats, used
                names = "abc"[:len(shape)]
                if len(shape) == 1:
                    return a
                return a.rearrange(f"p ({' '.join(names)}) -> p {' '.join(names)}", **dict(zip(names, shape)))
            return take

        ps = ctx.enter_context(nc.psum_tensor("ps", [P, 8 * 512], F32))

        def bank(b, n=512):
            return ps[:, 512 * b:512 * b + n]

        def chunk_kv(hh, n):
            c = (2 * hh + n // 2) * P if n % 2 == 0 else hh * P
            return bank(6 + n % 2)[:, c:c + P]

        def cc(name):
            a, b = CONSTS[name]
            return cst[:, a:b]

        def pp(name):
            a, b = PARAMS[name]
            return par[:, a:b]

        ident, eps = cc("ident"), cc("eps")
        attn_gain = pp("attn_norm").rearrange("p (l k) -> p l k", l=2)
        ffn_gain = pp("ffn_norm").rearrange("p (l k) -> p l k", l=2)
        kv_gain = pp("kv_norm")
        bounds = pp("bounds").rearrange("p (l k) -> p l k", l=2)
        router = pp("router").rearrange("p (k e) -> p k e", k=KT)

        def cols(s):
            return ring[:, s, :].rearrange("p (k n) -> p k n", k=KT)

        def rows(s):
            return ring[:, s, :].rearrange("p (k n) -> p k n", k=2)

        take = carve()
        decay_in = take(2, S)
        forget = take(2, S)
        keyk = take(2, S)
        logf = take(2, S)
        bsum = take(2, S)
        bdiff = take(2, S)
        eb = take(2, S)
        enb = take(2, S)
        eend = take(2, S)
        qdec = take(2, S)
        kdec = take(2, S)
        kend = take(2, S)
        kend_tok = take(2, TT, P)
        v_hg = take(TT, 2 * P)
        scores_hg = take(2, TT, P)
        states = take(2, 3, P)
        gate_hg = take(TT, 2 * P)
        square_hg = take(TT, 2 * P)
        lbound = sb("lbound", [P, 4, KT])
        ossq = sb("ossq", [P, 4, TT, 2])
        orstd = sb("orstd", [P, 4, TT, 2])
        take = carve()
        silu_ff = take(2, S)
        act_ff = take(2, S)
        take = carve()
        hTkv = take(KT, S)
        kbuf = [take(2, S) for _ in range(NBR)]
        qbuf = [take(2, S) for _ in range(NBR)]
        vbuf = take(TT, NBR, 256)
        rot = take(2, S)
        prob = [take(NBR * P), take(NBR * S)]
        probT = [take(NBR, P), take(NBR * 2, P)]
        rowmax = sb("rowmax", [P, UNITS])
        negmax = sb("negmax", [P, UNITS])
        rowsum = sb("rowsum", [P, UNITS])
        rowinv = sb("rowinv", [P, UNITS])
        take = carve()
        logits = take(TT, NEXP)
        probs = take(TT, NEXP)
        top = take(TT, 8)
        topi = take(TT, 8).bitcast(U32)
        topf = take(TT, 8)
        r1 = take(8)
        onehot = take(TT, NEXP)
        wa = take(TT, NEXP)
        chosen = take(TT, NEXP)
        place = take(TT, NEXP)
        key = take(ITEMS, TT)
        weight = take(ITEMS, TT)
        nj = BLOCKS * NEXP
        counts = take(NEXP)
        active = take(nj)
        order = take(nj)
        sel = take(EXTRA, nj)
        prod = take(EXTRA, nj)
        keymod = take(TT, nj)
        tablef = take(EXTRA + 2)
        gatherP = take(TT, CAP)
        scatterP = take(TT, CAP)
        scatterT = take(S)
        xeT = take(KT, CAP)
        silu_e = [take(2, CAP), take(2, CAP)]
        act_e = [take(2, CAP), take(2, CAP)]
        yT = take(KT, CAP)
        ytok = take(D)

        slot_filled = [sem(f"slot_filled{s}") for s in range(SLOTS)]
        consts_in, params_in, x_in, out_stored = sem("consts_in"), sem("params_in"), sem("x_in"), sem("out_stored")
        act_own, dve_own, pool_own = sem("act_own"), sem("dve_own"), sem("pool_own")
        act_own_end, dve_own_end = sem("act_own_end"), sem("dve_own_end")
        bounds_shifted, bounds_exp = sem("bounds_shifted"), sem("bounds_exp")
        zeroed = sem("zeroed")
        NN = 5
        rstd_ready = [sem(f"rstd_ready{n}") for n in range(NN)]
        hn_ready = [sem(f"hn_ready{n}") for n in range(NN)]
        hn_transposed = [sem(f"hn_transposed{n}") for n in range(NN)]
        hT_ready = [sem(f"hT_ready{n}") for n in range(NN)]
        h_ready = [sem(f"h_ready{n}") for n in range(NN)]
        f_proj, q_proj, v_proj, g_proj = sem("f_proj"), sem("q_proj"), sem("v_proj"), sem("g_proj")
        f_exp, f_done, f_log, b_done = sem("f_exp"), sem("f_done"), sem("f_log"), sem("b_done")
        bdiff_done, b_exps, bend_exp = sem("bdiff_done"), sem("b_exps"), sem("bend_exp")
        decayed, kend_transposed, kend_copied = sem("decayed"), sem("kend_transposed"), sem("kend_copied")
        v_copied, scores_hg_ready, scores_hg_masked = sem("v_copied"), sem("scores_hg_ready"), sem("scores_hg_masked")
        kv_ready, states_ready, g_exp = sem("kv_ready"), sem("states_ready"), sem("g_exp")
        o_ready, o_squared, o_gated = sem("o_ready"), sem("o_squared"), sem("o_gated")
        orstd_ready = sem("orstd_ready")
        mixed_ready = sem("mixed_ready")
        mixed_transposed = [sem("mixed_transposed0"), sem("mixed_transposed1")]
        mixedT_ready = [sem("mixedT_ready0"), sem("mixedT_ready1")]
        proj_out = [sem("proj_out0"), sem("proj_out1")]
        ff_gate, ff_up, ff_silu, ff_act, ff_down, ff_sum = (sem(n) for n in (
            "ff_gate", "ff_up", "ff_silu", "ff_act", "ff_down", "ff_sum"))
        kq_proj, kq_read, rope_parts, rope_done = sem("kq_proj"), sem("kq_read"), sem("rope_parts"), sem("rope_done")
        va_proj, va_copied = sem("va_proj"), sem("va_copied")
        s_ready, max_ready, exp_ready = sem("s_ready"), sem("max_ready"), sem("exp_ready")
        pT_ready, pT_dve, pT_act, pv_ready, o_evac = (sem("pT_ready"), sem("pT_dve"), sem("pT_act"), sem("pv_ready"),
                                                      sem("o_evac"))
        logits_ready, shifted, exped, chosen_ready, places_ready = (
            sem("logits_ready"), sem("shifted"), sem("exped"), sem("chosen_ready"), sem("places_ready"))
        table_ready = sem("table_ready")
        built, gathered, xe_ready = sem("built"), sem("gathered"), sem("xe_ready")
        sT_transposed, sT_ready = sem("sT_transposed"), sem("sT_ready")
        gate_used, gu_ready, down_used = sem("gate_used"), sem("gu_ready"), sem("down_used")
        silu_done, act_done = sem("silu_done"), sem("act_done")
        yT_act, yT_dve, y_transposed, yt_act, yt_dve = (sem("yT_act"), sem("yT_dve"), sem("y_transposed"),
                                                        sem("yt_act"), sem("yt_dve"))
        scattered, added = sem("scattered"), sem("added")
        normed = sem("normed")

        w_in = t["hgrn_w_in"][0].rearrange("(k p) n -> p k n", p=P)
        w_kv = t["w_kv"].rearrange("(k p) n -> p k n", p=P)
        w_q = t["dil_w_q"][0].rearrange("(k p) n -> p k n", p=P)
        hg_out = t["hgrn_w_out"][0].rearrange("(k p) n -> p k n", p=P)
        at_out = t["dil_w_out"][0].rearrange("(k p) n -> p k n", p=P)
        ff_g = t["ffn_w_gate"][0].rearrange("(k p) n -> p k n", p=P)
        ff_u = t["ffn_w_up"][0].rearrange("(k p) n -> p k n", p=P)
        ff_d = t["ffn_w_down"][0].rearrange("(k p) n -> p k n", p=P)
        moe_g = t["moe_w_gate"][0].rearrange("e (k p) n -> e p k n", p=P)
        moe_u = t["moe_w_up"][0].rearrange("e (k p) n -> e p k n", p=P)
        moe_d = t["moe_w_down"][0].rearrange("e (k p) n -> e p k n", p=P)
        x_tok = t["x"][0].rearrange("(t p) d -> p t d", p=P)
        out_tok = out[0].rearrange("(t p) d -> p t d", p=P)

        block = ctx.enter_context(nc.Block())

        @block.sync
        def _(sp):
            def load(s, dst, src):
                sp.dma_start(dst, src).then_inc(slot_filled[s], 16)

            def fill_hg(p, first=False):
                order = (1, 0, 2, 3) if first else (0, 1, 2, 3)
                for c in order:
                    name, used = (("q", q_proj), ("f", f_proj), ("v", v_proj), ("g", g_proj))[c]
                    if not first:
                        sp.wait_ge(used, p)
                    load(HG_SLOTS[name], cols(HG_SLOTS[name]), w_in[:, :, bass.ds(p * 256 + c * D, 256)])

            def fill_ff(i, first=False):
                for name, w, used in (("gate", ff_g, ff_gate), ("up", ff_u, ff_up)):
                    if not first:
                        sp.wait_ge(used, i)
                    load(FF_SLOTS[name], cols(FF_SLOTS[name]), w[:, :, bass.ds(i * 256, 256)])
                if not first:
                    sp.wait_ge(ff_down, i)
                load(FF_SLOTS["down"], rows(FF_SLOTS["down"]), ff_d[:, bass.ds(i * 2, 2), :])

            def fill_att(g, first=False):
                for j, s in enumerate(AT_SLOTS):
                    if first:
                        if s < 4:
                            sp.wait_ge((f_proj, q_proj, v_proj, g_proj)[s], 4)
                        elif s < 8:
                            sp.wait_ge(proj_out[0], 2 * TT)
                    elif j < 2 * NBR:
                        sp.wait_ge(kq_proj, g * (2 * NBR) + (j + 1 - 2 * NBR))
                    else:
                        sp.wait_ge(va_proj, g * NBR + (j + 1 - 3 * NBR))
                    w, c = ((w_kv, 0), (w_q, 0), (w_kv, NBR * D))[j // NBR]
                    load(s, cols(s), w[:, :, bass.ds(g * 256 + (c + j % NBR * D), 256)])

            def fill_moe(item, e, start=0, first=False):
                for j in range(start, 3 * EXP_PAIRS):
                    s, pair, last = MOE_ORDER[j % SLOTS], j // 3, j - SLOTS
                    if first and last < 0:
                        if s in AT_SLOTS[:2 * NBR]:
                            sp.wait_ge(kq_proj, 2 * NBR * (GROUPS - 1) + AT_SLOTS.index(s) + 1)
                        elif s in AT_SLOTS:
                            sp.wait_ge(va_proj, NBR * (GROUPS - 1) + AT_SLOTS.index(s) - 2 * NBR + 1)
                        elif s in AT_OUT:
                            sp.wait_ge(proj_out[1], 2 * TT)
                    else:
                        back = 3 * EXP_PAIRS if last < 0 else 0
                        used = (gate_used, gu_ready, down_used)[(last + back) % 3]
                        sp.wait_ge(used, item * EXP_PAIRS + ((last + back) // 3 + 1 - (EXP_PAIRS if back else 0)))
                    if j % 3 == 2:
                        load(s, rows(s), moe_d[e, :, 2 * pair:2 * pair + 2, :])
                    else:
                        load(s, cols(s), (moe_g, moe_u)[j % 3][e, :, :, 256 * pair:256 * pair + 256])

            for tt in range(TT):
                sp.dma_start(h[:, tt, :], x_tok[:, tt, :]).then_inc(x_in, 16)
            sp.dma_start(cst[:, :], consts).then_inc(consts_in, 16)
            sp.dma_start(par[:, :], params).then_inc(params_in, 16)
            fill_hg(0, first=True)
            for j, s in enumerate(HG_OUT):
                load(s, rows(s), hg_out[:, 2 * j:2 * j + 2, :])
            fill_ff(0, first=True)
            with sp.Fori(0, 3) as p:
                fill_hg(p + 1)
            with sp.Fori(0, FF_PAIRS - 1) as i:
                fill_ff(i + 1)
            fill_att(0, first=True)
            for j, s in enumerate(AT_OUT):
                if s != 12:
                    sp.wait_ge((ff_gate, ff_up, ff_sum)[s - 8], (FF_PAIRS, FF_PAIRS, TT)[s - 8])
                load(s, rows(s), at_out[:, 2 * j:2 * j + 2, :])
            load(MOE_ORDER[0], cols(MOE_ORDER[0]), moe_g[0, :, :, 0:256])
            with sp.Fori(0, GROUPS - 1) as g:
                fill_att(g + 1)
            fill_moe(0, 0, start=1, first=True)
            with sp.Fori(0, NEXP - 1) as e:
                fill_moe(e + 1, e + 1)
            sp.wait_ge(table_ready, 1)
            more = sp.value_load(table[0:1, EXTRA:EXTRA + 1], min_val=0, max_val=EXTRA)
            with sp.If(more > 0):
                with sp.Fori(0, more) as k:
                    e = sp.value_load(table[0:1, bass.ds(k, 1)], min_val=1, max_val=NEXP)
                    fill_moe(k + NEXP, e - 1)
            for tt in range(TT):
                sp.wait_ge(normed, tt + 1)
                sp.dma_start(out_tok[:, tt, :], hn[:, tt, :]).then_inc(out_stored, 16)
            sp.wait_ge(out_stored, 16 * TT)

        @block.tensor
        def _(pe):
            mm = nc.tensor.matmul

            def transposed_norm(n):
                for tt in range(TT):
                    pe.wait_ge(hn_ready[n], tt + 1)
                    for k in range(KT):
                        b = 4 + 2 * tt + k // 4
                        last = nc.tensor.transpose(bank(b)[:, (k % 4) * P:(k % 4 + 1) * P], hn[:, tt, k * P:(k + 1) * P], ident)
                        if k % 4 == 3:
                            last.then_inc(hn_transposed[n], 1)

            def feature_major(b, s, src):
                for half in range(2):
                    for k in range(KT):
                        last = mm(bank(b)[:, half * S:(half + 1) * S], cols(s)[:, k, half * P:(half + 1) * P], src[:, k, :],
                                  start=(k == 0), stop=(k == KT - 1))
                return last

            def token_major(b, s, src, tt):
                for k in range(KT):
                    last = mm(bank(b)[:, tt * 256:(tt + 1) * 256], src[:, k, tt * P:(tt + 1) * P], cols(s)[:, k, :],
                              start=(k == 0), stop=(k == KT - 1))
                return last

            def mixer_projection(m, slots, before, mixed_is_ready):
                for tt in range(TT):
                    pe.wait_ge(*mixed_is_ready[tt])
                    for k in range(KT):
                        b = 4 + 2 * tt + k // 4
                        last = nc.tensor.transpose(bank(b)[:, (k % 4) * P:(k % 4 + 1) * P], mixed[:, tt, k * P:(k + 1) * P], ident)
                        if k % 4 == 3:
                            last.then_inc(mixed_transposed[m], 1)
                for tt in range(TT):
                    pe.wait_ge(mixedT_ready[m], 2 * tt + 2)
                    for k in range(KT):
                        s = slots[k // 2]
                        if tt == 0 and k % 2 == 0:
                            pe.wait_ge(slot_filled[s], 16 * (before[s] + 1))
                        for half in range(2):
                            last = mm(bank(2 * tt + half), mixedT[:, k, tt * P:(tt + 1) * P],
                                      rows(s)[:, k % 2, half * 512:(half + 1) * 512], start=(k == 0), stop=(k == KT - 1))
                            if k == KT - 1:
                                last.then_inc(proj_out[m], 1)

            pe.wait_ge(consts_in, 16)
            transposed_norm(0)
            pe.wait_ge(hT_ready[0], 2 * TT)
            with pe.Fori(0, 4) as p:
                for name, b, done in (("f", 0, f_proj), ("q", 1, q_proj)):
                    s = HG_SLOTS[name]
                    pe.wait_ge(slot_filled[s], p * 16 + 16)
                    feature_major(b, s, hT).then_inc(done, 1)
                s = HG_SLOTS["v"]
                pe.wait_ge(slot_filled[s], p * 16 + 16)
                for tt in range(TT):
                    last = token_major(2, s, hT, tt)
                last.then_inc(v_proj, 1)
                pe.wait_ge(decayed, p * 2 + 1)
                for hh in range(2):
                    for tt in range(TT):
                        c = (2 * hh + tt) * P
                        last = mm(bank(5)[:, c:c + P], kdec[:, hh, tt * P:(tt + 1) * P], qdec[:, hh, tt * P:(tt + 1) * P],
                                  start=True, stop=True)
                last.then_inc(scores_hg_ready, 1)
                pe.wait_ge(decayed, p * 2 + 2)
                pe.wait_ge(o_gated, p + 1)
                for hh in range(2):
                    for tt in range(TT):
                        c = (2 * hh + tt) * P
                        last = nc.tensor.transpose(bank(4)[:, c:c + P], kend[:, hh, tt * P:(tt + 1) * P], ident)
                last.then_inc(kend_transposed, 1)
                s = HG_SLOTS["g"]
                pe.wait_ge(slot_filled[s], p * 16 + 16)
                token_major(3, s, hT, 0)
                pe.wait_ge(kend_copied, p + 1)
                pe.wait_ge(v_copied, p + 1)
                for hh in range(2):
                    for n in range(3):
                        q0 = CHUNK * (n % 2)
                        last = mm(chunk_kv(hh, n), kend_tok[q0:q0 + CHUNK, hh, n // 2, :],
                                  v_hg[q0:q0 + CHUNK, n // 2, hh * P:(hh + 1) * P], start=True, stop=True)
                last.then_inc(kv_ready, 1)
                token_major(3, s, hT, 1).then_inc(g_proj, 1)
                pe.wait_ge(scores_hg_masked, p + 1)
                pe.wait_ge(states_ready, p + 1)
                for tt in range(TT):
                    for hh in range(2):
                        o = bank(4)[:, (2 * tt + hh) * P:(2 * tt + hh + 1) * P]
                        last = mm(o, scores_hg[:, hh, tt, :], v_hg[:, tt, hh * P:(hh + 1) * P], start=True, stop=False,
                                  skip_group_check=True)
                        for n in (2 * tt, 2 * tt + 1):
                            if n == 0:
                                continue
                            q0 = CHUNK * (n % 2)
                            last = mm(o[q0:q0 + CHUNK, :], qdec[:, hh, n * CHUNK:(n + 1) * CHUNK], states[:, hh, n - 1, :],
                                      start=False, stop=(n % 2 == 1), skip_group_check=True)
                last.then_inc(o_ready, 1)
            mixer_projection(0, HG_OUT, dict.fromkeys(HG_OUT, 0), [(mixed_ready, tt + 1) for tt in range(TT)])

            transposed_norm(1)

            def ff_part(name, b, i, done):
                s = FF_SLOTS[name]
                pe.wait_ge(slot_filled[s], i * 16 + 16)
                feature_major(b, s, hT).then_inc(done, 1)

            def ff_downs(i, start=False, stop=False):
                s = FF_SLOTS["down"]
                pe.wait_ge(slot_filled[s], i * 16 + 16)
                pe.wait_ge(ff_act, i + 1)
                for tt in range(TT):
                    for f in range(2):
                        for half in range(2):
                            last = mm(bank(2 * tt + half), act_ff[:, f, tt * P:(tt + 1) * P],
                                      rows(s)[:, f, half * 512:(half + 1) * 512], start=start and f == 0,
                                      stop=stop and f == 1, skip_group_check=True)
                    if stop:
                        last.then_inc(ff_sum, 1)
                if not stop:
                    last.then_inc(ff_down, 1)

            pe.wait_ge(hT_ready[1], 2 * TT)
            ff_part("gate", 4, 0, ff_gate)
            ff_part("up", 5, 0, ff_up)
            pe.wait_ge(ff_silu, 1)
            ff_part("gate", 4, 1, ff_gate)
            ff_downs(0, start=True)
            ff_part("up", 5, 1, ff_up)
            with pe.Fori(2, FF_PAIRS) as i:
                pe.wait_ge(ff_silu, i)
                ff_part("gate", 4, i, ff_gate)
                ff_downs(i - 1)
                ff_part("up", 5, i, ff_up)
            ff_downs(FF_PAIRS - 1, stop=True)

            transposed_norm(2)
            pe.wait_ge(hT_ready[2], 4 * TT)
            with pe.Fori(0, GROUPS) as g:
                for j in range(2 * NBR):
                    s = AT_SLOTS[j]
                    pe.wait_ge(slot_filled[s], g * 16 + 16 * (BEFORE_ATT[s] + 1))
                    if j >= 2:
                        pe.wait_ge(kq_read, g * 6 + (j - 1))
                    feature_major(j % 2, s, hTkv if j < NBR else hT).then_inc(kq_proj, 1)

                def v_slot(b):
                    s = AT_SLOTS[2 * NBR + b]
                    pe.wait_ge(slot_filled[s], g * 16 + 16 * (BEFORE_ATT[s] + 1))
                    if b < 2:
                        pe.wait_ge(kq_read, g * 6 + (5 + b))
                    else:
                        pe.wait_ge(va_copied, g * 3 + 1)
                    for tt in range(TT):
                        last = token_major(b % 2, s, hTkv, tt)
                    last.then_inc(va_proj, 1)

                def scores(u):
                    hd, qt = u // 2, u % 2
                    a = HEAD * (hd % 2)
                    n = (qt + 1) * P
                    for b in range(NBR):
                        c = 512 * (2 + qt) + b * n
                        last = mm(ps[:, c:c + n], qbuf[b][a:a + HEAD, hd // 2, qt * P:(qt + 1) * P],
                                  kbuf[b][a:a + HEAD, hd // 2, 0:n], start=True, stop=True)
                    last.then_inc(s_ready, 1)

                def turn(u):
                    qt = u % 2
                    pe.wait_ge(exp_ready, g * UNITS + (u + 1))
                    if u:
                        pe.wait_ge(pT_dve, g * UNITS + u)
                        pe.wait_ge(pT_act, g * (UNITS // 2) + u // 2)
                    for j in range(NBR * (qt + 1)):
                        last = nc.tensor.transpose(ps[:, 512 * 5 + j * P:512 * 5 + (j + 1) * P], prob[qt][:, j * P:(j + 1) * P], ident)
                    last.then_inc(pT_ready, 1)

                def values(u):
                    hd, qt = u // 2, u % 2
                    pe.wait_ge(pT_dve, g * UNITS + (u + 1))
                    pe.wait_ge(pT_act, g * (UNITS // 2) + (u + 1) // 2)
                    if u:
                        pe.wait_ge(o_evac, g * UNITS + u)
                    n = NBR * (qt + 1)
                    for j in range(n):
                        b, kt = j // (qt + 1), j % (qt + 1)
                        last = mm(bank(7)[:, 0:HEAD], probT[qt][:, j, :], vbuf[:, kt, b, hd * HEAD:(hd + 1) * HEAD],
                                  start=(j == 0), stop=(j == n - 1))
                    last.then_inc(pv_ready, 1)

                pe.wait_ge(rope_done, g * 6 + 6)
                scores(0)
                v_slot(0)
                scores(1)
                v_slot(1)
                turn(0)
                v_slot(2)
                pe.wait_ge(va_copied, g * 3 + 3)
                for u in range(2, UNITS + 2):
                    if u < UNITS:
                        scores(u)
                    if u - 1 < UNITS:
                        turn(u - 1)
                    values(u - 2)
            mixer_projection(1, AT_OUT, BEFORE_ATO, [(o_evac, GROUPS * UNITS)] * TT)

            transposed_norm(3)
            pe.wait_ge(hT_ready[3], 2 * TT)
            for tt in range(TT):
                for k in range(KT):
                    last = mm(bank(0)[:, tt * NEXP:(tt + 1) * NEXP], hT[:, k, tt * P:(tt + 1) * P], router[:, k, :],
                              start=(k == 0), stop=(k == KT - 1))
            last.then_inc(logits_ready, 1)
            pe.wait_ge(chosen_ready, 1)
            ones, ustrict = cc("ones"), cc("ustrict")
            mm(bank(1)[:, 0:NEXP], ustrict, chosen[:, 0, :], start=True, stop=True)
            for c, w in ((1, ustrict), (2, ones)):
                mm(bank(1)[:, c * NEXP:(c + 1) * NEXP], ones, chosen[:, 0, :], start=True, stop=False)
                last = mm(bank(1)[:, c * NEXP:(c + 1) * NEXP], w, chosen[:, 1, :], start=False, stop=True)
            last.then_inc(places_ready, 1)

            def gather():
                for k in range(KT):
                    for tt in range(TT):
                        last = mm(bank(4 + k // 4)[:, (k % 4) * CAP:(k % 4 + 1) * CAP], hn[:, tt, k * P:(k + 1) * P],
                                  gatherP[:, tt, :], start=(tt == 0), stop=(tt == TT - 1))
                last.then_inc(gathered, 1)

            pe.wait_ge(built, 1)
            gather()
            pe.wait_ge(table_ready, 1)
            items = pe.value_load(table[0:1, EXTRA + 1:EXTRA + 2], min_val=NEXP, max_val=NEXP + EXTRA)
            with pe.Fori(0, items) as i:
                def slot_of(j):
                    s = MOE_ORDER[j % SLOTS]
                    pe.wait_ge(slot_filled[s], i * (16 * ROUNDS) + 16 * (BEFORE_MOE[s] + j // SLOTS + 1))
                    return s

                def gate_up(pair):
                    for w in range(2):
                        s = slot_of(3 * pair + w)
                        for f in range(2):
                            c = (2 * w + f) * CAP
                            for k in range(KT):
                                last = mm(bank(pair % 2)[:, c:c + CAP], cols(s)[:, k, f * P:(f + 1) * P], xeT[:, k, :],
                                          start=(k == 0), stop=(k == KT - 1))
                        last.then_inc((gate_used, gu_ready)[w], 1)

                def down(pair):
                    s = slot_of(3 * pair + 2)
                    pe.wait_ge(act_done, i * EXP_PAIRS + (pair + 1))
                    for f in range(2):
                        for k in range(KT):
                            last = mm(bank(2 + k // 4)[:, (k % 4) * CAP:(k % 4 + 1) * CAP], rows(s)[:, f, k * P:(k + 1) * P],
                                      act_e[pair % 2][:, f, :], start=(pair == 0 and f == 0 and k % 4 == 0),
                                      stop=(pair == EXP_PAIRS - 1 and f == 1), skip_group_check=True)
                    last.then_inc(down_used, 1)

                pe.wait_ge(xe_ready, i * 2 + 2)
                gate_up(0)
                gate_up(1)
                down(0)
                for tt in range(TT):
                    last = nc.tensor.transpose(bank(6)[0:CAP, tt * P:(tt + 1) * P], scatterP[:, tt, :], ident)
                last.then_inc(sT_transposed, 1)
                for pair in range(2, EXP_PAIRS):
                    gate_up(pair)
                    down(pair - 1)
                pe.wait_ge(built, i + 2)
                gather()
                down(EXP_PAIRS - 1)
                for q in range(2):
                    pe.wait_ge((yT_act, yT_dve)[q], i + 1)
                    if q == 0:
                        pe.wait_ge(sT_ready, i + 1)
                    for k in range(4 * q, 4 * q + 4):
                        last = nc.tensor.transpose(bank(6 + q)[0:CAP, (k % 4) * P:(k % 4 + 1) * P], yT[:, k, :], ident)
                    last.then_inc(y_transposed, 1)
                pe.wait_ge(xe_ready, i * 2 + 4)
                pe.wait_ge(yt_act, i + 1)
                pe.wait_ge(yt_dve, i + 1)
                for tt in range(TT):
                    for half in range(2):
                        mm(bank(4 + 2 * tt + half), scatterT[0:CAP, tt * P:(tt + 1) * P],
                           ytok[0:CAP, half * 512:(half + 1) * 512], start=True, stop=True).then_inc(scattered, 1)

        @block.scalar
        def _(act):
            a = nc.scalar.activation
            own = Chain(act, act_own)

            def inverse_norm(n, sem_of, values, own=own):
                for tt in range(TT):
                    act.wait_ge(sem_of, values[tt])
                    own(a(hn[:, tt, :], h[:, tt, :], ACT.Square, accum_out=ssq[:, tt:tt + 1]))
                    own(a(ssq[:, tt:tt + 1], ssq[:, tt:tt + 1], ACT.Ln, bias=eps, scale=1.0 / D))
                    a(rstd[:, tt:tt + 1], ssq[:, tt:tt + 1], ACT.Exp, scale=-0.5).then_inc(rstd_ready[n], 1)

            act.preload_act_table_set("natural_log_exp_and_others")
            act.wait_ge(consts_in, 16)
            inverse_norm(0, x_in, [16 * TT] * TT)
            act.wait_ge(bounds_shifted, 1)
            a(lbound[:, 2:4, :], lbound[:, 2:4, :], ACT.Exp).then_inc(bounds_exp, 1)

            with act.Fori(0, 4) as p:
                act.wait_ge(f_proj, p + 1)
                a(decay_in, bank(0).rearrange("p (a b) -> p a b", a=2), ACT.Exp, scale=-1.0).then_inc(f_exp, 1)
                act.wait_ge(f_done, p + 1)
                a(logf, forget, ACT.Ln).then_inc(f_log, 1)
                act.wait_ge(b_done, p + 1)
                a(eb, bsum, ACT.Exp)
                a(enb, bsum, ACT.Exp, scale=-1.0).then_inc(b_exps, 1)
                act.wait_ge(bdiff_done, p + 1)
                a(eend, bdiff, ACT.Exp).then_inc(bend_exp, 1)
                act.wait_ge(v_proj, p + 1)
                nc.scalar.copy(v_hg, bank(2).rearrange("p (a b) -> p a b", a=2)).then_inc(v_copied, 1)
                act.wait_ge(kend_transposed, p + 1)
                nc.scalar.copy(kend_tok, bank(4).rearrange("p (a b c) -> p a b c", a=2, b=TT)).then_inc(kend_copied, 1)
                act.wait_ge(g_proj, p + 1)
                a(gate_hg, bank(3).rearrange("p (a b) -> p a b", a=2), ACT.Exp, scale=-1.0).then_inc(g_exp, 1)
                act.wait_ge(o_ready, p + 1)
                a(square_hg, bank(4).rearrange("p (a b) -> p a b", a=2), ACT.Square).then_inc(o_squared, 1)
            act.wait_ge(o_gated, 5)
            own(a(orstd[:, :, :, :], ossq[:, :, :, :], ACT.Ln, bias=eps, scale=1.0 / P))
            a(orstd[:, :, :, :], orstd[:, :, :, :], ACT.Exp, scale=-0.5).then_inc(orstd_ready, 1)
            inverse_norm(1, h_ready[1], [2, 4])

            act.preload_act_table_set("silu_and_others")
            act.wait_ge(ff_gate, 1)
            a(silu_ff, bank(4).rearrange("p (a b) -> p a b", a=2), ACT.Silu).then_inc(ff_silu, 1)
            with act.Fori(1, FF_PAIRS) as i:
                act.wait_ge(ff_gate, i + 1)
                act.wait_ge(ff_act, i)
                a(silu_ff, bank(4).rearrange("p (a b) -> p a b", a=2), ACT.Silu).then_inc(ff_silu, 1)
            act.preload_act_table_set("natural_log_exp_and_others")
            inverse_norm(2, h_ready[2], [2, 4])

            with act.Fori(0, GROUPS) as g:
                def exps(u):
                    act.wait_ge(max_ready, g * UNITS + (u + 1))
                    a(prob[u % 2], prob[u % 2], ACT.Exp, bias=negmax[:, u:u + 1], scale=SCALE,
                      accum_out=rowsum[:, u:u + 1]).then_inc(exp_ready, 1)

                def value_copy(b):
                    act.wait_ge(va_proj, g * NBR + (b + 1))
                    nc.scalar.copy(vbuf[:, :, b, :], bank(b % 2).rearrange("p (a b) -> p a b", a=TT)).then_inc(va_copied, 1)

                exps(0)
                value_copy(0)
                exps(1)
                value_copy(1)
                value_copy(2)
                for u in range(2, UNITS + 1):
                    if u < UNITS:
                        exps(u)
                    if u % 2 == 0:
                        act.wait_ge(pT_ready, g * UNITS + u)
                        nc.scalar.copy(probT[1][:, 0:4, :], bank(5).rearrange("p (a b) -> p a b", a=4)).then_inc(pT_act, 1)
            inverse_norm(3, h_ready[3], [2, 4])

            act.wait_ge(shifted, 1)
            a(probs, probs, ACT.Exp).then_inc(exped, 1)

            act.preload_act_table_set("silu_and_others")
            act.wait_ge(table_ready, 1)
            items = act.value_load(table[0:1, EXTRA + 1:EXTRA + 2], min_val=NEXP, max_val=NEXP + EXTRA)
            with act.Fori(0, items) as i:
                for pair in range(EXP_PAIRS):
                    act.wait_ge(gu_ready, i * EXP_PAIRS + (pair + 1))
                    a(silu_e[pair % 2], bank(pair % 2)[:, 0:2 * CAP].rearrange("p (a b) -> p a b", a=2),
                      ACT.Silu).then_inc(silu_done, 1)
                act.wait_ge(down_used, i * EXP_PAIRS + EXP_PAIRS)
                nc.scalar.copy(yT[:, 0:4, :], bank(2)[:, 0:4 * CAP].rearrange("p (a b) -> p a b", a=4)).then_inc(yT_act, 1)
                act.wait_ge(y_transposed, i * 2 + 1)
                nc.scalar.copy(ytok[0:CAP, 0:512], bank(6)[0:CAP, :]).then_inc(yt_act, 1)
            act.preload_act_table_set("natural_log_exp_and_others")
            inverse_norm(4, added, [items * 4] * TT, own=Chain(act, act_own_end))

        @block.vector
        def _(dve):
            v = nc.vector
            own = Chain(dve, dve_own)

            def wide(ap, n):
                return ap.unsqueeze(len(ap.shape)).to_broadcast(list(ap.shape) + [n])

            def two(ap):
                return ap.unsqueeze(1).to_broadcast([ap.shape[0], 2, ap.shape[1]])

            def normalise(n, targets):
                for tt in range(TT):
                    dve.wait_ge(rstd_ready[n], tt + 1)
                    v.tensor_scalar(hn[:, tt, :], h[:, tt, :], rstd[:, tt:tt + 1], None, ALU.mult).then_inc(hn_ready[n], 1)
                for tt in range(TT):
                    for q in range(2):
                        dve.wait_ge(hn_transposed[n], 2 * tt + q + 1)
                        src = bank(4 + 2 * tt + q).rearrange("p (a b) -> p a b", a=4)
                        for dst, gain in targets:
                            v.tensor_tensor(dst[:, 4 * q:4 * q + 4, tt * P:(tt + 1) * P], src,
                                            wide(gain[:, 4 * q:4 * q + 4], P), ALU.mult).then_inc(hT_ready[n], 1)

            def mixer_output(m, n):
                for tt in range(TT):
                    for q in range(2):
                        dve.wait_ge(mixed_transposed[m], 2 * tt + q + 1)
                        v.tensor_copy(mixedT[:, 4 * q:4 * q + 4, tt * P:(tt + 1) * P],
                                      bank(4 + 2 * tt + q).rearrange("p (a b) -> p a b", a=4)).then_inc(mixedT_ready[m], 1)
                residual(n, proj_out[m], [1, 2, 3, 4])

            def residual(n, done, values):
                for j in range(4):
                    tt, half = j // 2, j % 2
                    dve.wait_ge(done, values[j])
                    part = h[:, tt, half * 512:(half + 1) * 512]
                    v.tensor_tensor(part, part, bank(j), ALU.add).then_inc(h_ready[n], 1)

            dve.wait_ge(params_in, 16)
            own(v.tensor_tensor(lbound[:, 0, :], bounds[:, 0, :], bounds[:, 1, :], ALU.max))
            v.tensor_tensor(lbound[:, 2:4, :], bounds, two(lbound[:, 0, :]), ALU.subtract).then_inc(bounds_shifted, 1)
            dve.wait_ge(x_in, 16 * TT)
            normalise(0, [(hT, attn_gain[:, 0, :])])
            dve.wait_ge(bounds_exp, 1)
            own(v.tensor_tensor(lbound[:, 0, :], lbound[:, 2, :], lbound[:, 3, :], ALU.add))
            own(v.reciprocal(lbound[:, 1, :], lbound[:, 0, :]))
            own(v.tensor_tensor(lbound[:, 2, :], lbound[:, 2, :], lbound[:, 1, :], ALU.mult))
            v.tensor_scalar(lbound[:, 3, :], lbound[:, 2, :], -1.0, 1.0, ALU.mult, ALU.add).then_inc(o_gated, 1)
            dve.wait_ge(o_gated, 1)

            flat = "p a b -> p (a b)"
            mask = cc("hgmask").bitcast(U32)
            with dve.Fori(0, 4) as p:
                own.enter(p, 8)
                dve.wait_ge(f_exp, p + 1)
                own(v.tensor_scalar(decay_in, decay_in, 1.0, None, ALU.add))
                own(v.reciprocal(decay_in, decay_in))
                for hh in range(2):
                    last = v.tensor_scalar(forget[:, hh, :], decay_in[:, hh, :], lbound[:, 3, bass.ds(p * 2 + hh, 1)],
                                           lbound[:, 2, bass.ds(p * 2 + hh, 1)], ALU.mult, ALU.add)
                last.then_inc(f_done, 1)
                dve.wait_ge(f_done, p + 1)
                v.tensor_scalar(keyk, forget, -1.0, 1.0, ALU.mult, ALU.add)
                dve.wait_ge(f_log, p + 1)
                v.tensor_tensor_scan(bsum.rearrange(flat), cc("reset"), logf.rearrange(flat), 0.0,
                                     ALU.mult, ALU.add).then_inc(b_done, 1)
                dve.wait_ge(b_done, p + 1)
                chunks = bsum.rearrange("p a (n c) -> p (a n) c", c=CHUNK)
                v.tensor_tensor(bdiff.rearrange("p a (n c) -> p (a n) c", c=CHUNK),
                                chunks[:, :, CHUNK - 1:CHUNK].to_broadcast([P, 2 * S // CHUNK, CHUNK]), chunks,
                                ALU.subtract).then_inc(bdiff_done, 1)
                dve.wait_ge(b_exps, p + 1)
                dve.wait_ge(q_proj, p + 1)
                v.tensor_tensor(qdec, bank(1).rearrange("p (a b) -> p a b", a=2), eb, ALU.mult)
                v.tensor_tensor(kdec, keyk, enb, ALU.mult).then_inc(decayed, 1)
                dve.wait_ge(bend_exp, p + 1)
                v.tensor_tensor(kend, keyk, eend, ALU.mult).then_inc(decayed, 1)
                dve.wait_ge(zeroed, 1)
                dve.wait_ge(scores_hg_ready, p + 1)
                v.copy_predicated(scores_hg.rearrange("p a b c -> p (a b) c"),
                                  mask.unsqueeze(1).to_broadcast([P, 4, P]),
                                  bank(5).rearrange("p (a c) -> p a c", a=4)).then_inc(scores_hg_masked, 1)
                dve.wait_ge(kv_ready, p + 1)
                own(v.tensor_copy(states[:, :, 0, :], bank(6).rearrange("p (a b) -> p a b", a=2)[:, :, 0:P]))
                for n in (1, 2):
                    for hh in range(2):
                        last = v.scalar_tensor_tensor(out=states[:, hh, n, :], in0=states[:, hh, n - 1, :],
                                                      scalar=eb[:, hh, (n + 1) * CHUNK - 1:(n + 1) * CHUNK],
                                                      in1=chunk_kv(hh, n), op0=ALU.mult, op1=ALU.add)
                    if n == 1:
                        own(last)
                last.then_inc(states_ready, 1)
                dve.wait_ge(g_exp, p + 1)
                own(v.tensor_scalar(gate_hg, gate_hg, 1.0, None, ALU.add))
                own(v.reciprocal(gate_hg, gate_hg))
                own(v.tensor_tensor(gate_hg, bank(3).rearrange("p (a b) -> p a b", a=2), gate_hg, ALU.mult))
                g4 = gate_hg.rearrange("p a (b c) -> p (a b) c", b=2)
                own(v.tensor_tensor(g4, g4, pp("out_norm").unsqueeze(1).to_broadcast([P, 4, P]), ALU.mult))
                dve.wait_ge(o_squared, p + 1)
                v.tensor_reduce(ossq[:, bass.ds(p, 1), :, :].rearrange("p x a b -> p (x a b)"),
                                square_hg.rearrange("p a (b c) -> p (a b) c", b=2), AX.X, ALU.add)
                v.tensor_tensor(mixed[:, :, bass.ds(p * 256, 256)], bank(4).rearrange("p (a b) -> p a b", a=2), gate_hg,
                                ALU.mult).then_inc(o_gated, 1)
            own.leave(4)
            dve.wait_ge(orstd_ready, 1)
            for tt in range(TT):
                for hh in range(2):
                    m4 = mixed[:, tt, :].rearrange("p (a b c) -> p a b c", a=4, b=2)[:, :, hh, :]
                    last = v.tensor_tensor(m4, m4, wide(orstd[:, :, tt, hh], P), ALU.mult)
                last.then_inc(mixed_ready, 1)
            mixer_output(0, 1)
            normalise(1, [(hT, ffn_gain[:, 0, :])])

            with dve.Fori(0, FF_PAIRS) as i:
                dve.wait_ge(ff_silu, i + 1)
                dve.wait_ge(ff_up, i + 1)
                v.tensor_tensor(act_ff, silu_ff, bank(5).rearrange("p (a b) -> p a b", a=2), ALU.mult).then_inc(ff_act, 1)
            residual(2, ff_sum, [1, 1, 2, 2])
            normalise(2, [(hT, attn_gain[:, 1, :]), (hTkv, kv_gain)])

            cos, sin = cc("cos"), cc("sin")
            with dve.Fori(0, GROUPS) as g:
                own.enter(g, 2 * UNITS)

                def rope(j):
                    buf = (kbuf + qbuf)[j]
                    src = bank(j % 2).rearrange("p (a b) -> p a b", a=2)
                    dve.wait_ge(kq_proj, g * 6 + (j + 1))
                    v.tensor_tensor(buf, src, two(cos), ALU.mult)
                    if j:
                        dve.wait_ge(rope_done, g * 6 + j)
                    for q in range(4):
                        a, b = 32 * q, 32 * (q ^ 1)
                        last = v.tensor_tensor(rot[b:b + 32], src[a:a + 32], two(sin[a:a + 32, :]), ALU.mult)
                    last.then_inc(kq_read, 1)

                def row_max(u):
                    qt = u % 2
                    n = NBR * P * (qt + 1)
                    dve.wait_ge(s_ready, g * UNITS + (u + 1))
                    v.memset(negmax[:, u:u + 1], 0.0)
                    own(v.tensor_tensor_reduce(prob[qt], ps[:, 512 * (2 + qt):512 * (2 + qt) + n], cc(f"mask{qt}"), 1.0, -3e38,
                                               ALU.add, ALU.max, rowmax[:, u:u + 1]))
                    v.tensor_scalar(negmax[:, u:u + 1], rowmax[:, u:u + 1], -SCALE, None, ALU.mult).then_inc(max_ready, 1)

                def turned(u):
                    dve.wait_ge(pT_ready, g * UNITS + (u + 1))
                    if u % 2 == 0:
                        dst, src = probT[0], bank(5)[:, 0:NBR * P]
                    else:
                        dst, src = probT[1][:, 4:6, :], bank(6)[:, 0:2 * P]
                    v.tensor_copy(dst, src.rearrange("p (a b) -> p a b", b=P)).then_inc(pT_dve, 1)

                def output(u):
                    hd, qt = u // 2, u % 2
                    dve.wait_ge(pv_ready, g * UNITS + (u + 1))
                    own(v.reciprocal(rowinv[:, u:u + 1], rowsum[:, u:u + 1]))
                    v.tensor_scalar(mixed[:, qt, bass.ds(g * 256 + hd * HEAD, HEAD)], bank(7)[:, 0:HEAD], rowinv[:, u:u + 1],
                                    None, ALU.mult).then_inc(o_evac, 1)

                for j in range(2 * NBR):
                    rope(j)
                for u in range(UNITS + 2):
                    if u < UNITS:
                        row_max(u)
                    if 1 <= u < UNITS + 1:
                        turned(u - 1)
                    if u >= 2:
                        output(u - 2)
            own.leave(GROUPS)
            mixer_output(1, 3)
            normalise(3, [(hT, ffn_gain[:, 1, :])])

            experts = cc("experts")
            lg = bank(0)[:, 0:TT * NEXP].rearrange("p (t e) -> p t e", t=TT)
            dve.wait_ge(logits_ready, 1)
            own(v.tensor_reduce(r1[:, 0:2], lg, AX.X, ALU.max))
            v.tensor_tensor(probs, lg, wide(r1[:, 0:2], NEXP), ALU.subtract).then_inc(shifted, 1)
            dve.wait_ge(exped, 1)
            own(v.tensor_reduce(r1[:, 2:4], probs, AX.X, ALU.add))
            own(v.reciprocal(r1[:, 4:6], r1[:, 2:4]))
            own(v.tensor_tensor(probs, probs, wide(r1[:, 4:6], NEXP), ALU.mult))
            for tt in range(TT):
                last = v.max(top[:, tt, :], probs[:, tt, :])
            own(last)
            for tt in range(TT):
                last = v.max_index(topi[:, tt, :], top[:, tt, :], probs[:, tt, :])
            own(last)
            v.tensor_copy(topf, topi)
            own(v.tensor_tensor(r1[:, 0:2], top[:, :, 0], top[:, :, 1], ALU.add))
            own(v.reciprocal(r1[:, 2:4], r1[:, 0:2]))
            own(v.tensor_tensor(top[:, :, 0:2], top[:, :, 0:2], wide(r1[:, 2:4], 2), ALU.mult))
            for tt in range(TT):
                v.tensor_scalar(onehot[:, tt, :], experts, topf[:, tt, 0:1], None, ALU.is_equal)
                v.tensor_scalar(chosen[:, tt, :], experts, topf[:, tt, 1:2], None, ALU.is_equal)
                v.tensor_scalar(wa[:, tt, :], experts, topf[:, tt, 0:1], top[:, tt, 0:1], ALU.is_equal, ALU.mult)
                last = v.tensor_scalar(place[:, tt, :], experts, topf[:, tt, 1:2], top[:, tt, 1:2], ALU.is_equal, ALU.mult)
            own(last)
            v.tensor_tensor(chosen, chosen, onehot, ALU.add).then_inc(chosen_ready, 1)
            v.memset(key[:, ITEMS - 1, :], ABSENT)
            v.memset(weight[:, ITEMS - 1, :], 0.0)
            w8 = weight[:, 0:NEXP, :].rearrange("p e t -> p t e")
            k8 = key[:, 0:NEXP, :].rearrange("p e t -> p t e")
            own(v.tensor_tensor(w8, wa, place, ALU.add))
            dve.wait_ge(places_ready, 1)
            dve.wait_ge(chosen_ready, 1)
            own(v.tensor_scalar(place, bank(1)[:, 0:TT * NEXP].rearrange("p (t e) -> p t e", t=TT), -ABSENT, None, ALU.add))
            own(v.tensor_copy(counts, bank(1)[:, TT * NEXP:(TT + 1) * NEXP]))
            own(v.tensor_tensor(place, place, chosen, ALU.mult))
            own(v.tensor_scalar(k8, place, ABSENT, None, ALU.add))

            def build(i, chain):
                chain(v.tensor_tensor(gatherP, cc("places").unsqueeze(1).to_broadcast([P, TT, CAP]),
                                      wide(key[:, bass.ds(i, 1), :].rearrange("p x t -> p (x t)"), CAP), ALU.is_equal))
                v.tensor_tensor(scatterP, gatherP, wide(weight[:, bass.ds(i, 1), :].rearrange("p x t -> p (x t)"), CAP),
                                ALU.mult).then_inc(built, 1)

            build(0, own)
            base3 = cc("over_base").rearrange("p (b e) -> p b e", b=BLOCKS)

            def over(ap):
                return ap.unsqueeze(1).to_broadcast([P, BLOCKS, NEXP])

            def each(ap):
                return ap.unsqueeze(1).to_broadcast([P, EXTRA, nj])

            own(v.tensor_tensor(active.rearrange("p (b e) -> p b e", b=BLOCKS), over(counts), base3, ALU.is_gt))
            own(v.tensor_tensor_scan(order, cc("ones")[:, 0:nj], active, 0.0, ALU.mult, ALU.add))
            v.tensor_reduce(tablef[:, EXTRA:EXTRA + 1], active, AX.X, ALU.add)
            own(v.tensor_tensor(order, order, active, ALU.subtract))
            own(v.tensor_scalar(order, order, -ABSENT, None, ALU.add))
            own(v.tensor_tensor(order, order, active, ALU.mult))
            own(v.tensor_scalar(order, order, ABSENT, None, ALU.add))
            own(v.tensor_tensor(sel, each(order), cc("over_k").rearrange("p (k j) -> p k j", k=EXTRA), ALU.is_equal))
            own(v.tensor_tensor(prod, sel, each(cc("over_e")), ALU.mult))
            v.tensor_scalar(tablef[:, EXTRA + 1:EXTRA + 2], tablef[:, EXTRA:EXTRA + 1], float(NEXP), None, ALU.add)
            own(v.tensor_reduce(tablef[:, 0:EXTRA], prod, AX.X, ALU.add))
            v.tensor_copy(table[:, 0:EXTRA + 2], tablef[:, 0:EXTRA + 2]).then_inc(table_ready, 1)

            def tokens_in(count):
                dve.wait_ge(gathered, count)
                for q in range(2):
                    v.tensor_tensor(xeT[:, 4 * q:4 * q + 4, :], bank(4 + q)[:, 0:4 * CAP].rearrange("p (a b) -> p a b", a=4),
                                    wide(ffn_gain[:, 1, 4 * q:4 * q + 4], CAP), ALU.mult).then_inc(xe_ready, 1)

            tokens_in(1)
            for tt in range(TT):
                k3 = keymod[:, tt, :].rearrange("p (b e) -> p b e", b=BLOCKS)
                own(v.tensor_tensor(k3, over(key[:, 0:NEXP, tt]), base3, ALU.subtract))
                own(v.tensor_tensor(prod, sel, each(keymod[:, tt, :]), ALU.mult))
                own(v.tensor_reduce(key[:, NEXP:NEXP + EXTRA, tt], prod, AX.X, ALU.add))
                own(v.tensor_copy(k3, over(weight[:, 0:NEXP, tt])))
                own(v.tensor_tensor(prod, sel, each(keymod[:, tt, :]), ALU.mult))
                own(v.tensor_reduce(weight[:, NEXP:NEXP + EXTRA, tt], prod, AX.X, ALU.add))
            dve.wait_ge(table_ready, 1)
            items = dve.value_load(table[0:1, EXTRA + 1:EXTRA + 2], min_val=NEXP, max_val=NEXP + EXTRA)
            with dve.Fori(0, items) as i:
                own.enter(i, 1)
                for pair in range(EXP_PAIRS):
                    dve.wait_ge(silu_done, i * EXP_PAIRS + (pair + 1))
                    v.tensor_tensor(act_e[pair % 2], silu_e[pair % 2],
                                    bank(pair % 2)[:, 2 * CAP:4 * CAP].rearrange("p (a b) -> p a b", a=2),
                                    ALU.mult).then_inc(act_done, 1)
                    if pair == 0:
                        dve.wait_ge(sT_transposed, i + 1)
                        v.tensor_copy(scatterT[0:CAP, :], bank(6)[0:CAP, 0:S]).then_inc(sT_ready, 1)
                        build(i + 1, own)
                tokens_in(i + 2)
                dve.wait_ge(down_used, i * EXP_PAIRS + EXP_PAIRS)
                v.tensor_copy(yT[:, 4:8, :], bank(3)[:, 0:4 * CAP].rearrange("p (a b) -> p a b", a=4)).then_inc(yT_dve, 1)
                dve.wait_ge(y_transposed, i * 2 + 2)
                v.tensor_copy(ytok[0:CAP, 512:1024], bank(7)[0:CAP, :]).then_inc(yt_dve, 1)
                for j in range(4):
                    tt, half = j // 2, j % 2
                    dve.wait_ge(scattered, i * 4 + (j + 1))
                    part = h[:, tt, half * 512:(half + 1) * 512]
                    v.tensor_tensor(part, part, bank(4 + j), ALU.add).then_inc(added, 1)

            dve.wait_ge(added, items * 4)
            for tt in range(TT):
                dve.wait_ge(rstd_ready[4], tt + 1)
                v.scalar_tensor_tensor(out=hn[:, tt, :], in0=h[:, tt, :], scalar=rstd[:, tt:tt + 1], in1=pp("final_norm"),
                                       op0=ALU.mult, op1=ALU.mult).then_inc(normed, 1)

        @block.gpsimd
        def _(pool):
            nc.gpsimd.memset(scores_hg, 0.0).then_inc(zeroed, 1)
            with pool.Fori(0, GROUPS) as g:
                for j in range(2 * NBR):
                    buf = (kbuf + qbuf)[j]
                    pool.wait_ge(kq_read, g * 6 + (j + 1))
                    nc.gpsimd.tensor_tensor(buf, buf, rot, ALU.add).then_inc(rope_done, 1)


_INS = ["x", "hgrn_w_in", "hgrn_w_out", "w_kv", "dil_w_q", "dil_w_out", "ffn_w_gate", "ffn_w_up", "ffn_w_down",
        "moe_w_gate", "moe_w_up", "moe_w_down"]


def kernel(**inputs):
    import concourse.bacc as bacc
    from concourse.bass_utils import run_bass_kernel_spmd

    def per_partition(a):
        a = np.asarray(a).reshape(-1, KT, P)
        return np.moveaxis(a, 2, 0).reshape(P, -1)

    router = np.asarray(inputs["moe_w_router"])[0].reshape(KT, P, NEXP)
    parts = {
        "attn_norm": per_partition(inputs["attn_norm"]),
        "ffn_norm": per_partition(inputs["ffn_norm"]),
        "kv_norm": per_partition(inputs["kv_norm"]),
        "bounds": per_partition(inputs["hgrn_lower_bounds"]),
        "router": np.moveaxis(router, 1, 0).reshape(P, -1),
        "out_norm": np.broadcast_to(np.asarray(inputs["hgrn_out_norm"])[0], (P, P)),
        "final_norm": np.broadcast_to(np.asarray(inputs["final_norm"]), (P, D)),
    }
    arrays = {name: np.ascontiguousarray(inputs[name]) for name in _INS}
    arrays["consts"] = constants()
    arrays["params"] = np.ascontiguousarray(np.concatenate([parts[n] for n in PARAMS], 1))
    nc = bacc.Bacc("TRN2", target_bir_lowering=False, num_devices=1)
    aps = {n: nc.dram_tensor(f"in_{n}", a.shape, mybir.dt.from_np(a.dtype), kind="ExternalInput").ap()
           for n, a in arrays.items()}
    out = nc.dram_tensor("out", (1, S, D), F32, kind="ExternalOutput").ap()
    trunk_kernel(nc, aps, aps["consts"], aps["params"], out)
    r = run_bass_kernel_spmd(nc, [{f"in_{n}": a for n, a in arrays.items()}], core_ids=[0])
    return r.results[0]["out"]
```

```python
from contextlib import ExitStack

import numpy as np

import concourse.bass as bass
from concourse import mybir

ACT = mybir.ActivationFunctionType
ALU = mybir.AluOpType
AX = mybir.AxisListType
F32 = mybir.dt.float32
FR = mybir.dt.float32r
I32 = mybir.dt.int32
U32 = mybir.dt.uint32

P = 128
D = 1024
S = 256
KT = D // P
TT = S // P
CHUNK = 64
HEAD = 64
NBR = 3
DILS = (1, 4, 16)
BAND = 128
DFF = 2816
DEXP = 3584
NEXP = 8
CAP = 96
EXTRA = (2 * S) // (CAP + 1)
BLOCKS = -(-S // CAP) - 1
ITEMS = NEXP + EXTRA + 1
EPS = 1e-6
SCALE = HEAD ** -0.5
ABSENT = -1000.0
LNEXP_SET = 6
FF_PAIRS = DFF // 256
EXP_PAIRS = DEXP // 256
GROUPS = 4
UNITS = 8
SLOT = 2048
CHUNKS = DEXP // 512
PER_ITEM = 6 * CHUNKS
PRIMED = 4

RAWS, SPLITS = 7, 3
RAW_OF, SPLIT_OF = [], []


def _phase(times, raw, split):
    first = len(RAW_OF)
    RAW_OF.extend(raw * times)
    SPLIT_OF.extend(split * times)
    return first


HG = _phase(4, [0, 1, 2, 3], [0, 1, 2, 1])
HG_OUT = _phase(1, [0, 1, 2, 3], [0, 1, 2, 1])
FF = _phase(FF_PAIRS, [0, 1, 2], [0, 1, 2])
AT = _phase(GROUPS, [0, 1, 2, 3, 4, 5, 6, 3, 4], [0, 1, 2] * 3)
AT_OUT = _phase(1, [0, 1, 2, 3], [0, 1, 2, 1])
MOE = _phase(3, [j % RAWS for j in range(PER_ITEM)], [j % SPLITS for j in range(PER_ITEM)])
MOE_LOADS = [(kind, c if kind != "down" else c - 1, half) for c in range(CHUNKS + 1) for kind in ("gate", "up", "down")
             for half in range(2) if (kind == "down" and c > 0) or (kind != "down" and c < CHUNKS)]


def distance(slots, n, per):
    last = [n - m for n_ in (n,) for m in range(n_ - 1, -1, -1) if slots[m] == slots[n_]][:1]
    if per and n + per < len(slots):
        last += [n + per - m for m in range(n + per - 1, -1, -1) if slots[m] == slots[n + per]][:1]
        assert slots[n] == slots[n + per], n
    return min(last) if last else None


def landed(n):
    return 16 * sum(RAW_OF[m] == RAW_OF[n] for m in range(n + 1))


CONSTS = {}
_at = 0
for _name, _n in (("ident", P), ("ustrict", P), ("ones", P), ("hgmask", P), ("reset", 2 * S), ("places", CAP),
                  ("experts", NEXP), ("over_k", EXTRA * BLOCKS * NEXP), ("over_e", BLOCKS * NEXP),
                  ("over_base", BLOCKS * NEXP), ("eps", 1), ("cos", S), ("sin", S),
                  ("mask0", NBR * P), ("mask1", NBR * S)):
    CONSTS[_name] = (_at, _at + _n)
    _at += _n
NCONST = _at
PARAMS = {}
_at = 0
for _name, _n in (("attn_norm", 2 * KT), ("ffn_norm", 2 * KT), ("kv_norm", KT), ("bounds", 2 * KT),
                  ("router", KT * NEXP), ("out_norm", P), ("final_norm", D)):
    PARAMS[_name] = (_at, _at + _n)
    _at += _n
NPARAM = _at


def constants():
    c = np.zeros((P, NCONST), np.float32)

    def put(name, value):
        a, b = CONSTS[name]
        c[:, a:b] = np.broadcast_to(np.asarray(value, np.float32), (P, b - a))

    r = np.arange(P)
    put("ident", np.eye(P))
    put("ustrict", r[:, None] < r[None, :])
    put("ones", np.ones((P, P)))
    put("hgmask", (r[:, None] <= r[None, :]) & (r[:, None] // CHUNK == r[None, :] // CHUNK))
    put("reset", (np.arange(2 * S) % CHUNK != 0)[None])
    put("places", np.arange(CAP)[None])
    put("experts", np.arange(NEXP)[None])
    nj = BLOCKS * NEXP
    put("over_k", np.repeat(np.arange(EXTRA), nj)[None])
    put("over_e", np.tile(np.arange(NEXP) + 1, BLOCKS)[None])
    put("over_base", (CAP * (1 + np.repeat(np.arange(BLOCKS), NEXP)))[None])
    put("eps", np.full((P, 1), EPS))
    half = HEAD // 2
    inv = np.float32(10000.0) ** (-np.arange(half, dtype=np.float32) / np.float32(half))
    ang = np.arange(S, dtype=np.float32)[None, :] * inv[:, None].astype(np.float32)
    put("cos", np.tile(np.cos(ang), (4, 1)))
    put("sin", np.concatenate([np.sin(ang), -np.sin(ang)] * 2, 0))
    for tt, name in ((0, "mask0"), (1, "mask1")):
        q = tt * P + r[:, None]
        k = np.arange((tt + 1) * P)[None, :]
        ok = [(k <= q) & ((q - k) % dil == 0) & (q - k <= BAND * dil) for dil in DILS]
        put(name, np.concatenate([np.where(m, 0.0, -1e30) for m in ok], 1))
    return c


class Chain:

    def __init__(self, eng, sem):
        self.eng, self.sem, self.base, self.n, self.i, self.per = eng, sem, 0, 0, 0, 0

    def __call__(self, ins):
        self.n += 1
        ins.then_inc(self.sem, 1)
        self.eng.wait_ge(self.sem, self.i * self.per + (self.base + self.n))

    def enter(self, i, per):
        self.base, self.n, self.i, self.per = self.base + self.n, 0, i, per

    def leave(self, trips):
        assert self.n == self.per, (self.n, self.per)
        self.base, self.n, self.i, self.per = self.base + trips * self.per, 0, 0, 0


def trunk_kernel(nc, t, consts, params, out):
    with ExitStack() as ctx:
        def sb(name, shape, dt=F32):
            return ctx.enter_context(nc.sbuf_tensor(name, shape, dt))

        def sem(name):
            return ctx.enter_context(nc.semaphore(name))

        raw = sb("raw", [P, RAWS, SLOT])
        split = sb("split", [P, SPLITS, 2, SLOT], FR)
        cst = sb("cst", [P, NCONST])
        par = sb("par", [P, NPARAM])
        h = sb("h", [P, TT, D])
        hn = sb("hn", [P, TT, D])
        mixed = hn
        hT = sb("hT", [P, 2, KT, S], FR)
        stage = sb("stage", [P, 2, 4, P])
        frarena = sb("frarena", [P, 2 * KT * S], FR)
        ssq = sb("ssq", [P, TT])
        rstd = sb("rstd", [P, TT])
        arena_floats = 8192
        arena = sb("arena", [P, arena_floats])
        table = sb("table", [P, EXTRA + 3], I32)

        def carve(arena=arena):
            used = [0]

            def take(*shape):
                n = int(np.prod(shape))
                a = arena[:, used[0]:used[0] + n]
                used[0] += n
                assert used[0] <= arena.shape[1], used
                names = "wxyz"[:len(shape)]
                if len(shape) == 1:
                    return a
                return a.rearrange(f"p ({' '.join(names)}) -> p {' '.join(names)}", **dict(zip(names, shape)))
            return take

        ps = ctx.enter_context(nc.psum_tensor("ps", [P, 8 * 512], F32))

        def bank(b, n=512):
            return ps[:, 512 * b:512 * b + n]

        def chunk_kv(hh, n):
            c = (2 * hh + n // 2) * P if n % 2 == 0 else hh * P
            return bank(6 + n % 2)[:, c:c + P]

        def cc(name):
            a, b = CONSTS[name]
            return cst[:, a:b]

        def pp(name):
            a, b = PARAMS[name]
            return par[:, a:b]

        ident, eps = cc("ident"), cc("eps")
        attn_gain = pp("attn_norm").rearrange("p (l k) -> p l k", l=2)
        ffn_gain = pp("ffn_norm").rearrange("p (l k) -> p l k", l=2)
        kv_gain = pp("kv_norm")
        bounds = pp("bounds").rearrange("p (l k) -> p l k", l=2)
        router = pp("router").rearrange("p (k e) -> p k e", k=KT)

        def part(n, w, k):
            return split[:, SPLIT_OF[n], w, :].rearrange("p (k n) -> p k n", k=k)

        take = carve()
        decay_in = take(2, S)
        logf = decay_in
        forget = take(2, S)
        bdiff = eend = kend = forget
        keyk = take(2, S)
        bsum = take(2, S)
        eb = take(2, S)
        enb = take(2, S)
        kdec = enb
        qdec = take(2, S)
        kend_tok = take(2, TT, P)
        v_hg = take(TT, 2 * P)
        scores_hg = take(2, TT, P)
        states = take(2, 3, P)
        gate_hg = take(TT, 2 * P)
        square_hg = take(TT, 2 * P)
        lbound = sb("lbound", [P, 4, KT])
        ossq = sb("ossq", [P, 4, TT, 2])
        orstd = sb("orstd", [P, 4, TT, 2])
        take = carve()
        silu_ff = take(2, S)
        act_ff = take(2, S)
        act_ff_hl = carve(frarena)(2, 2, S)
        take = carve()
        hTkv = carve(frarena)(2, KT, S)
        kbuf = [take(2, S) for _ in range(NBR)]
        qbuf = [take(2, S) for _ in range(NBR)]
        vbuf = take(TT, NBR, 256)
        rot = take(2, S)
        prob = [take(NBR * P), take(NBR * S)]
        probT = [take(NBR, P), take(NBR * 2, P)]
        rowmax = sb("rowmax", [P, UNITS])
        negmax = sb("negmax", [P, UNITS])
        rowsum = sb("rowsum", [P, UNITS])
        rowinv = sb("rowinv", [P, UNITS])
        take = carve()
        hT_router = take(KT, S)
        logits = take(TT, NEXP)
        probs = take(TT, NEXP)
        top = take(TT, 8)
        topi = take(TT, 8).bitcast(U32)
        topf = take(TT, 8)
        r1 = take(8)
        onehot = take(TT, NEXP)
        wa = take(TT, NEXP)
        chosen = take(TT, NEXP)
        place = take(TT, NEXP)
        key = take(ITEMS, TT)
        weight = take(ITEMS, TT)
        nj = BLOCKS * NEXP
        counts = take(NEXP)
        active = take(nj)
        order = take(nj)
        sel = take(EXTRA, nj)
        prod = take(EXTRA, nj)
        keymod = take(TT, nj)
        tablef = take(EXTRA + 3)
        gatherP = take(TT, CAP)
        scatterP = take(TT, CAP)
        scatterT = take(S)
        xe_stage = take(KT, CAP)
        silu_e = take(512)
        act_e = take(512)
        ytok = take(D)
        take = carve(frarena)
        xeT = take(2, KT, CAP)
        actT = take(2, 4, CAP)

        slot_filled = [sem(f"slot_filled{s}") for s in range(RAWS)]
        hi_ready, split_ready, weights_used = sem("hi_ready"), sem("split_ready"), sem("weights_used")
        consts_in, params_in, x_in, out_stored = sem("consts_in"), sem("params_in"), sem("x_in"), sem("out_stored")
        act_own, dve_own, pool_own = sem("act_own"), sem("dve_own"), sem("pool_own")
        act_own_end, dve_own_end = sem("act_own_end"), sem("dve_own_end")
        bounds_shifted, bounds_exp = sem("bounds_shifted"), sem("bounds_exp")
        zeroed = sem("zeroed")
        NN = 5
        rstd_ready = [sem(f"rstd_ready{n}") for n in range(NN)]
        hn_ready = [sem(f"hn_ready{n}") for n in range(NN)]
        hn_transposed = [sem(f"hn_transposed{n}") for n in range(NN)]
        hT_ready = [sem(f"hT_ready{n}") for n in range(NN)]
        staged = [sem(f"staged{n}") for n in range(NN)]
        hT_hi = [sem(f"hT_hi{n}") for n in range(NN)]
        h_ready = [sem(f"h_ready{n}") for n in range(NN)]
        f_exp, f_done, f_log, b_done = sem("f_exp"), sem("f_done"), sem("f_log"), sem("b_done")
        bdiff_done, b_exps, bend_exp = sem("bdiff_done"), sem("b_exps"), sem("bend_exp")
        decayed, kend_transposed, kend_copied = sem("decayed"), sem("kend_transposed"), sem("kend_copied")
        v_copied, scores_hg_ready, scores_hg_masked = sem("v_copied"), sem("scores_hg_ready"), sem("scores_hg_masked")
        kv_ready, states_ready, g_exp = sem("kv_ready"), sem("states_ready"), sem("g_exp")
        o_ready, o_squared, o_gated = sem("o_ready"), sem("o_squared"), sem("o_gated")
        orstd_ready = sem("orstd_ready")
        mixed_ready = sem("mixed_ready")
        mixed_transposed = [sem("mixed_transposed0"), sem("mixed_transposed1")]
        mixedT_hi = [sem("mixedT_hi0"), sem("mixedT_hi1")]
        mixedT_ready = [sem("mixedT_ready0"), sem("mixedT_ready1")]
        proj_out = [sem("proj_out0"), sem("proj_out1")]
        ff_silu, ff_act, ff_sum = sem("ff_silu"), sem("ff_act"), sem("ff_sum")
        kq_read, rope_done, va_copied = sem("kq_read"), sem("rope_done"), sem("va_copied")
        s_ready, max_ready, exp_ready = sem("s_ready"), sem("max_ready"), sem("exp_ready")
        pT_ready, pT_dve, pT_act, pv_ready, o_evac = (sem("pT_ready"), sem("pT_dve"), sem("pT_act"), sem("pv_ready"),
                                                      sem("o_evac"))
        logits_ready, shifted, exped, chosen_ready, places_ready = (
            sem("logits_ready"), sem("shifted"), sem("exped"), sem("chosen_ready"), sem("places_ready"))
        table_ready = sem("table_ready")
        built, gathered, xe_staged, xe_hi, xe_ready = (sem(n) for n in ("built", "gathered", "xe_staged", "xe_hi", "xe_ready"))
        sT_transposed, sT_ready = sem("sT_transposed"), sem("sT_ready")
        silu_done, act_done, act_turned, actT_hi, actT_ready = (sem(n) for n in (
            "silu_done", "act_done", "act_turned", "actT_hi", "actT_ready"))
        y_half, yt_act, yt_dve = sem("y_half"), sem("yt_act"), sem("yt_dve")
        scattered, added = sem("scattered"), sem("added")
        normed = sem("normed")

        w_in = t["hgrn_w_in"][0].rearrange("(k p) n -> p k n", p=P)
        w_kv = t["w_kv"].rearrange("(k p) n -> p k n", p=P)
        w_q = t["dil_w_q"][0].rearrange("(k p) n -> p k n", p=P)
        hg_out = t["hgrn_w_out"][0].rearrange("(k p) n -> p k n", p=P)
        at_out = t["dil_w_out"][0].rearrange("(k p) n -> p k n", p=P)
        ff_g = t["ffn_w_gate"][0].rearrange("(k p) n -> p k n", p=P)
        ff_u = t["ffn_w_up"][0].rearrange("(k p) n -> p k n", p=P)
        ff_d = t["ffn_w_down"][0].rearrange("(k p) n -> p k n", p=P)
        moe_g = t["moe_w_gate"][0].rearrange("e (k p) n -> e p k n", p=P)
        moe_u = t["moe_w_up"][0].rearrange("e (k p) n -> e p k n", p=P)
        moe_d = t["moe_w_down"][0].rearrange("e (k p) n -> e p k n", p=P)
        x_tok = t["x"][0].rearrange("(t p) d -> p t d", p=P)
        out_tok = out[0].rearrange("(t p) d -> p t d", p=P)

        block = ctx.enter_context(nc.Block())

        @block.sync
        def _(sp):
            def load(n, src, t=0, per=0):
                back = distance(RAW_OF, n, per)
                if back:
                    sp.wait_ge(split_ready, t * per + (n - back + 1))
                k = src.shape[1]
                sp.dma_start(raw[:, RAW_OF[n], :].rearrange("p (k n) -> p k n", k=k), src).then_inc(slot_filled[RAW_OF[n]], 16)

            def load_hg(p, first, **loop):
                for j, c in ((1, 0), (0, 1), (2, 2), (3, 3)):
                    load(first + j, w_in[:, :, bass.ds(p * 256 + c * D, 256)], **loop)

            def load_out(first, w):
                for j in range(4):
                    load(first + j, w[:, 2 * j:2 * j + 2, :])

            def load_ff(kind, i, n, **loop):
                if kind == "down":
                    load(n, ff_d[:, bass.ds(i * 2, 2), :], **loop)
                else:
                    load(n, (ff_g if kind == "gate" else ff_u)[:, :, bass.ds(i * 256, 256)], **loop)

            def load_att(g, first, **loop):
                for j in range(3 * NBR):
                    w, c = ((w_kv, 0), (w_q, 0), (w_kv, NBR * D))[j // NBR]
                    load(first + j, w[:, :, bass.ds(g * 256 + (c + j % NBR * D), 256)], **loop)

            def load_moe(e, js, first, **loop):
                for j in js:
                    kind, c, half = MOE_LOADS[j]
                    if kind == "down":
                        src = moe_d[e, :, 4 * c + 2 * half:4 * c + 2 * half + 2, :]
                    else:
                        src = (moe_g if kind == "gate" else moe_u)[e, :, 4 * half:4 * half + 4, 512 * c:512 * c + 512]
                    load(first + j, src, **loop)

            for tt in range(TT):
                sp.dma_start(h[:, tt, :], x_tok[:, tt, :]).then_inc(x_in, 16)
            sp.dma_start(cst[:, :], consts).then_inc(consts_in, 16)
            sp.dma_start(par[:, :], params).then_inc(params_in, 16)
            load_hg(0, HG)
            with sp.Fori(0, 3) as t:
                load_hg(t + 1, HG + 4, t=t, per=4)
            load_out(HG_OUT, hg_out)
            load_ff("gate", 0, FF)
            load_ff("up", 0, FF + 1)
            with sp.Fori(0, FF_PAIRS - 1) as t:
                load_ff("gate", t + 1, FF + 2, t=t, per=3)
                load_ff("down", t, FF + 3, t=t, per=3)
                load_ff("up", t + 1, FF + 4, t=t, per=3)
            load_ff("down", FF_PAIRS - 1, AT - 1)
            load_att(0, AT)
            with sp.Fori(0, GROUPS - 1) as t:
                load_att(t + 1, AT + 9, t=t, per=9)
            load_out(AT_OUT, at_out)
            load_moe(0, range(PER_ITEM), MOE)
            nxt = MOE + PER_ITEM
            load_moe(1, (0, 1), nxt)
            with sp.Fori(0, NEXP - 2) as t:
                load_moe(t + 1, range(2, PER_ITEM), nxt, t=t, per=PER_ITEM)
                load_moe(t + 2, (0, 1), nxt + PER_ITEM, t=t, per=PER_ITEM)
            load_moe(NEXP - 1, range(2, PER_ITEM), nxt, t=NEXP - 2, per=PER_ITEM)
            sp.wait_ge(table_ready, 1)
            e = sp.value_load(table[0:1, 0:1], min_val=1, max_val=NEXP)
            load_moe(e - 1, (0, 1), nxt + PER_ITEM, t=NEXP - 2, per=PER_ITEM)
            more = sp.value_load(table[0:1, EXTRA + 1:EXTRA + 2], min_val=0, max_val=EXTRA)
            with sp.If(more > 0):
                with sp.Fori(0, more) as k:
                    e = sp.value_load(table[0:1, bass.ds(k, 1)], min_val=1, max_val=NEXP)
                    load_moe(e - 1, range(2, PER_ITEM), nxt, t=k + (NEXP - 1), per=PER_ITEM)
                    e = sp.value_load(table[0:1, bass.ds(k + 1, 1)], min_val=1, max_val=NEXP)
                    load_moe(e - 1, (0, 1), nxt + PER_ITEM, t=k + (NEXP - 1), per=PER_ITEM)
            for tt in range(TT):
                sp.wait_ge(normed, tt + 1)
                sp.dma_start(out_tok[:, tt, :], hn[:, tt, :]).then_inc(out_stored, 16)
            sp.wait_ge(out_stored, 16 * TT)

        @block.tensor
        def _(pe):
            mm = nc.tensor.matmul

            def transposed_norm(n):
                for tt in range(TT):
                    pe.wait_ge(hn_ready[n], tt + 1)
                    for k in range(KT):
                        b = 4 + 2 * tt + k // 4
                        last = nc.tensor.transpose(bank(b)[:, (k % 4) * P:(k % 4 + 1) * P], hn[:, tt, k * P:(k + 1) * P], ident)
                        if k % 4 == 3:
                            last.then_inc(hn_transposed[n], 1)
                        elif n == 0 and k % 4 < 2 and tt == 0:
                            last.then_inc(weights_used, 1)

            def product(out, stationary, moving, start, stop, **more):
                mm(out, stationary(0), moving(0), start=start, stop=False, **more)
                mm(out, stationary(0), moving(1), start=False, stop=False, **more)
                return mm(out, stationary(1), moving(0), start=False, stop=stop, **more)

            def take_load(n, t=0, per=0):
                pe.wait_ge(split_ready, t * per + (n + 1))

            def feature_major(b, n, src, t=0, per=0):
                take_load(n, t, per)
                for half in range(2):
                    for k in range(KT):
                        last = product(bank(b)[:, half * S:(half + 1) * S],
                                       lambda w: part(n, w, KT)[:, k, half * P:(half + 1) * P],
                                       lambda w: src[:, w, k, :], k == 0, k == KT - 1)
                last.then_inc(weights_used, 1)

            def token_major(b, n, src, t=0, per=0):
                take_load(n, t, per)
                for tt in range(TT):
                    for k in range(KT):
                        last = product(bank(b)[:, tt * 256:(tt + 1) * 256], lambda w: src[:, w, k, tt * P:(tt + 1) * P],
                                       lambda w: part(n, w, KT)[:, k, :], k == 0, k == KT - 1)
                last.then_inc(weights_used, 1)

            def output_rows(n, src, start, stop, first_done=None):
                for tt in range(TT):
                    for k in range(2):
                        for half in range(2):
                            last = product(bank(2 * tt + half), lambda w: src(w, k, tt),
                                           lambda w: part(n, w, 2)[:, k, half * 512:(half + 1) * 512],
                                           start and k == 0, stop and k == 1, skip_group_check=True)
                    if tt == 0 and first_done is not None:
                        last.then_inc(first_done, 1)
                last.then_inc(weights_used, 1)

            def mixer_projection(m, first, mixed_is_ready):
                for tt in range(TT):
                    pe.wait_ge(*mixed_is_ready[tt])
                    for k in range(KT):
                        b = 4 + 2 * tt + k // 4
                        last = nc.tensor.transpose(bank(b)[:, (k % 4) * P:(k % 4 + 1) * P], mixed[:, tt, k * P:(k + 1) * P], ident)
                        if k % 4 == 3:
                            last.then_inc(mixed_transposed[m], 1)
                pe.wait_ge(mixedT_ready[m], 2 * TT)
                for j in range(4):
                    take_load(first + j)
                    output_rows(first + j, lambda w, k, tt: hT[:, w, 2 * j + k, tt * P:(tt + 1) * P], j == 0, j == 3,
                                proj_out[m] if j == 3 else None)

            pe.wait_ge(consts_in, 16)
            transposed_norm(0)
            pe.wait_ge(hT_ready[0], 2 * TT)
            with pe.Fori(0, 4) as p:
                feature_major(0, HG, hT, p, 4)
                feature_major(1, HG + 1, hT, p, 4)
                token_major(2, HG + 2, hT, p, 4)
                pe.wait_ge(decayed, p * 2 + 1)
                for hh in range(2):
                    for tt in range(TT):
                        c = (2 * hh + tt) * P
                        last = mm(bank(5)[:, c:c + P], kdec[:, hh, tt * P:(tt + 1) * P], qdec[:, hh, tt * P:(tt + 1) * P],
                                  start=True, stop=True)
                last.then_inc(scores_hg_ready, 1)
                pe.wait_ge(decayed, p * 2 + 2)
                pe.wait_ge(o_gated, p + 1)
                for hh in range(2):
                    for tt in range(TT):
                        c = (2 * hh + tt) * P
                        last = nc.tensor.transpose(bank(4)[:, c:c + P], kend[:, hh, tt * P:(tt + 1) * P], ident)
                last.then_inc(kend_transposed, 1)
                token_major(3, HG + 3, hT, p, 4)
                pe.wait_ge(kend_copied, p + 1)
                pe.wait_ge(v_copied, p + 1)
                for hh in range(2):
                    for n in range(3):
                        q0 = CHUNK * (n % 2)
                        last = mm(chunk_kv(hh, n), kend_tok[q0:q0 + CHUNK, hh, n // 2, :],
                                  v_hg[q0:q0 + CHUNK, n // 2, hh * P:(hh + 1) * P], start=True, stop=True)
                last.then_inc(kv_ready, 1)
                pe.wait_ge(scores_hg_masked, p + 1)
                pe.wait_ge(states_ready, p + 1)
                for tt in range(TT):
                    for hh in range(2):
                        o = bank(4)[:, (2 * tt + hh) * P:(2 * tt + hh + 1) * P]
                        last = mm(o, scores_hg[:, hh, tt, :], v_hg[:, tt, hh * P:(hh + 1) * P], start=True, stop=False,
                                  skip_group_check=True)
                        for n in (2 * tt, 2 * tt + 1):
                            if n == 0:
                                continue
                            q0 = CHUNK * (n % 2)
                            last = mm(o[q0:q0 + CHUNK, :], qdec[:, hh, n * CHUNK:(n + 1) * CHUNK], states[:, hh, n - 1, :],
                                      start=False, stop=(n % 2 == 1), skip_group_check=True)
                last.then_inc(o_ready, 1)
            mixer_projection(0, HG_OUT, [(mixed_ready, tt + 1) for tt in range(TT)])

            transposed_norm(1)

            def ff_down(i, n, t=0, per=0, start=False, stop=False):
                take_load(n, t, per)
                pe.wait_ge(ff_act, i + 1)
                output_rows(n, lambda w, k, tt: act_ff_hl[:, w, k, tt * P:(tt + 1) * P], start, stop, ff_sum if stop else None)

            pe.wait_ge(hT_ready[1], 2 * TT)
            feature_major(4, FF, hT)
            feature_major(5, FF + 1, hT)
            pe.wait_ge(ff_silu, 1)
            feature_major(4, FF + 2, hT)
            ff_down(0, FF + 3, start=True)
            feature_major(5, FF + 4, hT)
            with pe.Fori(0, FF_PAIRS - 2) as t:
                pe.wait_ge(ff_silu, t + 2)
                feature_major(4, FF + 5, hT, t, 3)
                ff_down(t + 1, FF + 6, t, 3)
                feature_major(5, FF + 7, hT, t, 3)
            ff_down(FF_PAIRS - 1, AT - 1, stop=True)

            transposed_norm(2)
            pe.wait_ge(hT_ready[2], 4 * TT)
            with pe.Fori(0, GROUPS) as g:
                for j in range(2 * NBR):
                    if j >= 2:
                        pe.wait_ge(kq_read, g * 6 + (j - 1))
                    feature_major(j % 2, AT + j, hTkv if j < NBR else hT, g, 9)

                def v_slot(b):
                    if b < 2:
                        pe.wait_ge(kq_read, g * 6 + (5 + b))
                    else:
                        pe.wait_ge(va_copied, g * 3 + 1)
                    token_major(b % 2, AT + 2 * NBR + b, hTkv, g, 9)

                def scores(u):
                    hd, qt = u // 2, u % 2
                    a = HEAD * (hd % 2)
                    n = (qt + 1) * P
                    for b in range(NBR):
                        c = 512 * (2 + qt) + b * n
                        last = mm(ps[:, c:c + n], qbuf[b][a:a + HEAD, hd // 2, qt * P:(qt + 1) * P],
                                  kbuf[b][a:a + HEAD, hd // 2, 0:n], start=True, stop=True)
                    last.then_inc(s_ready, 1)

                def turn(u):
                    qt = u % 2
                    pe.wait_ge(exp_ready, g * UNITS + (u + 1))
                    if u:
                        pe.wait_ge(pT_dve, g * UNITS + u)
                        pe.wait_ge(pT_act, g * (UNITS // 2) + u // 2)
                    for j in range(NBR * (qt + 1)):
                        last = nc.tensor.transpose(ps[:, 512 * 5 + j * P:512 * 5 + (j + 1) * P], prob[qt][:, j * P:(j + 1) * P], ident)
                    last.then_inc(pT_ready, 1)

                def values(u):
                    hd, qt = u // 2, u % 2
                    pe.wait_ge(pT_dve, g * UNITS + (u + 1))
                    pe.wait_ge(pT_act, g * (UNITS // 2) + (u + 1) // 2)
                    if u:
                        pe.wait_ge(o_evac, g * UNITS + u)
                    n = NBR * (qt + 1)
                    for j in range(n):
                        b, kt = j // (qt + 1), j % (qt + 1)
                        last = mm(bank(7)[:, 0:HEAD], probT[qt][:, j, :], vbuf[:, kt, b, hd * HEAD:(hd + 1) * HEAD],
                                  start=(j == 0), stop=(j == n - 1))
                    last.then_inc(pv_ready, 1)

                pe.wait_ge(rope_done, g * 6 + 6)
                scores(0)
                v_slot(0)
                scores(1)
                v_slot(1)
                turn(0)
                v_slot(2)
                pe.wait_ge(va_copied, g * 3 + 3)
                for u in range(2, UNITS + 2):
                    if u < UNITS:
                        scores(u)
                    if u - 1 < UNITS:
                        turn(u - 1)
                    values(u - 2)
            mixer_projection(1, AT_OUT, [(o_evac, GROUPS * UNITS)] * TT)

            transposed_norm(3)
            pe.wait_ge(hT_ready[3], 2 * TT)
            for tt in range(TT):
                for k in range(KT):
                    last = mm(bank(0)[:, tt * NEXP:(tt + 1) * NEXP], hT_router[:, k, tt * P:(tt + 1) * P], router[:, k, :],
                              start=(k == 0), stop=(k == KT - 1))
            last.then_inc(logits_ready, 1)
            pe.wait_ge(chosen_ready, 1)
            ones, ustrict = cc("ones"), cc("ustrict")
            mm(bank(1)[:, 0:NEXP], ustrict, chosen[:, 0, :], start=True, stop=True)
            for c, w in ((1, ustrict), (2, ones)):
                mm(bank(1)[:, c * NEXP:(c + 1) * NEXP], ones, chosen[:, 0, :], start=True, stop=False)
                last = mm(bank(1)[:, c * NEXP:(c + 1) * NEXP], w, chosen[:, 1, :], start=False, stop=True)
            last.then_inc(places_ready, 1)

            def gather():
                for k in range(KT):
                    for tt in range(TT):
                        last = mm(bank(5 + k // 4)[:, (k % 4) * CAP:(k % 4 + 1) * CAP], hn[:, tt, k * P:(k + 1) * P],
                                  gatherP[:, tt, :], start=(tt == 0), stop=(tt == TT - 1))
                last.then_inc(gathered, 1)

            pe.wait_ge(built, 1)
            gather()
            pe.wait_ge(table_ready, 1)
            items = pe.value_load(table[0:1, EXTRA + 2:EXTRA + 3], min_val=NEXP, max_val=NEXP + EXTRA)
            with pe.Fori(0, items) as i:
                def turn_act(c):
                    pe.wait_ge(act_done, i * CHUNKS + (c + 1))
                    for f in range(4):
                        last = nc.tensor.transpose(bank(4)[:, f * CAP:(f + 1) * CAP], act_e[0:CAP, f * P:(f + 1) * P],
                                                   ident[0:CAP, 0:CAP])
                    last.then_inc(act_turned, 1)

                pe.wait_ge(xe_ready, i * 2 + 2)
                for j, (kind, c, half) in enumerate(MOE_LOADS):
                    n = MOE + j
                    if kind == "gate" and half == 0 and c > 0:
                        pe.wait_ge(silu_done, i * CHUNKS + c)
                    take_load(n, i, PER_ITEM)
                    if kind != "down":
                        for k in range(4):
                            last = product(bank(int(kind == "up"))[0:CAP, :], lambda w: xeT[:, w, 4 * half + k, :],
                                           lambda w: part(n, w, 4)[:, k, :], half == 0 and k == 0, half == 1 and k == 3)
                    else:
                        if half == 0:
                            pe.wait_ge(actT_ready, i * CHUNKS + (c + 1))
                        for d in range(2):
                            for k in range(2):
                                last = product(bank(2 + d)[0:CAP, :], lambda w: actT[:, w, 2 * half + k, :],
                                               lambda w: part(n, w, 2)[:, k, d * 512:(d + 1) * 512],
                                               c == 0 and half == 0 and k == 0, c == CHUNKS - 1 and half == 1 and k == 1,
                                               skip_group_check=True)
                            if j == PER_ITEM - 1 and d == 0:
                                last.then_inc(y_half, 1)
                    last.then_inc(weights_used, 1)
                    if j == 2:
                        for tt in range(TT):
                            last = nc.tensor.transpose(bank(7)[0:CAP, tt * P:(tt + 1) * P], scatterP[:, tt, :], ident)
                        last.then_inc(sT_transposed, 1)
                    if kind == "gate" and half == 0 and c > 0:
                        turn_act(c - 1)
                    if j == PER_ITEM - 3:
                        turn_act(CHUNKS - 1)
                        pe.wait_ge(built, i + 2)
                        gather()
                pe.wait_ge(sT_ready, i + 1)
                pe.wait_ge(xe_ready, i * 2 + 4)
                for tt in range(TT):
                    for d in range(2):
                        if tt == 0:
                            pe.wait_ge((yt_act, yt_dve)[d], i + 1)
                        mm(bank(4 + 2 * tt + d), scatterT[0:CAP, tt * P:(tt + 1) * P],
                           ytok[0:CAP, d * 512:(d + 1) * 512], start=True, stop=True).then_inc(scattered, 1)

        @block.scalar
        def _(act):
            a = nc.scalar.activation
            own = Chain(act, act_own)

            def inverse_norm(n, sem_of, values, own=own):
                for tt in range(TT):
                    act.wait_ge(sem_of, values[tt])
                    own(a(hn[:, tt, :], h[:, tt, :], ACT.Square, accum_out=ssq[:, tt:tt + 1]))
                    own(a(ssq[:, tt:tt + 1], ssq[:, tt:tt + 1], ACT.Ln, bias=eps, scale=1.0 / D))
                    a(rstd[:, tt:tt + 1], ssq[:, tt:tt + 1], ACT.Exp, scale=-0.5).then_inc(rstd_ready[n], 1)

            def used(n, t=0, per=0):
                act.wait_ge(weights_used, t * per + (n + 1 + PRIMED))

            def hi(n, t=0, per=0):
                back = distance(SPLIT_OF, n, per)
                if back:
                    used(n - back, t, per)
                after = landed(n + per) - landed(n) if per else 0
                act.wait_ge(slot_filled[RAW_OF[n]], t * after + landed(n))
                nc.scalar.copy(split[:, SPLIT_OF[n], 0, :], raw[:, RAW_OF[n], :]).then_inc(hi_ready, 1)

            def hi_norm(n, targets):
                for x in range(2 * TT * len(targets)):
                    act.wait_ge(staged[n], x + 1)
                    y = x // len(targets)
                    dst = targets[x % len(targets)]
                    nc.scalar.copy(dst[:, 0, 4 * (y % 2):4 * (y % 2) + 4, (y // 2) * P:(y // 2 + 1) * P],
                                   stage[:, x % 2, :, :]).then_inc(hT_hi[n], 1)

            def hi_mixed(m, first):
                hi(first + 2)
                for y in range(2 * TT):
                    act.wait_ge(mixed_transposed[m], y + 1)
                    nc.scalar.copy(hT[:, 0, 4 * (y % 2):4 * (y % 2) + 4, (y // 2) * P:(y // 2 + 1) * P],
                                   bank(4 + y).rearrange("p (a b) -> p a b", a=4)).then_inc(mixedT_hi[m], 1)
                hi(first + 3)
                hi(first + 4)

            act.preload_act_table_set("natural_log_exp_and_others")
            act.wait_ge(consts_in, 16)
            inverse_norm(0, x_in, [16 * TT] * TT)
            act.wait_ge(bounds_shifted, 1)
            a(lbound[:, 2:4, :], lbound[:, 2:4, :], ACT.Exp).then_inc(bounds_exp, 1)
            hi(HG)
            hi(HG + 1)
            hi_norm(0, [hT])

            with act.Fori(0, 4) as p:
                used(HG, p, 4)
                a(decay_in, bank(0).rearrange("p (a b) -> p a b", a=2), ACT.Exp, scale=-1.0).then_inc(f_exp, 1)
                hi(HG + 2, p, 4)
                act.wait_ge(f_done, p + 1)
                a(logf, forget, ACT.Ln).then_inc(f_log, 1)
                act.wait_ge(b_done, p + 1)
                a(eb, bsum, ACT.Exp)
                a(enb, bsum, ACT.Exp, scale=-1.0).then_inc(b_exps, 1)
                act.wait_ge(bdiff_done, p + 1)
                a(eend, bdiff, ACT.Exp).then_inc(bend_exp, 1)
                hi(HG + 3, p, 4)
                used(HG + 2, p, 4)
                nc.scalar.copy(v_hg, bank(2).rearrange("p (a b) -> p a b", a=2)).then_inc(v_copied, 1)
                act.wait_ge(kend_transposed, p + 1)
                nc.scalar.copy(kend_tok, bank(4).rearrange("p (a b c) -> p a b c", a=2, b=TT)).then_inc(kend_copied, 1)
                hi(HG + 4, p, 4)
                used(HG + 3, p, 4)
                a(gate_hg, bank(3).rearrange("p (a b) -> p a b", a=2), ACT.Exp, scale=-1.0).then_inc(g_exp, 1)
                hi(HG + 5, p, 4)
                act.wait_ge(o_ready, p + 1)
                a(square_hg, bank(4).rearrange("p (a b) -> p a b", a=2), ACT.Square).then_inc(o_squared, 1)
            act.wait_ge(o_gated, 5)
            own(a(orstd[:, :, :, :], ossq[:, :, :, :], ACT.Ln, bias=eps, scale=1.0 / P))
            a(orstd[:, :, :, :], orstd[:, :, :, :], ACT.Exp, scale=-0.5).then_inc(orstd_ready, 1)
            hi_mixed(0, HG_OUT)
            inverse_norm(1, h_ready[1], [2, 4])
            hi(FF + 1)
            hi_norm(1, [hT])

            act.preload_act_table_set("silu_and_others")
            hi(FF + 2)
            used(FF)
            a(silu_ff, bank(4).rearrange("p (a b) -> p a b", a=2), ACT.Silu).then_inc(ff_silu, 1)
            hi(FF + 3)
            with act.Fori(0, FF_PAIRS - 1) as t:
                hi(FF + 4, t, 3)
                used(FF + 2, t, 3)
                act.wait_ge(ff_act, t + 1)
                a(silu_ff, bank(4).rearrange("p (a b) -> p a b", a=2), ACT.Silu).then_inc(ff_silu, 1)
                hi(FF + 5, t, 3)
                hi(FF + 6, t, 3)
            act.preload_act_table_set("natural_log_exp_and_others")
            inverse_norm(2, h_ready[2], [2, 4])
            hi(AT + 1)
            hi_norm(2, [hT, hTkv])

            with act.Fori(0, GROUPS) as g:
                for j in range(2 * NBR + 1):
                    hi(AT + 2 + j, g, 9)

                def exps(u):
                    act.wait_ge(max_ready, g * UNITS + (u + 1))
                    a(prob[u % 2], prob[u % 2], ACT.Exp, bias=negmax[:, u:u + 1], scale=SCALE,
                      accum_out=rowsum[:, u:u + 1]).then_inc(exp_ready, 1)

                def value_copy(b):
                    used(AT + 2 * NBR + b, g, 9)
                    nc.scalar.copy(vbuf[:, :, b, :], bank(b % 2).rearrange("p (a b) -> p a b", a=TT)).then_inc(va_copied, 1)

                exps(0)
                value_copy(0)
                hi(AT + 9, g, 9)
                exps(1)
                value_copy(1)
                hi(AT + 10, g, 9)
                value_copy(2)
                for u in range(2, UNITS + 1):
                    if u < UNITS:
                        exps(u)
                    if u % 2 == 0:
                        act.wait_ge(pT_ready, g * UNITS + u)
                        nc.scalar.copy(probT[1][:, 0:4, :], bank(5).rearrange("p (a b) -> p a b", a=4)).then_inc(pT_act, 1)
            hi_mixed(1, AT_OUT)
            inverse_norm(3, h_ready[3], [2, 4])
            hi(MOE + 1)

            act.wait_ge(shifted, 1)
            a(probs, probs, ACT.Exp).then_inc(exped, 1)

            act.preload_act_table_set("silu_and_others")
            act.wait_ge(table_ready, 1)
            items = act.value_load(table[0:1, EXTRA + 2:EXTRA + 3], min_val=NEXP, max_val=NEXP + EXTRA)

            def tokens_hi(i):
                for q in range(2):
                    act.wait_ge(xe_staged, i * 2 + (q + 1))
                    nc.scalar.copy(xeT[:, 0, 4 * q:4 * q + 4, :], xe_stage[:, 4 * q:4 * q + 4, :]).then_inc(xe_hi, 1)

            def actT_round(c, i):
                act.wait_ge(act_turned, i * CHUNKS + (c + 1))
                nc.scalar.copy(actT[:, 0, :, :], bank(4)[:, 0:4 * CAP].rearrange("p (a b) -> p a b", a=4)).then_inc(actT_hi, 1)

            tokens_hi(0)
            with act.Fori(0, items) as i:
                for j in range(PER_ITEM):
                    kind, c, half = MOE_LOADS[j - 1]
                    if j and kind == "gate" and half == 1:
                        used(MOE + j - 1, i, PER_ITEM)
                        a(silu_e[0:CAP, :], bank(0)[0:CAP, :], ACT.Silu).then_inc(silu_done, 1)
                    if j and kind == "gate" and half == 0 and c > 0:
                        actT_round(c - 1, i)
                    if j == PER_ITEM - 2:
                        actT_round(CHUNKS - 1, i)
                    hi(MOE + j + 2, i, PER_ITEM)
                    if j == PER_ITEM - 2:
                        tokens_hi(i + 1)
                act.wait_ge(y_half, i + 1)
                nc.scalar.copy(ytok[0:CAP, 0:512], bank(2)[0:CAP, :]).then_inc(yt_act, 1)
            act.preload_act_table_set("natural_log_exp_and_others")
            inverse_norm(4, added, [items * 4] * TT, own=Chain(act, act_own_end))

        @block.vector
        def _(dve):
            v = nc.vector
            own = Chain(dve, dve_own)

            def wide(ap, n):
                return ap.unsqueeze(len(ap.shape)).to_broadcast(list(ap.shape) + [n])

            def two(ap):
                return ap.unsqueeze(1).to_broadcast([ap.shape[0], 2, ap.shape[1]])

            def used(n, t=0, per=0):
                dve.wait_ge(weights_used, t * per + (n + 1 + PRIMED))

            def lo(n, t=0, per=0):
                s = SPLIT_OF[n]
                dve.wait_ge(hi_ready, t * per + (n + 1))
                v.tensor_tensor(split[:, s, 1, :], raw[:, RAW_OF[n], :], split[:, s, 0, :].bitcast(F32),
                                ALU.subtract).then_inc(split_ready, 1)

            def scale_norm(n):
                for tt in range(TT):
                    dve.wait_ge(rstd_ready[n], tt + 1)
                    v.tensor_scalar(hn[:, tt, :], h[:, tt, :], rstd[:, tt:tt + 1], None, ALU.mult).then_inc(hn_ready[n], 1)

            def split_norm(n, targets):
                count = 2 * TT * len(targets)
                for x in range(count + 1):
                    if x < count:
                        y, (dst, gain) = x // len(targets), targets[x % len(targets)]
                        if x >= 2:
                            dve.wait_ge(hT_ready[n], x - 1)
                        dve.wait_ge(hn_transposed[n], y + 1)
                        v.tensor_tensor(stage[:, x % 2, :, :], bank(4 + y).rearrange("p (a b) -> p a b", a=4),
                                        wide(gain[:, 4 * (y % 2):4 * (y % 2) + 4], P), ALU.mult).then_inc(staged[n], 1)
                    if x:
                        y, (dst, gain) = (x - 1) // len(targets), targets[(x - 1) % len(targets)]
                        q, c = slice(4 * (y % 2), 4 * (y % 2) + 4), slice((y // 2) * P, (y // 2 + 1) * P)
                        dve.wait_ge(hT_hi[n], x)
                        v.tensor_tensor(dst[:, 1, q, c], stage[:, (x - 1) % 2, :, :], dst[:, 0, q, c].bitcast(F32),
                                        ALU.subtract).then_inc(hT_ready[n], 1)

            def mixer_output(m, n, first):
                lo(first + 2)
                for y in range(2 * TT):
                    q, c = slice(4 * (y % 2), 4 * (y % 2) + 4), slice((y // 2) * P, (y // 2 + 1) * P)
                    dve.wait_ge(mixedT_hi[m], y + 1)
                    v.tensor_tensor(hT[:, 1, q, c], bank(4 + y).rearrange("p (a b) -> p a b", a=4),
                                    hT[:, 0, q, c].bitcast(F32), ALU.subtract).then_inc(mixedT_ready[m], 1)
                lo(first + 3)
                lo(first + 4)
                residual(n, proj_out[m], first + 3)

            def residual(n, first_done, last_load):
                for j in range(4):
                    tt, half = j // 2, j % 2
                    if j == 0:
                        dve.wait_ge(first_done, 1)
                    if j == 2:
                        used(last_load)
                    piece = h[:, tt, half * 512:(half + 1) * 512]
                    v.tensor_tensor(piece, piece, bank(j), ALU.add).then_inc(h_ready[n], 1)

            dve.wait_ge(params_in, 16)
            own(v.tensor_tensor(lbound[:, 0, :], bounds[:, 0, :], bounds[:, 1, :], ALU.max))
            v.tensor_tensor(lbound[:, 2:4, :], bounds, two(lbound[:, 0, :]), ALU.subtract).then_inc(bounds_shifted, 1)
            dve.wait_ge(x_in, 16 * TT)
            scale_norm(0)
            dve.wait_ge(bounds_exp, 1)
            own(v.tensor_tensor(lbound[:, 0, :], lbound[:, 2, :], lbound[:, 3, :], ALU.add))
            own(v.reciprocal(lbound[:, 1, :], lbound[:, 0, :]))
            own(v.tensor_tensor(lbound[:, 2, :], lbound[:, 2, :], lbound[:, 1, :], ALU.mult))
            v.tensor_scalar(lbound[:, 3, :], lbound[:, 2, :], -1.0, 1.0, ALU.mult, ALU.add).then_inc(o_gated, 1)
            dve.wait_ge(o_gated, 1)
            lo(HG)
            lo(HG + 1)
            split_norm(0, [(hT, attn_gain[:, 0, :])])

            flat = "p a b -> p (a b)"
            mask = cc("hgmask").bitcast(U32)
            with dve.Fori(0, 4) as p:
                own.enter(p, 8)
                dve.wait_ge(f_exp, p + 1)
                own(v.tensor_scalar(decay_in, decay_in, 1.0, None, ALU.add))
                own(v.reciprocal(decay_in, decay_in))
                for hh in range(2):
                    last = v.tensor_scalar(forget[:, hh, :], decay_in[:, hh, :], lbound[:, 3, bass.ds(p * 2 + hh, 1)],
                                           lbound[:, 2, bass.ds(p * 2 + hh, 1)], ALU.mult, ALU.add)
                last.then_inc(f_done, 1)
                dve.wait_ge(f_done, p + 1)
                v.tensor_scalar(keyk, forget, -1.0, 1.0, ALU.mult, ALU.add)
                lo(HG + 2, p, 4)
                dve.wait_ge(f_log, p + 1)
                v.tensor_tensor_scan(bsum.rearrange(flat), cc("reset"), logf.rearrange(flat), 0.0,
                                     ALU.mult, ALU.add).then_inc(b_done, 1)
                dve.wait_ge(b_done, p + 1)
                chunks = bsum.rearrange("p a (n c) -> p (a n) c", c=CHUNK)
                v.tensor_tensor(bdiff.rearrange("p a (n c) -> p (a n) c", c=CHUNK),
                                chunks[:, :, CHUNK - 1:CHUNK].to_broadcast([P, 2 * S // CHUNK, CHUNK]), chunks,
                                ALU.subtract).then_inc(bdiff_done, 1)
                dve.wait_ge(b_exps, p + 1)
                used(HG + 1, p, 4)
                v.tensor_tensor(qdec, bank(1).rearrange("p (a b) -> p a b", a=2), eb, ALU.mult)
                v.tensor_tensor(kdec, keyk, enb, ALU.mult).then_inc(decayed, 1)
                dve.wait_ge(bend_exp, p + 1)
                v.tensor_tensor(kend, keyk, eend, ALU.mult).then_inc(decayed, 1)
                lo(HG + 3, p, 4)
                dve.wait_ge(zeroed, 1)
                dve.wait_ge(scores_hg_ready, p + 1)
                v.copy_predicated(scores_hg.rearrange("p a b c -> p (a b) c"),
                                  mask.unsqueeze(1).to_broadcast([P, 4, P]),
                                  bank(5).rearrange("p (a c) -> p a c", a=4)).then_inc(scores_hg_masked, 1)
                lo(HG + 4, p, 4)
                dve.wait_ge(kv_ready, p + 1)
                own(v.tensor_copy(states[:, :, 0, :], bank(6).rearrange("p (a b) -> p a b", a=2)[:, :, 0:P]))
                for n in (1, 2):
                    for hh in range(2):
                        last = v.scalar_tensor_tensor(out=states[:, hh, n, :], in0=states[:, hh, n - 1, :],
                                                      scalar=eb[:, hh, (n + 1) * CHUNK - 1:(n + 1) * CHUNK],
                                                      in1=chunk_kv(hh, n), op0=ALU.mult, op1=ALU.add)
                    if n == 1:
                        own(last)
                last.then_inc(states_ready, 1)
                dve.wait_ge(g_exp, p + 1)
                own(v.tensor_scalar(gate_hg, gate_hg, 1.0, None, ALU.add))
                own(v.reciprocal(gate_hg, gate_hg))
                own(v.tensor_tensor(gate_hg, bank(3).rearrange("p (a b) -> p a b", a=2), gate_hg, ALU.mult))
                g4 = gate_hg.rearrange("p a (b c) -> p (a b) c", b=2)
                own(v.tensor_tensor(g4, g4, pp("out_norm").unsqueeze(1).to_broadcast([P, 4, P]), ALU.mult))
                lo(HG + 5, p, 4)
                dve.wait_ge(o_squared, p + 1)
                v.tensor_reduce(ossq[:, bass.ds(p, 1), :, :].rearrange("p x a b -> p (x a b)"),
                                square_hg.rearrange("p a (b c) -> p (a b) c", b=2), AX.X, ALU.add)
                v.tensor_tensor(mixed[:, :, bass.ds(p * 256, 256)], bank(4).rearrange("p (a b) -> p a b", a=2), gate_hg,
                                ALU.mult).then_inc(o_gated, 1)
            own.leave(4)
            dve.wait_ge(orstd_ready, 1)
            for tt in range(TT):
                for hh in range(2):
                    m4 = mixed[:, tt, :].rearrange("p (a b c) -> p a b c", a=4, b=2)[:, :, hh, :]
                    last = v.tensor_tensor(m4, m4, wide(orstd[:, :, tt, hh], P), ALU.mult)
                last.then_inc(mixed_ready, 1)
            mixer_output(0, 1, HG_OUT)
            scale_norm(1)
            lo(FF + 1)
            split_norm(1, [(hT, ffn_gain[:, 0, :])])

            def ff_activation(n, i, t=0, per=0):
                dve.wait_ge(ff_silu, i + 1)
                used(n, t, per)
                own(v.tensor_tensor(act_ff, silu_ff, bank(5).rearrange("p (a b) -> p a b", a=2), ALU.mult))
                own(v.tensor_copy(act_ff_hl[:, 0, :, :], act_ff))
                v.tensor_tensor(act_ff_hl[:, 1, :, :], act_ff, act_ff_hl[:, 0, :, :].bitcast(F32), ALU.subtract).then_inc(ff_act, 1)

            lo(FF + 2)
            lo(FF + 3)
            ff_activation(FF + 1, 0)
            with dve.Fori(0, FF_PAIRS - 1) as t:
                own.enter(t, 2)
                lo(FF + 4, t, 3)
                lo(FF + 5, t, 3)
                lo(FF + 6, t, 3)
                ff_activation(FF + 4, t + 1, t, 3)
            own.leave(FF_PAIRS - 1)
            residual(2, ff_sum, AT - 1)
            scale_norm(2)
            lo(AT + 1)
            split_norm(2, [(hT, attn_gain[:, 1, :]), (hTkv, kv_gain)])

            cos, sin = cc("cos"), cc("sin")
            with dve.Fori(0, GROUPS) as g:
                own.enter(g, 2 * UNITS)

                def rope(j):
                    buf = (kbuf + qbuf)[j]
                    src = bank(j % 2).rearrange("p (a b) -> p a b", a=2)
                    used(AT + j, g, 9)
                    v.tensor_tensor(buf, src, two(cos), ALU.mult)
                    if j:
                        dve.wait_ge(rope_done, g * 6 + j)
                    for q in range(4):
                        a, b = 32 * q, 32 * (q ^ 1)
                        last = v.tensor_tensor(rot[b:b + 32], src[a:a + 32], two(sin[a:a + 32, :]), ALU.mult)
                    last.then_inc(kq_read, 1)

                def row_max(u):
                    qt = u % 2
                    n = NBR * P * (qt + 1)
                    dve.wait_ge(s_ready, g * UNITS + (u + 1))
                    v.memset(negmax[:, u:u + 1], 0.0)
                    own(v.tensor_tensor_reduce(prob[qt], ps[:, 512 * (2 + qt):512 * (2 + qt) + n], cc(f"mask{qt}"), 1.0, -3e38,
                                               ALU.add, ALU.max, rowmax[:, u:u + 1]))
                    v.tensor_scalar(negmax[:, u:u + 1], rowmax[:, u:u + 1], -SCALE, None, ALU.mult).then_inc(max_ready, 1)

                def turned(u):
                    dve.wait_ge(pT_ready, g * UNITS + (u + 1))
                    if u % 2 == 0:
                        dst, src = probT[0], bank(5)[:, 0:NBR * P]
                    else:
                        dst, src = probT[1][:, 4:6, :], bank(6)[:, 0:2 * P]
                    v.tensor_copy(dst, src.rearrange("p (a b) -> p a b", b=P)).then_inc(pT_dve, 1)

                def output(u):
                    hd, qt = u // 2, u % 2
                    dve.wait_ge(pv_ready, g * UNITS + (u + 1))
                    own(v.reciprocal(rowinv[:, u:u + 1], rowsum[:, u:u + 1]))
                    v.tensor_scalar(mixed[:, qt, bass.ds(g * 256 + hd * HEAD, HEAD)], bank(7)[:, 0:HEAD], rowinv[:, u:u + 1],
                                    None, ALU.mult).then_inc(o_evac, 1)

                for j in range(2 * NBR):
                    lo(AT + 2 + j, g, 9)
                    rope(j)
                lo(AT + 2 + 2 * NBR, g, 9)
                for u in range(UNITS + 2):
                    if u < UNITS:
                        row_max(u)
                    if u == 1:
                        lo(AT + 9, g, 9)
                        lo(AT + 10, g, 9)
                    if 1 <= u < UNITS + 1:
                        turned(u - 1)
                    if u >= 2:
                        output(u - 2)
            own.leave(GROUPS)
            mixer_output(1, 3, AT_OUT)
            scale_norm(3)
            for y in range(2 * TT):
                dve.wait_ge(hn_transposed[3], y + 1)
                v.tensor_tensor(hT_router[:, 4 * (y % 2):4 * (y % 2) + 4, (y // 2) * P:(y // 2 + 1) * P],
                                bank(4 + y).rearrange("p (a b) -> p a b", a=4),
                                wide(ffn_gain[:, 1, 4 * (y % 2):4 * (y % 2) + 4], P), ALU.mult).then_inc(hT_ready[3], 1)
            lo(MOE + 1)

            experts = cc("experts")
            lg = bank(0)[:, 0:TT * NEXP].rearrange("p (t e) -> p t e", t=TT)
            dve.wait_ge(logits_ready, 1)
            own(v.tensor_reduce(r1[:, 0:2], lg, AX.X, ALU.max))
            v.tensor_tensor(probs, lg, wide(r1[:, 0:2], NEXP), ALU.subtract).then_inc(shifted, 1)
            dve.wait_ge(exped, 1)
            own(v.tensor_reduce(r1[:, 2:4], probs, AX.X, ALU.add))
            own(v.reciprocal(r1[:, 4:6], r1[:, 2:4]))
            own(v.tensor_tensor(probs, probs, wide(r1[:, 4:6], NEXP), ALU.mult))
            for tt in range(TT):
                last = v.max(top[:, tt, :], probs[:, tt, :])
            own(last)
            for tt in range(TT):
                last = v.max_index(topi[:, tt, :], top[:, tt, :], probs[:, tt, :])
            own(last)
            v.tensor_copy(topf, topi)
            own(v.tensor_tensor(r1[:, 0:2], top[:, :, 0], top[:, :, 1], ALU.add))
            own(v.reciprocal(r1[:, 2:4], r1[:, 0:2]))
            own(v.tensor_tensor(top[:, :, 0:2], top[:, :, 0:2], wide(r1[:, 2:4], 2), ALU.mult))
            for tt in range(TT):
                v.tensor_scalar(onehot[:, tt, :], experts, topf[:, tt, 0:1], None, ALU.is_equal)
                v.tensor_scalar(chosen[:, tt, :], experts, topf[:, tt, 1:2], None, ALU.is_equal)
                v.tensor_scalar(wa[:, tt, :], experts, topf[:, tt, 0:1], top[:, tt, 0:1], ALU.is_equal, ALU.mult)
                last = v.tensor_scalar(place[:, tt, :], experts, topf[:, tt, 1:2], top[:, tt, 1:2], ALU.is_equal, ALU.mult)
            own(last)
            v.tensor_tensor(chosen, chosen, onehot, ALU.add).then_inc(chosen_ready, 1)
            v.memset(key[:, ITEMS - 1, :], ABSENT)
            v.memset(weight[:, ITEMS - 1, :], 0.0)
            w8 = weight[:, 0:NEXP, :].rearrange("p e t -> p t e")
            k8 = key[:, 0:NEXP, :].rearrange("p e t -> p t e")
            own(v.tensor_tensor(w8, wa, place, ALU.add))
            dve.wait_ge(places_ready, 1)
            dve.wait_ge(chosen_ready, 1)
            own(v.tensor_scalar(place, bank(1)[:, 0:TT * NEXP].rearrange("p (t e) -> p t e", t=TT), -ABSENT, None, ALU.add))
            own(v.tensor_copy(counts, bank(1)[:, TT * NEXP:(TT + 1) * NEXP]))
            own(v.tensor_tensor(place, place, chosen, ALU.mult))
            own(v.tensor_scalar(k8, place, ABSENT, None, ALU.add))

            def build(i, chain):
                chain(v.tensor_tensor(gatherP, cc("places").unsqueeze(1).to_broadcast([P, TT, CAP]),
                                      wide(key[:, bass.ds(i, 1), :].rearrange("p x t -> p (x t)"), CAP), ALU.is_equal))
                v.tensor_tensor(scatterP, gatherP, wide(weight[:, bass.ds(i, 1), :].rearrange("p x t -> p (x t)"), CAP),
                                ALU.mult).then_inc(built, 1)

            build(0, own)
            base3 = cc("over_base").rearrange("p (b e) -> p b e", b=BLOCKS)

            def over(ap):
                return ap.unsqueeze(1).to_broadcast([P, BLOCKS, NEXP])

            def each(ap):
                return ap.unsqueeze(1).to_broadcast([P, EXTRA, nj])

            own(v.tensor_tensor(active.rearrange("p (b e) -> p b e", b=BLOCKS), over(counts), base3, ALU.is_gt))
            own(v.tensor_tensor_scan(order, cc("ones")[:, 0:nj], active, 0.0, ALU.mult, ALU.add))
            v.tensor_reduce(tablef[:, EXTRA + 1:EXTRA + 2], active, AX.X, ALU.add)
            v.memset(tablef[:, EXTRA:EXTRA + 1], 1.0)
            own(v.tensor_tensor(order, order, active, ALU.subtract))
            own(v.tensor_scalar(order, order, -ABSENT, None, ALU.add))
            own(v.tensor_tensor(order, order, active, ALU.mult))
            own(v.tensor_scalar(order, order, ABSENT, None, ALU.add))
            own(v.tensor_tensor(sel, each(order), cc("over_k").rearrange("p (k j) -> p k j", k=EXTRA), ALU.is_equal))
            own(v.tensor_tensor(prod, sel, each(cc("over_e")), ALU.mult))
            v.tensor_scalar(tablef[:, EXTRA + 2:EXTRA + 3], tablef[:, EXTRA + 1:EXTRA + 2], float(NEXP), None, ALU.add)
            own(v.tensor_reduce(tablef[:, 0:EXTRA], prod, AX.X, ALU.add))
            own(v.tensor_scalar(tablef[:, 0:EXTRA], tablef[:, 0:EXTRA], 1.0, None, ALU.max))
            v.tensor_copy(table[:, :], tablef).then_inc(table_ready, 1)

            def tokens_in(i):
                dve.wait_ge(gathered, i + 1)
                for q in range(2):
                    v.tensor_tensor(xe_stage[:, 4 * q:4 * q + 4, :], bank(5 + q)[:, 0:4 * CAP].rearrange("p (a b) -> p a b", a=4),
                                    wide(ffn_gain[:, 1, 4 * q:4 * q + 4], CAP), ALU.mult).then_inc(xe_staged, 1)

            def tokens_lo(i):
                for q in range(2):
                    dve.wait_ge(xe_hi, i * 2 + (q + 1))
                    v.tensor_tensor(xeT[:, 1, 4 * q:4 * q + 4, :], xe_stage[:, 4 * q:4 * q + 4, :],
                                    xeT[:, 0, 4 * q:4 * q + 4, :].bitcast(F32), ALU.subtract).then_inc(xe_ready, 1)

            def actT_rest(c, i):
                dve.wait_ge(actT_hi, i * CHUNKS + (c + 1))
                v.tensor_tensor(actT[:, 1, :, :], bank(4)[:, 0:4 * CAP].rearrange("p (a b) -> p a b", a=4),
                                actT[:, 0, :, :].bitcast(F32), ALU.subtract).then_inc(actT_ready, 1)

            tokens_in(0)
            tokens_lo(0)
            for tt in range(TT):
                k3 = keymod[:, tt, :].rearrange("p (b e) -> p b e", b=BLOCKS)
                own(v.tensor_tensor(k3, over(key[:, 0:NEXP, tt]), base3, ALU.subtract))
                own(v.tensor_tensor(prod, sel, each(keymod[:, tt, :]), ALU.mult))
                own(v.tensor_reduce(key[:, NEXP:NEXP + EXTRA, tt], prod, AX.X, ALU.add))
                own(v.tensor_copy(k3, over(weight[:, 0:NEXP, tt])))
                own(v.tensor_tensor(prod, sel, each(keymod[:, tt, :]), ALU.mult))
                own(v.tensor_reduce(weight[:, NEXP:NEXP + EXTRA, tt], prod, AX.X, ALU.add))
            dve.wait_ge(table_ready, 1)
            items = dve.value_load(table[0:1, EXTRA + 2:EXTRA + 3], min_val=NEXP, max_val=NEXP + EXTRA)
            with dve.Fori(0, items) as i:
                own.enter(i, 1)
                for j in range(PER_ITEM):
                    kind, c, half = MOE_LOADS[j - 1]
                    if j and kind == "up" and half == 1:
                        dve.wait_ge(silu_done, i * CHUNKS + (c + 1))
                        used(MOE + j - 1, i, PER_ITEM)
                        v.tensor_tensor(act_e[0:CAP, :], silu_e[0:CAP, :], bank(1)[0:CAP, :], ALU.mult).then_inc(act_done, 1)
                    if j and kind == "gate" and half == 0 and c > 0:
                        actT_rest(c - 1, i)
                    if j == PER_ITEM - 2:
                        actT_rest(CHUNKS - 1, i)
                        tokens_in(i + 1)
                    lo(MOE + j + 2, i, PER_ITEM)
                    if j == PER_ITEM - 2:
                        tokens_lo(i + 1)
                    if j == 3:
                        dve.wait_ge(sT_transposed, i + 1)
                        v.tensor_copy(scatterT[0:CAP, :], bank(7)[0:CAP, 0:S]).then_inc(sT_ready, 1)
                        build(i + 1, own)
                used(MOE + PER_ITEM - 1, i, PER_ITEM)
                v.tensor_copy(ytok[0:CAP, 512:1024], bank(3)[0:CAP, :]).then_inc(yt_dve, 1)
                for j in range(4):
                    tt, half = j // 2, j % 2
                    dve.wait_ge(scattered, i * 4 + (j + 1))
                    piece = h[:, tt, half * 512:(half + 1) * 512]
                    v.tensor_tensor(piece, piece, bank(4 + j), ALU.add).then_inc(added, 1)

            dve.wait_ge(added, items * 4)
            for tt in range(TT):
                dve.wait_ge(rstd_ready[4], tt + 1)
                v.scalar_tensor_tensor(out=hn[:, tt, :], in0=h[:, tt, :], scalar=rstd[:, tt:tt + 1], in1=pp("final_norm"),
                                       op0=ALU.mult, op1=ALU.mult).then_inc(normed, 1)

        @block.gpsimd
        def _(pool):
            nc.gpsimd.memset(scores_hg, 0.0).then_inc(zeroed, 1)
            with pool.Fori(0, GROUPS) as g:
                for j in range(2 * NBR):
                    buf = (kbuf + qbuf)[j]
                    pool.wait_ge(kq_read, g * 6 + (j + 1))
                    nc.gpsimd.tensor_tensor(buf, buf, rot, ALU.add).then_inc(rope_done, 1)


_INS = ["x", "hgrn_w_in", "hgrn_w_out", "w_kv", "dil_w_q", "dil_w_out", "ffn_w_gate", "ffn_w_up", "ffn_w_down",
        "moe_w_gate", "moe_w_up", "moe_w_down"]


def kernel(**inputs):
    import concourse.bacc as bacc
    from concourse.bass_utils import run_bass_kernel_spmd

    def per_partition(a):
        a = np.asarray(a).reshape(-1, KT, P)
        return np.moveaxis(a, 2, 0).reshape(P, -1)

    router = np.asarray(inputs["moe_w_router"])[0].reshape(KT, P, NEXP)
    parts = {
        "attn_norm": per_partition(inputs["attn_norm"]),
        "ffn_norm": per_partition(inputs["ffn_norm"]),
        "kv_norm": per_partition(inputs["kv_norm"]),
        "bounds": per_partition(inputs["hgrn_lower_bounds"]),
        "router": np.moveaxis(router, 1, 0).reshape(P, -1),
        "out_norm": np.broadcast_to(np.asarray(inputs["hgrn_out_norm"])[0], (P, P)),
        "final_norm": np.broadcast_to(np.asarray(inputs["final_norm"]), (P, D)),
    }
    arrays = {name: np.ascontiguousarray(inputs[name]) for name in _INS}
    arrays["consts"] = constants()
    arrays["params"] = np.ascontiguousarray(np.concatenate([parts[n] for n in PARAMS], 1))
    nc = bacc.Bacc("TRN2", target_bir_lowering=False, num_devices=1)
    aps = {n: nc.dram_tensor(f"in_{n}", a.shape, mybir.dt.from_np(a.dtype), kind="ExternalInput").ap()
           for n, a in arrays.items()}
    out = nc.dram_tensor("out", (1, S, D), F32, kind="ExternalOutput").ap()
    trunk_kernel(nc, aps, aps["consts"], aps["params"], out)
    r = run_bass_kernel_spmd(nc, [{f"in_{n}": a for n, a in arrays.items()}], core_ids=[0])
    return r.results[0]["out"]
```

```python
from contextlib import ExitStack

import numpy as np

import concourse.bass as bass
from concourse import mybir

ACT = mybir.ActivationFunctionType
ALU = mybir.AluOpType
AX = mybir.AxisListType
F32 = mybir.dt.float32
FR = mybir.dt.float32r
I32 = mybir.dt.int32
U32 = mybir.dt.uint32

P = 128
D = 1024
S = 256
KT = D // P
TT = S // P
CHUNK = 64
HEAD = 64
NBR = 3
DILS = (1, 4, 16)
BAND = 128
DFF = 2816
DEXP = 3584
NEXP = 8
CAP = 96
EXTRA = (2 * S) // (CAP + 1)
BLOCKS = -(-S // CAP) - 1
ITEMS = NEXP + EXTRA + 1
EPS = 1e-6
SCALE = HEAD ** -0.5
ABSENT = -1000.0
LNEXP_SET = 6
FF_PAIRS = DFF // 256
GROUPS = 4
UNITS = 8
SLOT = 2048
CHUNKS = DEXP // 512
PER_ITEM = 6 * CHUNKS
PRIMED = 4

RAWS, SPLITS = 7, 3
MORE_RAWS = 2
RAW_OF, SPLIT_OF = [], []


def _phase(times, raw, split):
    first = len(RAW_OF)
    RAW_OF.extend(raw * times)
    SPLIT_OF.extend(split * times)
    return first


HG = _phase(4, [0, 1, 2, 3], [0, 1, 2, 1])
HG_OUT = _phase(1, [0, 1, 2, 3], [0, 1, 2, 0])
FF = _phase(FF_PAIRS, [0, 1, 2], [1, 2, 0])
AT = _phase(GROUPS, [0, 1, 2, 3, 4, 5, 6, 3, 4], [1, 2, 0] * 3)
AT_OUT = _phase(1, [0, 1, 2, 3], [1, 2, 0, 1])
MOE = _phase(3, [j for turn in (9, 9, 8, 8, 8) for j in range(turn)], [(j + 2) % SPLITS for j in range(PER_ITEM)])
MOE_LOADS = [(kind, c if kind != "down" else c - 1, half) for c in range(CHUNKS + 1) for kind in ("gate", "up", "down")
             for half in range(2) if (kind == "down" and c > 0) or (kind != "down" and c < CHUNKS)]


def distance(slots, n, per):
    last = [n - m for n_ in (n,) for m in range(n_ - 1, -1, -1) if slots[m] == slots[n_]][:1]
    if per and n + per < len(slots):
        last += [n + per - m for m in range(n + per - 1, -1, -1) if slots[m] == slots[n + per]][:1]
        assert slots[n] == slots[n + per], n
    return min(last) if last else None


def landed(n):
    return 16 * sum(RAW_OF[m] == RAW_OF[n] for m in range(n + 1))


CONSTS = {}
_at = 0
for _name, _n in (("ident", P), ("eps", 1), ("one", 1), ("ustrict", P), ("ones", P), ("hgmask", P), ("places", CAP),
                  ("experts", NEXP), ("over_k", EXTRA * BLOCKS * NEXP), ("over_e", BLOCKS * NEXP),
                  ("over_base", BLOCKS * NEXP), ("reset", 2 * S), ("cos", S), ("sin", S),
                  ("mask0", NBR * P), ("mask1", NBR * S)):
    CONSTS[_name] = (_at, _at + _n)
    _at += _n
NCONST = _at
assert NCONST - CONSTS["reset"][0] >= SLOT
NEARLY = P + 2
PARAMS = {}
_at = 0
for _name, _n in (("bounds", 2 * KT), ("router", KT * NEXP), ("out_norm", P)):
    PARAMS[_name] = (_at, _at + _n)
    _at += _n
NPARAM = _at


def constants():
    c = np.zeros((P, NCONST), np.float32)

    def put(name, value):
        a, b = CONSTS[name]
        c[:, a:b] = np.broadcast_to(np.asarray(value, np.float32), (P, b - a))

    r = np.arange(P)
    put("ident", np.eye(P))
    put("ustrict", r[:, None] < r[None, :])
    put("ones", np.ones((P, P)))
    put("hgmask", (r[:, None] <= r[None, :]) & (r[:, None] // CHUNK == r[None, :] // CHUNK))
    put("reset", (np.arange(2 * S) % CHUNK != 0)[None])
    put("places", np.arange(CAP)[None])
    put("experts", np.arange(NEXP)[None])
    nj = BLOCKS * NEXP
    put("over_k", np.repeat(np.arange(EXTRA), nj)[None])
    put("over_e", np.tile(np.arange(NEXP) + 1, BLOCKS)[None])
    put("over_base", (CAP * (1 + np.repeat(np.arange(BLOCKS), NEXP)))[None])
    put("eps", np.full((P, 1), EPS))
    put("one", np.ones((P, 1)))
    half = HEAD // 2
    inv = np.float32(10000.0) ** (-np.arange(half, dtype=np.float32) / np.float32(half))
    ang = np.arange(S, dtype=np.float32)[None, :] * inv[:, None].astype(np.float32)
    put("cos", np.tile(np.cos(ang), (4, 1)))
    put("sin", np.concatenate([np.sin(ang), -np.sin(ang)] * 2, 0))
    for tt, name in ((0, "mask0"), (1, "mask1")):
        q = tt * P + r[:, None]
        k = np.arange((tt + 1) * P)[None, :]
        ok = [(k <= q) & ((q - k) % dil == 0) & (q - k <= BAND * dil) for dil in DILS]
        put(name, np.concatenate([np.where(m, 0.0, -1e30) for m in ok], 1))
    return c


class Chain:

    def __init__(self, eng, sem):
        self.eng, self.sem, self.base, self.n, self.i, self.per = eng, sem, 0, 0, 0, 0

    def __call__(self, ins):
        self.n += 1
        ins.then_inc(self.sem, 1)
        self.eng.wait_ge(self.sem, self.i * self.per + (self.base + self.n))

    def enter(self, i, per):
        self.base, self.n, self.i, self.per = self.base + self.n, 0, i, per

    def leave(self, trips):
        assert self.n == self.per, (self.n, self.per)
        self.base, self.n, self.i, self.per = self.base + trips * self.per, 0, 0, 0


def trunk_kernel(nc, t, out):
    with ExitStack() as ctx:
        def sb(name, shape, dt=F32):
            return ctx.enter_context(nc.sbuf_tensor(name, shape, dt))

        def sem(name):
            return ctx.enter_context(nc.semaphore(name))

        raw = sb("raw", [P, RAWS, SLOT])
        split = sb("split", [P, SPLITS, 2, SLOT], FR)
        cst = sb("cst", [P, NCONST])
        par = sb("par", [P, NPARAM])
        h = sb("h", [P, TT, D])
        hn = sb("hn", [P, TT, D])
        mixed = hn
        hT = sb("hT", [P, 2, KT, S], FR)
        gain = sb("gain", [P, 2, D])
        frarena = sb("frarena", [P, 2 * KT * S], FR)
        ssq = sb("ssq", [P, TT])
        rstd = sb("rstd", [P, TT])
        arena_floats = 8192
        arena = sb("arena", [P, arena_floats])
        table = sb("table", [P, EXTRA + 3], I32)

        def carve(arena=arena):
            used = [0]

            def take(*shape):
                n = int(np.prod(shape))
                a = arena[:, used[0]:used[0] + n]
                used[0] += n
                assert used[0] <= arena.shape[1], used
                names = "wxyz"[:len(shape)]
                if len(shape) == 1:
                    return a
                return a.rearrange(f"p ({' '.join(names)}) -> p {' '.join(names)}", **dict(zip(names, shape)))
            return take

        ps = ctx.enter_context(nc.psum_tensor("ps", [P, 8 * 512], F32))

        def bank(b, n=512):
            return ps[:, 512 * b:512 * b + n]

        def chunk_kv(hh, n):
            c = (2 * hh + n // 2) * P if n % 2 == 0 else hh * P
            return bank(6 + n % 2)[:, c:c + P]

        def cc(name):
            a, b = CONSTS[name]
            return cst[:, a:b]

        def pp(name):
            a, b = PARAMS[name]
            return par[:, a:b]

        ident, eps, one = cc("ident"), cc("eps"), cc("one")
        bounds = pp("bounds").rearrange("p (l k) -> p l k", l=2)
        router = pp("router").rearrange("p (k e) -> p k e", k=KT)

        def raw_of(n):
            s = RAW_OF[n]
            if s < RAWS:
                return raw[:, s, :]
            if s == RAWS:
                return cst[:, CONSTS["reset"][0]:CONSTS["reset"][0] + SLOT]
            return arena[:, 0:SLOT]

        def part(n, w, k):
            return split[:, SPLIT_OF[n], w, :].rearrange("p (k n) -> p k n", k=k)

        take = carve()
        decay_in = take(2, S)
        logf = decay_in
        forget = take(2, S)
        bdiff = eend = kend = forget
        keyk = take(2, S)
        bsum = take(2, S)
        eb = take(2, S)
        enb = take(2, S)
        kdec = enb
        qdec = take(2, S)
        kend_tok = take(2, TT, P)
        v_hg = take(TT, 2 * P)
        scores_hg = take(2, TT, P)
        states = take(2, 3, P)
        gate_hg = take(TT, 2 * P)
        square_hg = take(TT, 2 * P)
        lbound = sb("lbound", [P, 4, KT])
        ossq = sb("ossq", [P, 4, TT, 2])
        orstd = sb("orstd", [P, 4, TT, 2])
        take = carve()
        silu_ff = take(2, S)
        act_ff = take(2, S)
        act_ff_hl = carve(frarena)(2, 2, 2, S)
        take = carve()
        hTkv = carve(frarena)(2, KT, S)
        hn_kv = arena[:, 0:TT * D].rearrange("p (a b) -> p a b", a=TT)
        kbuf = [take(2, S) for _ in range(NBR)]
        qbuf = [take(2, S) for _ in range(NBR)]
        vbuf = take(TT, NBR, 256)
        rot = take(2, S)
        prob = [take(NBR * P), take(NBR * S)]
        probT = [take(NBR, P), take(NBR * 2, P)]
        rowmax = sb("rowmax", [P, UNITS])
        negmax = sb("negmax", [P, UNITS])
        rowsum = sb("rowsum", [P, UNITS])
        rowinv = sb("rowinv", [P, UNITS])
        take = carve()
        hT_router = take(KT, S)
        probs = take(TT, NEXP)
        top = take(TT, 8)
        topi = take(TT, 8).bitcast(U32)
        topf = take(TT, 8)
        r1 = take(8)
        onehot = take(TT, NEXP)
        wa = take(TT, NEXP)
        chosen = take(TT, NEXP)
        place = take(TT, NEXP)
        key = take(ITEMS, TT)
        weight = take(ITEMS, TT)
        nj = BLOCKS * NEXP
        counts = take(NEXP)
        active = take(nj)
        order = take(nj)
        sel = take(EXTRA, nj)
        prod = take(EXTRA, nj)
        keymod = take(TT, nj)
        tablef = take(EXTRA + 3)
        gatherP = take(TT, CAP)
        scatterP = take(TT, CAP)
        scatterT = take(S)
        silu_e = take(512)
        act_e = take(512)
        ytok = take(D)
        take = carve(frarena)
        xeT = take(2, KT, CAP)
        actT = take(2, 4, CAP)

        slot_filled = [sem(f"slot_filled{s}") for s in range(RAWS + MORE_RAWS)]
        hi_ready, split_ready, weights_used = sem("hi_ready"), sem("split_ready"), sem("weights_used")
        x_in = [sem(f"x_in{tt}") for tt in range(TT)]
        consts_in, tables_in, params_in = sem("consts_in"), sem("tables_in"), sem("params_in")
        gain_in = [sem("gain_in0"), sem("gain_in1")]
        out_stored = sem("out_stored")
        act_own, dve_own, pool_own = sem("act_own"), sem("dve_own"), sem("pool_own")
        act_own_end, dve_own_end = sem("act_own_end"), sem("dve_own_end")
        bounds_shifted, bounds_exp = sem("bounds_shifted"), sem("bounds_exp")
        zeroed = sem("zeroed")
        NN = 5
        rstd_ready = [sem(f"rstd_ready{n}") for n in range(NN)]
        hn_ready = [sem(f"hn_ready{n}") for n in range(NN)]
        hn_transposed = [sem(f"hn_transposed{n}") for n in range(NN)]
        hT_ready = [sem(f"hT_ready{n}") for n in range(NN)]
        hT_hi = [sem(f"hT_hi{n}") for n in range(NN)]
        h_ready = [sem(f"h_ready{n}") for n in range(NN)]
        f_sigmoid, f_done, f_log, b_done = sem("f_sigmoid"), sem("f_done"), sem("f_log"), sem("b_done")
        bdiff_done, b_exps, bend_exp = sem("bdiff_done"), sem("b_exps"), sem("bend_exp")
        decayed, kend_transposed, kend_copied = sem("decayed"), sem("kend_transposed"), sem("kend_copied")
        v_copied, scores_hg_ready, scores_hg_masked = sem("v_copied"), sem("scores_hg_ready"), sem("scores_hg_masked")
        kv_ready, states_ready, g_sigmoid = sem("kv_ready"), sem("states_ready"), sem("g_sigmoid")
        f_softplus, f_logsig, g_softplus, g_logsig = (sem(n) for n in ("f_softplus", "f_logsig", "g_softplus", "g_logsig"))
        o_ready, o_squared, o_gated = sem("o_ready"), sem("o_squared"), sem("o_gated")
        orstd_ready = sem("orstd_ready")
        mixed_ready = sem("mixed_ready")
        mixed_transposed = [sem("mixed_transposed0"), sem("mixed_transposed1")]
        mixedT_hi = [sem("mixedT_hi0"), sem("mixedT_hi1")]
        mixedT_ready = [sem("mixedT_ready0"), sem("mixedT_ready1")]
        proj_out = [sem("proj_out0"), sem("proj_out1")]
        ff_silu, ff_act, ff_sum = sem("ff_silu"), sem("ff_act"), sem("ff_sum")
        kq_read, rope_done, va_copied = sem("kq_read"), sem("rope_done"), sem("va_copied")
        s_ready, max_ready, exp_ready = sem("s_ready"), sem("max_ready"), sem("exp_ready")
        pT_ready, pT_dve, pT_act, pv_ready, o_evac = (sem("pT_ready"), sem("pT_dve"), sem("pT_act"), sem("pv_ready"),
                                                      sem("o_evac"))
        logits_ready, shifted, exped, chosen_ready, places_ready = (
            sem("logits_ready"), sem("shifted"), sem("exped"), sem("chosen_ready"), sem("places_ready"))
        table_ready = sem("table_ready")
        built, gathered, xe_hi, xe_ready = (sem(n) for n in ("built", "gathered", "xe_hi", "xe_ready"))
        sT_transposed, sT_ready = sem("sT_transposed"), sem("sT_ready")
        silu_done, act_done, act_turned, actT_hi, actT_ready = (sem(n) for n in (
            "silu_done", "act_done", "act_turned", "actT_hi", "actT_ready"))
        y_half, yt_act, yt_dve = sem("y_half"), sem("yt_act"), sem("yt_dve")
        scattered, added = sem("scattered"), [sem(f"added{tt}") for tt in range(TT)]
        normed = sem("normed")

        w_in = t["hgrn_w_in"][0].rearrange("(k p) n -> p k n", p=P)
        w_kv = t["w_kv"].rearrange("(k p) n -> p k n", p=P)
        w_q = t["dil_w_q"][0].rearrange("(k p) n -> p k n", p=P)
        hg_out = t["hgrn_w_out"][0].rearrange("(k p) n -> p k n", p=P)
        at_out = t["dil_w_out"][0].rearrange("(k p) n -> p k n", p=P)
        ff_g = t["ffn_w_gate"][0].rearrange("(k p) n -> p k n", p=P)
        ff_u = t["ffn_w_up"][0].rearrange("(k p) n -> p k n", p=P)
        ff_d = t["ffn_w_down"][0].rearrange("(k p) n -> p k n", p=P)
        moe_g = t["moe_w_gate"][0].rearrange("e (k p) n -> e p k n", p=P)
        moe_u = t["moe_w_up"][0].rearrange("e (k p) n -> e p k n", p=P)
        moe_d = t["moe_w_down"][0].rearrange("e (k p) n -> e p k n", p=P)
        consts, params, gains = t["consts"], t["params"], t["gains"]
        x_tok = t["x"][0].rearrange("(t p) d -> p t d", p=P)
        out_tok = out[0].rearrange("(t p) d -> p t d", p=P)

        NORM_PARTS = [[(dst, src, tt, q, b + 2 * tt + q) for tt in range(TT) for dst, src, b in targets for q in range(2)]
                      for targets in ([(hT, hn, 4)], [(hT, hn, 4)], [(hT, hn, 4), (hTkv, hn_kv, 0)], [(None, hn, 4)])]

        block = ctx.enter_context(nc.Block())

        @block.sync
        def _(sp):
            def load(n, src, t=0, per=0):
                back = distance(RAW_OF, n, per)
                if back:
                    sp.wait_ge(split_ready, t * per + (n - back + 1))
                k = src.shape[1]
                sp.dma_start(raw_of(n).rearrange("p (k n) -> p k n", k=k), src).then_inc(slot_filled[RAW_OF[n]], 16)

            def load_hg(p, first, order=(1, 0, 2, 3), **loop):
                for j in order:
                    c = (1, 0, 2, 3)[j]
                    load(first + j, w_in[:, :, bass.ds(p * 256 + c * D, 256)], **loop)

            def load_out(first, w):
                for j in range(4):
                    load(first + j, w[:, 2 * j:2 * j + 2, :])

            def load_ff(kind, i, n, **loop):
                if kind == "down":
                    load(n, ff_d[:, bass.ds(i * 2, 2), :], **loop)
                else:
                    load(n, (ff_g if kind == "gate" else ff_u)[:, :, bass.ds(i * 256, 256)], **loop)

            def load_att(g, first, **loop):
                for j in range(3 * NBR):
                    w, c = ((w_kv, 0), (w_q, 0), (w_kv, NBR * D))[j // NBR]
                    load(first + j, w[:, :, bass.ds(g * 256 + (c + j % NBR * D), 256)], **loop)

            def load_moe(e, js, first, **loop):
                for j in js:
                    kind, c, half = MOE_LOADS[j]
                    if kind == "down":
                        src = moe_d[e, :, 4 * c + 2 * half:4 * c + 2 * half + 2, :]
                    else:
                        src = (moe_g if kind == "gate" else moe_u)[e, :, 4 * half:4 * half + 4, 512 * c:512 * c + 512]
                    load(first + j, src, **loop)

            def load_gain(g, row):
                sp.dma_start(gain[:, row, :], gains[:, g, :]).then_inc(gain_in[row], 16)

            sp.dma_start(h[:, 0, :], x_tok[:, 0, :]).then_inc(x_in[0], 16)
            sp.dma_start(cst[:, 0:NEARLY], consts[:, 0:NEARLY]).then_inc(consts_in, 16)
            sp.dma_start(par[:, :], params).then_inc(params_in, 16)
            load_gain(0, 0)
            sp.dma_start(h[:, 1, :], x_tok[:, 1, :]).then_inc(x_in[1], 16)
            load_hg(0, HG, order=(0, 1, 2, 3))
            sp.dma_start(cst[:, NEARLY:], consts[:, NEARLY:]).then_inc(tables_in, 16)
            load_gain(1, 1)
            with sp.Fori(0, 3) as t:
                load_hg(t + 1, HG + 4, t=t, per=4)
            load_out(HG_OUT, hg_out)
            sp.wait_ge(hn_ready[0], 2 * TT)
            load_gain(2, 0)
            load_ff("gate", 0, FF)
            load_ff("up", 0, FF + 1)
            with sp.Fori(0, FF_PAIRS - 2) as t:
                load_ff("gate", t + 1, FF + 2, t=t, per=3)
                load_ff("down", t, FF + 3, t=t, per=3)
                load_ff("up", t + 1, FF + 4, t=t, per=3)
            load_ff("gate", FF_PAIRS - 1, AT - 4)
            load_ff("up", FF_PAIRS - 1, AT - 3)
            load_ff("down", FF_PAIRS - 2, AT - 2)
            load_ff("down", FF_PAIRS - 1, AT - 1)
            sp.wait_ge(hn_ready[1], 2 * TT)
            load_gain(3, 1)
            load_att(0, AT)
            with sp.Fori(0, GROUPS - 1) as t:
                load_att(t + 1, AT + 9, t=t, per=9)
            load_out(AT_OUT, at_out)
            sp.wait_ge(hn_ready[2], 4 * TT)
            load_gain(4, 0)
            load_gain(5, 1)
            load_moe(0, range(RAWS), MOE)
            sp.wait_ge(o_evac, GROUPS * UNITS)
            load_moe(0, (RAWS,), MOE)
            sp.wait_ge(logits_ready, 1)
            load_moe(0, range(RAWS + 1, PER_ITEM), MOE)
            nxt = MOE + PER_ITEM
            ahead, rest = (0, 1), range(2, PER_ITEM)
            load_moe(1, ahead, nxt)
            with sp.Fori(0, NEXP - 2) as t:
                load_moe(t + 1, rest, nxt, t=t, per=PER_ITEM)
                load_moe(t + 2, ahead, nxt + PER_ITEM, t=t, per=PER_ITEM)
            load_moe(NEXP - 1, rest, nxt, t=NEXP - 2, per=PER_ITEM)
            sp.wait_ge(table_ready, 1)
            e = sp.value_load(table[0:1, 0:1], min_val=1, max_val=NEXP)
            load_moe(e - 1, ahead, nxt + PER_ITEM, t=NEXP - 2, per=PER_ITEM)
            more = sp.value_load(table[0:1, EXTRA + 1:EXTRA + 2], min_val=0, max_val=EXTRA)
            with sp.If(more > 0):
                with sp.Fori(0, more) as k:
                    e = sp.value_load(table[0:1, bass.ds(k, 1)], min_val=1, max_val=NEXP)
                    load_moe(e - 1, rest, nxt, t=k + (NEXP - 1), per=PER_ITEM)
                    e = sp.value_load(table[0:1, bass.ds(k + 1, 1)], min_val=1, max_val=NEXP)
                    load_moe(e - 1, ahead, nxt + PER_ITEM, t=k + (NEXP - 1), per=PER_ITEM)
            load_moe(0, (2,), nxt + PER_ITEM, t=more + (NEXP - 2), per=PER_ITEM)
            for tt in range(TT):
                sp.wait_ge(normed, tt + 1)
                sp.dma_start(out_tok[:, tt, :], hn[:, tt, :]).then_inc(out_stored, 16)
            sp.wait_ge(out_stored, 16 * TT)

        @block.tensor
        def _(pe):
            mm = nc.tensor.matmul

            def transposed_norm(n):
                for x, (dst, src, tt, q, b) in enumerate(NORM_PARTS[n]):
                    pe.wait_ge(hn_ready[n], x + 1)
                    for k in range(4):
                        last = nc.tensor.transpose(bank(b)[:, k * P:(k + 1) * P], src[:, tt, (4 * q + k) * P:(4 * q + k + 1) * P], ident)
                        if k == 3:
                            last.then_inc(hn_transposed[n], 1)
                        elif n == 0 and k < 2 and tt == 0:
                            last.then_inc(weights_used, 1)

            def product(out, stationary, moving, start, stop, **more):
                mm(out, stationary(0), moving(0), start=start, stop=False, **more)
                mm(out, stationary(0), moving(1), start=False, stop=False, **more)
                return mm(out, stationary(1), moving(0), start=False, stop=stop, **more)

            def take_load(n, t=0, per=0):
                pe.wait_ge(split_ready, t * per + (n + 1))

            def feature_major(b, n, src, t=0, per=0, halves=(0, 1)):
                take_load(n, t, per)
                for half in halves:
                    for k in range(KT):
                        last = product(bank(b)[:, half * S:(half + 1) * S],
                                       lambda w: part(n, w, KT)[:, k, half * P:(half + 1) * P],
                                       lambda w: src[:, w, k, :], k == 0, k == KT - 1)
                if halves[-1] == 1:
                    last.then_inc(weights_used, 1)

            def token_major(b, n, src, t=0, per=0):
                take_load(n, t, per)
                for tt in range(TT):
                    for k in range(KT):
                        last = product(bank(b)[:, tt * 256:(tt + 1) * 256], lambda w: src[:, w, k, tt * P:(tt + 1) * P],
                                       lambda w: part(n, w, KT)[:, k, :], k == 0, k == KT - 1)
                last.then_inc(weights_used, 1)

            def output_rows(loads, start=False, first_done=None):
                for tt in range(TT):
                    for n, src in loads:
                        end = first_done is not None and n == loads[-1][0]
                        for k in range(2):
                            for half in range(2):
                                last = product(bank(2 * tt + half), lambda w: src(w, k, tt),
                                               lambda w: part(n, w, 2)[:, k, half * 512:(half + 1) * 512],
                                               start and k == 0, end and k == 1, skip_group_check=True)
                        if tt == TT - 1:
                            last.then_inc(weights_used, 1)
                        elif end:
                            last.then_inc(first_done, 1)

            def mixer_projection(m, first, mixed_is_ready):
                for tt in range(TT):
                    pe.wait_ge(*mixed_is_ready[tt])
                    for k in range(KT):
                        b = 4 + 2 * tt + k // 4
                        last = nc.tensor.transpose(bank(b)[:, (k % 4) * P:(k % 4 + 1) * P], mixed[:, tt, k * P:(k + 1) * P], ident)
                        if k % 4 == 3:
                            last.then_inc(mixed_transposed[m], 1)

                def rows(j):
                    take_load(first + j)
                    return first + j, lambda w, k, tt: hT[:, w, 2 * j + k, tt * P:(tt + 1) * P]

                pe.wait_ge(mixedT_ready[m], 2 * TT - 1)
                output_rows([rows(0)], start=True)
                output_rows([rows(1)])
                pe.wait_ge(mixedT_ready[m], 2 * TT)
                output_rows([rows(2), rows(3)], first_done=proj_out[m])

            pe.wait_ge(consts_in, 16)
            transposed_norm(0)
            pe.wait_ge(hT_ready[0], 2 * TT)
            feature_major(0, HG, hT)

            def head_pair(p):
                feature_major(1, HG + 1, hT, p, 4)
                token_major(2, HG + 2, hT, p, 4)
                pe.wait_ge(o_gated, p + 1)
                token_major(3, HG + 3, hT, p, 4)
                pe.wait_ge(decayed, p * 2 + 2)
                for hh in range(2):
                    for tt in range(TT):
                        c = (2 * hh + tt) * P
                        last = nc.tensor.transpose(bank(4)[:, c:c + P], kend[:, hh, tt * P:(tt + 1) * P], ident)
                last.then_inc(kend_transposed, 1)
                for hh in range(2):
                    for tt in range(TT):
                        c = (2 * hh + tt) * P
                        last = mm(bank(5)[:, c:c + P], kdec[:, hh, tt * P:(tt + 1) * P], qdec[:, hh, tt * P:(tt + 1) * P],
                                  start=True, stop=True)
                last.then_inc(scores_hg_ready, 1)
                pe.wait_ge(kend_copied, p + 1)
                pe.wait_ge(v_copied, p + 1)
                for hh in range(2):
                    for n in range(3):
                        q0 = CHUNK * (n % 2)
                        last = mm(chunk_kv(hh, n), kend_tok[q0:q0 + CHUNK, hh, n // 2, :],
                                  v_hg[q0:q0 + CHUNK, n // 2, hh * P:(hh + 1) * P], start=True, stop=True)
                last.then_inc(kv_ready, 1)

            def head_outputs(p):
                pe.wait_ge(scores_hg_masked, p + 1)
                pe.wait_ge(states_ready, p + 1)
                for tt in range(TT):
                    for hh in range(2):
                        o = bank(4)[:, (2 * tt + hh) * P:(2 * tt + hh + 1) * P]
                        last = mm(o, scores_hg[:, hh, tt, :], v_hg[:, tt, hh * P:(hh + 1) * P], start=True, stop=False,
                                  skip_group_check=True)
                        for n in (2 * tt, 2 * tt + 1):
                            if n == 0:
                                continue
                            q0 = CHUNK * (n % 2)
                            last = mm(o[q0:q0 + CHUNK, :], qdec[:, hh, n * CHUNK:(n + 1) * CHUNK], states[:, hh, n - 1, :],
                                      start=False, stop=(n % 2 == 1), skip_group_check=True)
                last.then_inc(o_ready, 1)

            with pe.Fori(0, 3) as p:
                head_pair(p)
                feature_major(0, HG + 4, hT, p, 4)
                head_outputs(p)
            head_pair(3)
            head_outputs(3)
            mixer_projection(0, HG_OUT, [(mixed_ready, tt + 1) for tt in range(TT)])

            transposed_norm(1)

            def ff_down(i, n, t=0, per=0, buf=0):
                take_load(n, t, per)
                pe.wait_ge(ff_act, i + 1)
                return n, lambda w, k, tt: act_ff_hl[:, buf, w, k, tt * P:(tt + 1) * P]

            pe.wait_ge(hT_ready[1], 2 * TT)
            feature_major(4, FF, hT)
            feature_major(5, FF + 1, hT)
            pe.wait_ge(ff_silu, 1)
            feature_major(4, FF + 2, hT)
            output_rows([ff_down(0, FF + 3)], start=True)
            feature_major(5, FF + 4, hT)
            with pe.Fori(0, FF_PAIRS - 3) as t:
                pe.wait_ge(ff_silu, t + 2)
                feature_major(4, FF + 5, hT, t, 3)
                output_rows([ff_down(t + 1, FF + 6, t, 3)])
                feature_major(5, FF + 7, hT, t, 3)
            pe.wait_ge(ff_silu, FF_PAIRS - 1)
            feature_major(4, AT - 4, hT)
            pe.wait_ge(ff_act, FF_PAIRS - 1)
            feature_major(5, AT - 3, hT)
            output_rows([ff_down(FF_PAIRS - 2, AT - 2)])
            output_rows([ff_down(FF_PAIRS - 1, AT - 1, buf=1)], first_done=ff_sum)

            transposed_norm(2)
            pe.wait_ge(hT_ready[2], 4 * TT)
            def head_group(g, more):
                for j in range(1, 2 * NBR):
                    if j >= 2:
                        pe.wait_ge(kq_read, g * 6 + (j - 1))
                    feature_major(j % 2, AT + j, hTkv if j < NBR else hT, g, 9)

                def v_slot(b):
                    if b < 2:
                        pe.wait_ge(kq_read, g * 6 + (5 + b))
                    else:
                        pe.wait_ge(va_copied, g * 3 + 1)
                    token_major(b % 2, AT + 2 * NBR + b, hTkv, g, 9)

                def scores(u):
                    hd, qt = u // 2, u % 2
                    a = HEAD * (hd % 2)
                    n = (qt + 1) * P
                    for b in range(NBR):
                        c = 512 * (2 + qt) + b * n
                        last = mm(ps[:, c:c + n], qbuf[b][a:a + HEAD, hd // 2, qt * P:(qt + 1) * P],
                                  kbuf[b][a:a + HEAD, hd // 2, 0:n], start=True, stop=True)
                    last.then_inc(s_ready, 1)

                def turn(u):
                    qt = u % 2
                    pe.wait_ge(exp_ready, g * UNITS + (u + 1))
                    if u >= 2:
                        pe.wait_ge(pT_dve, g * UNITS + (u - 1))
                        if qt == 1:
                            pe.wait_ge(pT_act, g * (UNITS // 2) + u // 2)
                    for j in range(NBR * (qt + 1)):
                        c = 512 * (1, 5)[qt] + j * P
                        last = nc.tensor.transpose(ps[:, c:c + P], prob[qt][:, j * P:(j + 1) * P], ident)
                    last.then_inc(pT_ready, 1)

                def values(u):
                    hd, qt = u // 2, u % 2
                    pe.wait_ge(pT_dve, g * UNITS + (u + 1))
                    pe.wait_ge(pT_act, g * (UNITS // 2) + (u + 1) // 2)
                    if u:
                        pe.wait_ge(o_evac, g * UNITS + u)
                    n = NBR * (qt + 1)
                    for j in range(n):
                        b, kt = j // (qt + 1), j % (qt + 1)
                        last = mm(bank(7)[:, 0:HEAD], probT[qt][:, j, :], vbuf[:, kt, b, hd * HEAD:(hd + 1) * HEAD],
                                  start=(j == 0), stop=(j == n - 1))
                    last.then_inc(pv_ready, 1)

                v_slot(0)
                v_slot(1)
                pe.wait_ge(rope_done, g * 6 + 6)
                scores(0)
                scores(1)
                v_slot(2)
                pe.wait_ge(va_copied, g * 3 + 2)
                turn(0)
                pe.wait_ge(va_copied, g * 3 + 3)
                for u in range(2, UNITS + 2):
                    if u < UNITS:
                        scores(u)
                    if more and u >= UNITS:
                        feature_major(0, AT + 9, hTkv, g, 9, halves=(u - UNITS,))
                    if u - 1 < UNITS:
                        turn(u - 1)
                    values(u - 2)

            feature_major(0, AT, hTkv)
            with pe.Fori(0, GROUPS - 1) as g:
                head_group(g, True)
            head_group(GROUPS - 1, False)
            mixer_projection(1, AT_OUT, [(o_evac, GROUPS * UNITS)] * TT)

            transposed_norm(3)
            pe.wait_ge(hT_ready[3], 2 * TT)
            for tt in range(TT):
                for k in range(KT):
                    last = mm(bank(0)[:, tt * NEXP:(tt + 1) * NEXP], hT_router[:, k, tt * P:(tt + 1) * P], router[:, k, :],
                              start=(k == 0), stop=(k == KT - 1))
            last.then_inc(logits_ready, 1)
            pe.wait_ge(chosen_ready, 1)
            ones, ustrict = cc("ones"), cc("ustrict")
            mm(bank(1)[:, 0:NEXP], ustrict, chosen[:, 0, :], start=True, stop=True)
            for c, w in ((1, ustrict), (2, ones)):
                mm(bank(1)[:, c * NEXP:(c + 1) * NEXP], ones, chosen[:, 0, :], start=True, stop=False)
                last = mm(bank(1)[:, c * NEXP:(c + 1) * NEXP], w, chosen[:, 1, :], start=False, stop=True)
            last.then_inc(places_ready, 1)

            def gather():
                for k in range(KT):
                    for tt in range(TT):
                        last = mm(bank(5 + k // 4)[:, (k % 4) * CAP:(k % 4 + 1) * CAP], hn[:, tt, k * P:(k + 1) * P],
                                  gatherP[:, tt, :], start=(tt == 0), stop=(tt == TT - 1))
                    if k % 4 == 3:
                        last.then_inc(gathered, 1)

            pe.wait_ge(built, 1)
            gather()
            pe.wait_ge(table_ready, 1)
            items = pe.value_load(table[0:1, EXTRA + 2:EXTRA + 3], min_val=NEXP, max_val=NEXP + EXTRA)
            with pe.Fori(0, items) as i:
                def turn_act(c):
                    pe.wait_ge(act_done, i * CHUNKS + (c + 1))
                    for f in range(4):
                        last = nc.tensor.transpose(bank(4)[:, f * CAP:(f + 1) * CAP], act_e[0:CAP, f * P:(f + 1) * P],
                                                   ident[0:CAP, 0:CAP])
                    last.then_inc(act_turned, 1)

                pe.wait_ge(xe_ready, i * 2 + 2)
                for j, (kind, c, half) in enumerate(MOE_LOADS):
                    n = MOE + j
                    if kind == "gate" and half == 0 and c > 0:
                        pe.wait_ge(silu_done, i * CHUNKS + c)
                    take_load(n, i, PER_ITEM)
                    if kind != "down":
                        for k in range(4):
                            last = product(bank(int(kind == "up"))[0:CAP, :], lambda w: xeT[:, w, 4 * half + k, :],
                                           lambda w: part(n, w, 4)[:, k, :], half == 0 and k == 0, half == 1 and k == 3)
                    else:
                        if half == 0:
                            pe.wait_ge(actT_ready, i * CHUNKS + (c + 1))
                        for d in range(2):
                            for k in range(2):
                                last = product(bank(2 + d)[0:CAP, :], lambda w: actT[:, w, 2 * half + k, :],
                                               lambda w: part(n, w, 2)[:, k, d * 512:(d + 1) * 512],
                                               c == 0 and half == 0 and k == 0, c == CHUNKS - 1 and half == 1 and k == 1,
                                               skip_group_check=True)
                            if j == PER_ITEM - 1 and d == 0:
                                last.then_inc(y_half, 1)
                    last.then_inc(weights_used, 1)
                    if j == 2:
                        for tt in range(TT):
                            last = nc.tensor.transpose(bank(7)[0:CAP, tt * P:(tt + 1) * P], scatterP[:, tt, :], ident)
                        last.then_inc(sT_transposed, 1)
                    if kind == "gate" and half == 0 and c > 0:
                        turn_act(c - 1)
                    if j == PER_ITEM - 3:
                        turn_act(CHUNKS - 1)
                        pe.wait_ge(built, i + 2)
                        gather()
                pe.wait_ge(sT_ready, i + 1)
                pe.wait_ge(xe_ready, i * 2 + 4)
                for d in range(2):
                    for tt in range(TT):
                        if tt == 0:
                            pe.wait_ge((yt_act, yt_dve)[d], i + 1)
                        mm(bank(4 + 2 * tt + d), scatterT[0:CAP, tt * P:(tt + 1) * P],
                           ytok[0:CAP, d * 512:(d + 1) * 512], start=True, stop=True).then_inc(scattered, 1)

        @block.scalar
        def _(act):
            a = nc.scalar.activation
            own = Chain(act, act_own)

            def inverse_norm(n, inputs, own=own):
                for tt in range(TT):
                    act.wait_ge(*inputs[tt])
                    own(a(hn[:, tt, :], h[:, tt, :], ACT.Square, accum_out=ssq[:, tt:tt + 1]))
                    own(a(ssq[:, tt:tt + 1], ssq[:, tt:tt + 1], ACT.Ln, bias=eps, scale=1.0 / D))
                    a(rstd[:, tt:tt + 1], ssq[:, tt:tt + 1], ACT.Exp, scale=-0.5).then_inc(rstd_ready[n], 1)

            def used(n, t=0, per=0):
                act.wait_ge(weights_used, t * per + (n + 1 + PRIMED))

            def hi(n, t=0, per=0):
                back = distance(SPLIT_OF, n, per)
                if back:
                    used(n - back, t, per)
                after = landed(n + per) - landed(n) if per else 0
                act.wait_ge(slot_filled[RAW_OF[n]], t * after + landed(n))
                nc.scalar.copy(split[:, SPLIT_OF[n], 0, :], raw_of(n)).then_inc(hi_ready, 1)

            def hi_norm(n):
                for x, (dst, src, tt, q, b) in enumerate(NORM_PARTS[n]):
                    act.wait_ge(hn_transposed[n], x + 1)
                    nc.scalar.copy(dst[:, 0, 4 * q:4 * q + 4, tt * P:(tt + 1) * P],
                                   bank(b).rearrange("p (a b) -> p a b", a=4)).then_inc(hT_hi[n], 1)

            def hi_mixed(m, first):
                hi(first + 2)
                for y in range(2 * TT):
                    act.wait_ge(mixed_transposed[m], y + 1)
                    nc.scalar.copy(hT[:, 0, 4 * (y % 2):4 * (y % 2) + 4, (y // 2) * P:(y // 2 + 1) * P],
                                   bank(4 + y).rearrange("p (a b) -> p a b", a=4)).then_inc(mixedT_hi[m], 1)
                hi(first + 3)
                hi(first + 4)

            act.preload_act_table_set("natural_log_exp_and_others")
            act.wait_ge(consts_in, 16)
            inverse_norm(0, [(x_in[tt], 16) for tt in range(TT)])
            act.wait_ge(bounds_shifted, 1)
            a(lbound[:, 2:4, :], lbound[:, 2:4, :], ACT.Exp).then_inc(bounds_exp, 1)
            hi(HG)
            hi_norm(0)
            hi(HG + 1)

            def softplus(dst, src):
                own(a(dst, src, ACT.Abs))
                own(a(dst, dst, ACT.Exp, scale=-1.0))
                return a(dst, dst, ACT.Ln, bias=one)

            def decay_softplus(n, p=0, per=0):
                used(n, p, per)
                softplus(decay_in, bank(0).rearrange("p (a b) -> p a b", a=2)).then_inc(f_softplus, 1)

            def decay_sigmoid(p):
                act.wait_ge(f_logsig, p + 1)
                a(decay_in, decay_in, ACT.Exp).then_inc(f_sigmoid, 1)

            def head_pair(p):
                act.wait_ge(f_done, p + 1)
                a(logf, forget, ACT.Ln).then_inc(f_log, 1)
                hi(HG + 3, p, 4)
                act.wait_ge(b_done, p + 1)
                a(eb, bsum, ACT.Exp)
                a(enb, bsum, ACT.Exp, scale=-1.0).then_inc(b_exps, 1)
                act.wait_ge(bdiff_done, p + 1)
                a(eend, bdiff, ACT.Exp).then_inc(bend_exp, 1)
                used(HG + 2, p, 4)
                nc.scalar.copy(v_hg, bank(2).rearrange("p (a b) -> p a b", a=2)).then_inc(v_copied, 1)
                hi(HG + 4, p, 4)
                act.wait_ge(kend_transposed, p + 1)
                nc.scalar.copy(kend_tok, bank(4).rearrange("p (a b c) -> p a b c", a=2, b=TT)).then_inc(kend_copied, 1)
                used(HG + 3, p, 4)
                softplus(gate_hg, bank(3).rearrange("p (a b) -> p a b", a=2)).then_inc(g_softplus, 1)
                hi(HG + 5, p, 4)
                act.wait_ge(g_logsig, p + 1)
                a(gate_hg, gate_hg, ACT.Exp).then_inc(g_sigmoid, 1)

            def squares(p):
                act.wait_ge(o_ready, p + 1)
                a(square_hg, bank(4).rearrange("p (a b) -> p a b", a=2), ACT.Square).then_inc(o_squared, 1)

            decay_softplus(HG)
            hi(HG + 2)
            decay_sigmoid(0)
            with act.Fori(0, 3) as p:
                own.enter(p, 4)
                head_pair(p)
                decay_softplus(HG + 4, p, 4)
                squares(p)
                hi(HG + 6, p, 4)
                decay_sigmoid(p + 1)
            own.leave(3)
            head_pair(3)
            squares(3)
            act.wait_ge(o_gated, 5)
            own(a(orstd[:, :, :, :], ossq[:, :, :, :], ACT.Ln, bias=eps, scale=1.0 / P))
            a(orstd[:, :, :, :], orstd[:, :, :, :], ACT.Exp, scale=-0.5).then_inc(orstd_ready, 1)
            hi_mixed(0, HG_OUT)
            inverse_norm(1, [(h_ready[1], 2), (h_ready[1], 4)])
            hi_norm(1)
            hi(FF + 1)

            act.preload_act_table_set("silu_and_others")
            hi(FF + 2)
            used(FF)
            a(silu_ff, bank(4).rearrange("p (a b) -> p a b", a=2), ACT.Silu).then_inc(ff_silu, 1)
            hi(FF + 3)
            with act.Fori(0, FF_PAIRS - 2) as t:
                hi(FF + 4, t, 3)
                used(FF + 2, t, 3)
                act.wait_ge(ff_act, t + 1)
                a(silu_ff, bank(4).rearrange("p (a b) -> p a b", a=2), ACT.Silu).then_inc(ff_silu, 1)
                hi(FF + 5, t, 3)
                hi(FF + 6, t, 3)
            hi(AT - 2)
            used(AT - 4)
            act.wait_ge(ff_act, FF_PAIRS - 1)
            a(silu_ff, bank(4).rearrange("p (a b) -> p a b", a=2), ACT.Silu).then_inc(ff_silu, 1)
            hi(AT - 1)
            hi(AT)
            act.preload_act_table_set("natural_log_exp_and_others")
            inverse_norm(2, [(h_ready[2], 2), (h_ready[2], 4)])
            hi_norm(2)
            hi(AT + 1)

            with act.Fori(0, GROUPS) as g:
                for j in range(2 * NBR + 1):
                    hi(AT + 2 + j, g, 9)

                def exps(u):
                    act.wait_ge(max_ready, g * UNITS + (u + 1))
                    a(prob[u % 2], prob[u % 2], ACT.Exp, bias=negmax[:, u:u + 1], scale=SCALE,
                      accum_out=rowsum[:, u:u + 1]).then_inc(exp_ready, 1)

                def value_copy(b):
                    used(AT + 2 * NBR + b, g, 9)
                    nc.scalar.copy(vbuf[:, :, b, :], bank(b % 2).rearrange("p (a b) -> p a b", a=TT)).then_inc(va_copied, 1)

                value_copy(0)
                hi(AT + 9, g, 9)
                value_copy(1)
                hi(AT + 10, g, 9)
                exps(0)
                exps(1)
                value_copy(2)
                for u in range(2, UNITS + 1):
                    if u < UNITS:
                        exps(u)
                    if u % 2 == 0:
                        act.wait_ge(pT_ready, g * UNITS + u)
                        nc.scalar.copy(probT[1][:, 0:4, :], bank(5).rearrange("p (a b) -> p a b", a=4)).then_inc(pT_act, 1)
            hi_mixed(1, AT_OUT)
            inverse_norm(3, [(h_ready[3], 2), (h_ready[3], 4)])
            for x, (dst, src, tt, q, b) in enumerate(NORM_PARTS[3]):
                act.wait_ge(hn_transposed[3], x + 1)
                nc.scalar.copy(hT_router[:, 4 * q:4 * q + 4, tt * P:(tt + 1) * P],
                               bank(b).rearrange("p (a b) -> p a b", a=4)).then_inc(hT_ready[3], 1)
            hi(MOE + 1)

            act.wait_ge(shifted, 1)
            a(probs, probs, ACT.Exp).then_inc(exped, 1)
            hi(MOE + 2)

            act.preload_act_table_set("silu_and_others")
            act.wait_ge(table_ready, 1)
            items = act.value_load(table[0:1, EXTRA + 2:EXTRA + 3], min_val=NEXP, max_val=NEXP + EXTRA)

            def tokens_hi(i):
                for q in range(2):
                    act.wait_ge(gathered, i * 2 + (q + 1))
                    nc.scalar.copy(xeT[:, 0, 4 * q:4 * q + 4, :],
                                   bank(5 + q)[:, 0:4 * CAP].rearrange("p (a b) -> p a b", a=4)).then_inc(xe_hi, 1)

            def actT_round(c, i):
                act.wait_ge(act_turned, i * CHUNKS + (c + 1))
                nc.scalar.copy(actT[:, 0, :, :], bank(4)[:, 0:4 * CAP].rearrange("p (a b) -> p a b", a=4)).then_inc(actT_hi, 1)

            tokens_hi(0)
            with act.Fori(0, items) as i:
                for j in range(1, PER_ITEM):
                    kind, c, half = MOE_LOADS[j - 1]
                    if kind == "gate" and half == 1:
                        used(MOE + j - 1, i, PER_ITEM)
                        a(silu_e[0:CAP, :], bank(0)[0:CAP, :], ACT.Silu).then_inc(silu_done, 1)
                    if kind == "gate" and half == 0 and c > 0:
                        actT_round(c - 1, i)
                    if j == PER_ITEM - 2:
                        actT_round(CHUNKS - 1, i)
                    hi(MOE + j + 2, i, PER_ITEM)
                    if j == PER_ITEM - 2:
                        tokens_hi(i + 1)
                act.wait_ge(y_half, i + 1)
                nc.scalar.copy(ytok[0:CAP, 0:512], bank(2)[0:CAP, :]).then_inc(yt_act, 1)
                hi(MOE + PER_ITEM + 2, i, PER_ITEM)
            act.preload_act_table_set("natural_log_exp_and_others")
            inverse_norm(4, [(added[tt], items * 2) for tt in range(TT)], own=Chain(act, act_own_end))

        @block.vector
        def _(dve):
            v = nc.vector
            own = Chain(dve, dve_own)

            def wide(ap, n):
                return ap.unsqueeze(len(ap.shape)).to_broadcast(list(ap.shape) + [n])

            def two(ap):
                return ap.unsqueeze(1).to_broadcast([ap.shape[0], 2, ap.shape[1]])

            def used(n, t=0, per=0):
                dve.wait_ge(weights_used, t * per + (n + 1 + PRIMED))

            def lo(n, t=0, per=0):
                s = SPLIT_OF[n]
                dve.wait_ge(hi_ready, t * per + (n + 1))
                v.tensor_tensor(split[:, s, 1, :], raw_of(n), split[:, s, 0, :].bitcast(F32),
                                ALU.subtract).then_inc(split_ready, 1)

            def scale_norm(n, rows):
                for tt in range(TT):
                    dve.wait_ge(rstd_ready[n], tt + 1)
                    for dst, row, use in rows:
                        dve.wait_ge(gain_in[row], 16 * use)
                        for q in range(2):
                            c = slice(512 * q, 512 * (q + 1))
                            v.scalar_tensor_tensor(out=dst[:, tt, c], in0=h[:, tt, c], scalar=rstd[:, tt:tt + 1],
                                                   in1=gain[:, row, c], op0=ALU.mult, op1=ALU.mult).then_inc(hn_ready[n], 1)

            def lo_norm(n):
                for x, (dst, src, tt, q, b) in enumerate(NORM_PARTS[n]):
                    dve.wait_ge(hT_hi[n], x + 1)
                    to = dst[:, :, 4 * q:4 * q + 4, tt * P:(tt + 1) * P]
                    v.tensor_tensor(to[:, 1], bank(b).rearrange("p (a b) -> p a b", a=4), to[:, 0].bitcast(F32),
                                    ALU.subtract).then_inc(hT_ready[n], 1)

            def mixer_output(m, n, first):
                for y in range(2 * TT):
                    q, c = slice(4 * (y % 2), 4 * (y % 2) + 4), slice((y // 2) * P, (y // 2 + 1) * P)
                    dve.wait_ge(mixedT_hi[m], y + 1)
                    v.tensor_tensor(hT[:, 1, q, c], bank(4 + y).rearrange("p (a b) -> p a b", a=4),
                                    hT[:, 0, q, c].bitcast(F32), ALU.subtract).then_inc(mixedT_ready[m], 1)
                lo(first + 2)
                lo(first + 3)
                lo(first + 4)
                residual(n, proj_out[m], first + 3)

            def residual(n, first_done, last_load):
                for j in range(4):
                    tt, half = j // 2, j % 2
                    if j == 0:
                        dve.wait_ge(first_done, 1)
                    if j == 2:
                        used(last_load)
                    piece = h[:, tt, half * 512:(half + 1) * 512]
                    v.tensor_tensor(piece, piece, bank(j), ALU.add).then_inc(h_ready[n], 1)

            dve.wait_ge(params_in, 16)
            own(v.tensor_tensor(lbound[:, 0, :], bounds[:, 0, :], bounds[:, 1, :], ALU.max))
            v.tensor_tensor(lbound[:, 2:4, :], bounds, two(lbound[:, 0, :]), ALU.subtract).then_inc(bounds_shifted, 1)
            scale_norm(0, [(hn, 0, 1)])
            dve.wait_ge(bounds_exp, 1)
            own(v.tensor_tensor(lbound[:, 0, :], lbound[:, 2, :], lbound[:, 3, :], ALU.add))
            own(v.reciprocal(lbound[:, 1, :], lbound[:, 0, :]))
            own(v.tensor_tensor(lbound[:, 2, :], lbound[:, 2, :], lbound[:, 1, :], ALU.mult))
            v.tensor_scalar(lbound[:, 3, :], lbound[:, 2, :], -1.0, 1.0, ALU.mult, ALU.add).then_inc(o_gated, 1)
            dve.wait_ge(o_gated, 1)
            lo(HG)
            lo_norm(0)
            lo(HG + 1)
            dve.wait_ge(tables_in, 16)

            flat = "p a b -> p (a b)"
            mask = cc("hgmask").bitcast(U32)
            with dve.Fori(0, 4) as p:
                own.enter(p, 4)
                dve.wait_ge(f_softplus, p + 1)
                v.scalar_tensor_tensor(out=decay_in, in0=bank(0).rearrange("p (a b) -> p a b", a=2), scalar=0.0, in1=decay_in,
                                       op0=ALU.min, op1=ALU.subtract).then_inc(f_logsig, 1)
                lo(HG + 2, p, 4)
                dve.wait_ge(f_sigmoid, p + 1)
                for hh in range(2):
                    last = v.tensor_scalar(forget[:, hh, :], decay_in[:, hh, :], lbound[:, 3, bass.ds(p * 2 + hh, 1)],
                                           lbound[:, 2, bass.ds(p * 2 + hh, 1)], ALU.mult, ALU.add)
                last.then_inc(f_done, 1)
                dve.wait_ge(f_done, p + 1)
                v.tensor_scalar(keyk, forget, -1.0, 1.0, ALU.mult, ALU.add)
                dve.wait_ge(f_log, p + 1)
                v.tensor_tensor_scan(bsum.rearrange(flat), cc("reset"), logf.rearrange(flat), 0.0,
                                     ALU.mult, ALU.add).then_inc(b_done, 1)
                dve.wait_ge(b_done, p + 1)
                chunks = bsum.rearrange("p a (n c) -> p (a n) c", c=CHUNK)
                v.tensor_tensor(bdiff.rearrange("p a (n c) -> p (a n) c", c=CHUNK),
                                chunks[:, :, CHUNK - 1:CHUNK].to_broadcast([P, 2 * S // CHUNK, CHUNK]), chunks,
                                ALU.subtract).then_inc(bdiff_done, 1)
                lo(HG + 3, p, 4)
                dve.wait_ge(b_exps, p + 1)
                used(HG + 1, p, 4)
                v.tensor_tensor(qdec, bank(1).rearrange("p (a b) -> p a b", a=2), eb, ALU.mult)
                v.tensor_tensor(kdec, keyk, enb, ALU.mult).then_inc(decayed, 1)
                dve.wait_ge(bend_exp, p + 1)
                v.tensor_tensor(kend, keyk, eend, ALU.mult).then_inc(decayed, 1)
                lo(HG + 4, p, 4)
                dve.wait_ge(g_softplus, p + 1)
                v.scalar_tensor_tensor(out=gate_hg, in0=bank(3).rearrange("p (a b) -> p a b", a=2), scalar=0.0, in1=gate_hg,
                                       op0=ALU.min, op1=ALU.subtract).then_inc(g_logsig, 1)
                dve.wait_ge(zeroed, 1)
                dve.wait_ge(scores_hg_ready, p + 1)
                v.copy_predicated(scores_hg.rearrange("p a b c -> p (a b) c"),
                                  mask.unsqueeze(1).to_broadcast([P, 4, P]),
                                  bank(5).rearrange("p (a c) -> p a c", a=4)).then_inc(scores_hg_masked, 1)
                dve.wait_ge(kv_ready, p + 1)
                own(v.tensor_copy(states[:, :, 0, :], bank(6).rearrange("p (a b) -> p a b", a=2)[:, :, 0:P]))
                for n in (1, 2):
                    for hh in range(2):
                        last = v.scalar_tensor_tensor(out=states[:, hh, n, :], in0=states[:, hh, n - 1, :],
                                                      scalar=eb[:, hh, (n + 1) * CHUNK - 1:(n + 1) * CHUNK],
                                                      in1=chunk_kv(hh, n), op0=ALU.mult, op1=ALU.add)
                    if n == 1:
                        own(last)
                last.then_inc(states_ready, 1)
                dve.wait_ge(g_sigmoid, p + 1)
                own(v.tensor_tensor(gate_hg, bank(3).rearrange("p (a b) -> p a b", a=2), gate_hg, ALU.mult))
                g4 = gate_hg.rearrange("p a (b c) -> p (a b) c", b=2)
                own(v.tensor_tensor(g4, g4, pp("out_norm").unsqueeze(1).to_broadcast([P, 4, P]), ALU.mult))
                lo(HG + 5, p, 4)
                dve.wait_ge(o_squared, p + 1)
                v.tensor_reduce(ossq[:, bass.ds(p, 1), :, :].rearrange("p x a b -> p (x a b)"),
                                square_hg.rearrange("p a (b c) -> p (a b) c", b=2), AX.X, ALU.add)
                v.tensor_tensor(mixed[:, :, bass.ds(p * 256, 256)], bank(4).rearrange("p (a b) -> p a b", a=2), gate_hg,
                                ALU.mult).then_inc(o_gated, 1)
            own.leave(4)
            dve.wait_ge(orstd_ready, 1)
            for tt in range(TT):
                for hh in range(2):
                    m4 = mixed[:, tt, :].rearrange("p (a b c) -> p a b c", a=4, b=2)[:, :, hh, :]
                    last = v.tensor_tensor(m4, m4, wide(orstd[:, :, tt, hh], P), ALU.mult)
                last.then_inc(mixed_ready, 1)
            mixer_output(0, 1, HG_OUT)
            scale_norm(1, [(hn, 1, 1)])
            lo_norm(1)
            lo(FF + 1)

            def ff_activation(n, i, t=0, per=0, buf=0):
                dve.wait_ge(ff_silu, i + 1)
                used(n, t, per)
                own(v.tensor_tensor(act_ff, silu_ff, bank(5).rearrange("p (a b) -> p a b", a=2), ALU.mult))
                own(v.tensor_copy(act_ff_hl[:, buf, 0, :, :], act_ff))
                v.tensor_tensor(act_ff_hl[:, buf, 1, :, :], act_ff, act_ff_hl[:, buf, 0, :, :].bitcast(F32),
                                ALU.subtract).then_inc(ff_act, 1)

            lo(FF + 2)
            lo(FF + 3)
            ff_activation(FF + 1, 0)
            with dve.Fori(0, FF_PAIRS - 2) as t:
                own.enter(t, 2)
                lo(FF + 4, t, 3)
                lo(FF + 5, t, 3)
                lo(FF + 6, t, 3)
                ff_activation(FF + 4, t + 1, t, 3)
            own.leave(FF_PAIRS - 2)
            lo(AT - 2)
            lo(AT - 1)
            ff_activation(AT - 3, FF_PAIRS - 1, buf=1)
            lo(AT)
            residual(2, ff_sum, AT - 1)
            scale_norm(2, [(hn, 0, 2), (hn_kv, 1, 2)])
            lo_norm(2)
            lo(AT + 1)

            cos, sin = cc("cos"), cc("sin")
            def rope(j, n, g=0, per=0):
                buf = (kbuf + qbuf)[j]
                src = bank(j % 2).rearrange("p (a b) -> p a b", a=2)
                used(n, g, per)
                v.tensor_tensor(buf, src, two(cos), ALU.mult)
                if j:
                    dve.wait_ge(rope_done, g * 6 + j)
                for q in range(4):
                    a, b = 32 * q, 32 * (q ^ 1)
                    last = v.tensor_tensor(rot[b:b + 32], src[a:a + 32], two(sin[a:a + 32, :]), ALU.mult)
                last.then_inc(kq_read, 1)

            def head_group(g, more):
                def row_max(u):
                    qt = u % 2
                    n = NBR * P * (qt + 1)
                    dve.wait_ge(s_ready, g * UNITS + (u + 1))
                    v.memset(negmax[:, u:u + 1], 0.0)
                    own(v.tensor_tensor_reduce(prob[qt], ps[:, 512 * (2 + qt):512 * (2 + qt) + n], cc(f"mask{qt}"), 1.0, -3e38,
                                               ALU.add, ALU.max, rowmax[:, u:u + 1]))
                    v.tensor_scalar(negmax[:, u:u + 1], rowmax[:, u:u + 1], -SCALE, None, ALU.mult).then_inc(max_ready, 1)

                def turned(u):
                    dve.wait_ge(pT_ready, g * UNITS + (u + 1))
                    if u % 2 == 0:
                        dst, src = probT[0], bank(1)[:, 0:NBR * P]
                    else:
                        dst, src = probT[1][:, 4:6, :], bank(6)[:, 0:2 * P]
                    v.tensor_copy(dst, src.rearrange("p (a b) -> p a b", b=P)).then_inc(pT_dve, 1)

                def output(u):
                    hd, qt = u // 2, u % 2
                    dve.wait_ge(pv_ready, g * UNITS + (u + 1))
                    own(v.reciprocal(rowinv[:, u:u + 1], rowsum[:, u:u + 1]))
                    v.tensor_scalar(mixed[:, qt, bass.ds(g * 256 + hd * HEAD, HEAD)], bank(7)[:, 0:HEAD], rowinv[:, u:u + 1],
                                    None, ALU.mult).then_inc(o_evac, 1)

                lo(AT + 2, g, 9)
                for j in range(1, 2 * NBR):
                    lo(AT + 2 + j, g, 9)
                    rope(j, AT + j, g, 9)
                lo(AT + 2 + 2 * NBR, g, 9)
                lo(AT + 9, g, 9)
                for u in range(UNITS + 2):
                    if u < UNITS:
                        row_max(u)
                    if u == 1:
                        lo(AT + 10, g, 9)
                    if 1 <= u < UNITS + 1:
                        turned(u - 1)
                    if u >= 2:
                        output(u - 2)
                if more:
                    rope(0, AT + 9, g, 9)

            rope(0, AT)
            with dve.Fori(0, GROUPS - 1) as g:
                own.enter(g, 2 * UNITS)
                head_group(g, True)
            own.leave(GROUPS - 1)
            head_group(GROUPS - 1, False)
            mixer_output(1, 3, AT_OUT)
            scale_norm(3, [(hn, 0, 3)])
            lo(MOE + 1)

            experts = cc("experts")
            lg = bank(0)[:, 0:TT * NEXP].rearrange("p (t e) -> p t e", t=TT)
            dve.wait_ge(logits_ready, 1)
            own(v.tensor_reduce(r1[:, 0:2], lg, AX.X, ALU.max))
            v.tensor_tensor(probs, lg, wide(r1[:, 0:2], NEXP), ALU.subtract).then_inc(shifted, 1)
            dve.wait_ge(exped, 1)
            own(v.tensor_reduce(r1[:, 2:4], probs, AX.X, ALU.add))
            own(v.reciprocal(r1[:, 4:6], r1[:, 2:4]))
            own(v.tensor_tensor(probs, probs, wide(r1[:, 4:6], NEXP), ALU.mult))
            for tt in range(TT):
                last = v.max(top[:, tt, :], probs[:, tt, :])
            own(last)
            for tt in range(TT):
                last = v.max_index(topi[:, tt, :], top[:, tt, :], probs[:, tt, :])
            own(last)
            own(v.tensor_copy(topf, topi))
            for tt in range(TT):
                v.tensor_scalar(onehot[:, tt, :], experts, topf[:, tt, 0:1], None, ALU.is_equal)
                last = v.tensor_scalar(chosen[:, tt, :], experts, topf[:, tt, 1:2], None, ALU.is_equal)
            own(last)
            v.tensor_tensor(chosen, chosen, onehot, ALU.add).then_inc(chosen_ready, 1)
            own(v.tensor_tensor(r1[:, 0:2], top[:, :, 0], top[:, :, 1], ALU.add))
            own(v.reciprocal(r1[:, 2:4], r1[:, 0:2]))
            own(v.tensor_tensor(top[:, :, 0:2], top[:, :, 0:2], wide(r1[:, 2:4], 2), ALU.mult))
            for tt in range(TT):
                v.tensor_scalar(wa[:, tt, :], experts, topf[:, tt, 0:1], top[:, tt, 0:1], ALU.is_equal, ALU.mult)
                last = v.tensor_scalar(place[:, tt, :], experts, topf[:, tt, 1:2], top[:, tt, 1:2], ALU.is_equal, ALU.mult)
            own(last)
            v.memset(key[:, ITEMS - 1, :], ABSENT)
            v.memset(weight[:, ITEMS - 1, :], 0.0)
            w8 = weight[:, 0:NEXP, :].rearrange("p e t -> p t e")
            k8 = key[:, 0:NEXP, :].rearrange("p e t -> p t e")
            own(v.tensor_tensor(w8, wa, place, ALU.add))
            dve.wait_ge(places_ready, 1)
            dve.wait_ge(chosen_ready, 1)
            own(v.tensor_scalar(place, bank(1)[:, 0:TT * NEXP].rearrange("p (t e) -> p t e", t=TT), -ABSENT, None, ALU.add))
            own(v.tensor_copy(counts, bank(1)[:, TT * NEXP:(TT + 1) * NEXP]))
            own(v.tensor_tensor(place, place, chosen, ALU.mult))
            own(v.tensor_scalar(k8, place, ABSENT, None, ALU.add))

            def build(i, chain):
                chain(v.tensor_tensor(gatherP, cc("places").unsqueeze(1).to_broadcast([P, TT, CAP]),
                                      wide(key[:, bass.ds(i, 1), :].rearrange("p x t -> p (x t)"), CAP), ALU.is_equal))
                v.tensor_tensor(scatterP, gatherP, wide(weight[:, bass.ds(i, 1), :].rearrange("p x t -> p (x t)"), CAP),
                                ALU.mult).then_inc(built, 1)

            build(0, own)
            lo(MOE + 2)
            base3 = cc("over_base").rearrange("p (b e) -> p b e", b=BLOCKS)

            def over(ap):
                return ap.unsqueeze(1).to_broadcast([P, BLOCKS, NEXP])

            def each(ap):
                return ap.unsqueeze(1).to_broadcast([P, EXTRA, nj])

            own(v.tensor_tensor(active.rearrange("p (b e) -> p b e", b=BLOCKS), over(counts), base3, ALU.is_gt))
            own(v.tensor_tensor_scan(order, cc("ones")[:, 0:nj], active, 0.0, ALU.mult, ALU.add))
            v.tensor_reduce(tablef[:, EXTRA + 1:EXTRA + 2], active, AX.X, ALU.add)
            v.memset(tablef[:, EXTRA:EXTRA + 1], 1.0)
            own(v.tensor_tensor(order, order, active, ALU.subtract))
            own(v.tensor_scalar(order, order, -ABSENT, None, ALU.add))
            own(v.tensor_tensor(order, order, active, ALU.mult))
            own(v.tensor_scalar(order, order, ABSENT, None, ALU.add))
            own(v.tensor_tensor(sel, each(order), cc("over_k").rearrange("p (k j) -> p k j", k=EXTRA), ALU.is_equal))
            own(v.tensor_tensor(prod, sel, each(cc("over_e")), ALU.mult))
            v.tensor_scalar(tablef[:, EXTRA + 2:EXTRA + 3], tablef[:, EXTRA + 1:EXTRA + 2], float(NEXP), None, ALU.add)
            own(v.tensor_reduce(tablef[:, 0:EXTRA], prod, AX.X, ALU.add))
            own(v.tensor_scalar(tablef[:, 0:EXTRA], tablef[:, 0:EXTRA], 1.0, None, ALU.max))
            v.tensor_copy(table[:, :], tablef).then_inc(table_ready, 1)

            def tokens_lo(i):
                for q in range(2):
                    dve.wait_ge(xe_hi, i * 2 + (q + 1))
                    v.tensor_tensor(xeT[:, 1, 4 * q:4 * q + 4, :], bank(5 + q)[:, 0:4 * CAP].rearrange("p (a b) -> p a b", a=4),
                                    xeT[:, 0, 4 * q:4 * q + 4, :].bitcast(F32), ALU.subtract).then_inc(xe_ready, 1)

            def actT_rest(c, i):
                dve.wait_ge(actT_hi, i * CHUNKS + (c + 1))
                v.tensor_tensor(actT[:, 1, :, :], bank(4)[:, 0:4 * CAP].rearrange("p (a b) -> p a b", a=4),
                                actT[:, 0, :, :].bitcast(F32), ALU.subtract).then_inc(actT_ready, 1)

            tokens_lo(0)
            for tt in range(TT):
                k3 = keymod[:, tt, :].rearrange("p (b e) -> p b e", b=BLOCKS)
                own(v.tensor_tensor(k3, over(key[:, 0:NEXP, tt]), base3, ALU.subtract))
                own(v.tensor_tensor(prod, sel, each(keymod[:, tt, :]), ALU.mult))
                own(v.tensor_reduce(key[:, NEXP:NEXP + EXTRA, tt], prod, AX.X, ALU.add))
                own(v.tensor_copy(k3, over(weight[:, 0:NEXP, tt])))
                own(v.tensor_tensor(prod, sel, each(keymod[:, tt, :]), ALU.mult))
                own(v.tensor_reduce(weight[:, NEXP:NEXP + EXTRA, tt], prod, AX.X, ALU.add))
            dve.wait_ge(table_ready, 1)
            items = dve.value_load(table[0:1, EXTRA + 2:EXTRA + 3], min_val=NEXP, max_val=NEXP + EXTRA)
            with dve.Fori(0, items) as i:
                own.enter(i, 1)
                for j in range(1, PER_ITEM):
                    kind, c, half = MOE_LOADS[j - 1]
                    if kind == "up" and half == 1:
                        dve.wait_ge(silu_done, i * CHUNKS + (c + 1))
                        used(MOE + j - 1, i, PER_ITEM)
                        v.tensor_tensor(act_e[0:CAP, :], silu_e[0:CAP, :], bank(1)[0:CAP, :], ALU.mult).then_inc(act_done, 1)
                    if kind == "gate" and half == 0 and c > 0:
                        actT_rest(c - 1, i)
                    if j == PER_ITEM - 2:
                        actT_rest(CHUNKS - 1, i)
                    lo(MOE + j + 2, i, PER_ITEM)
                    if j == PER_ITEM - 2:
                        tokens_lo(i + 1)
                    if j == 9:
                        dve.wait_ge(sT_transposed, i + 1)
                        v.tensor_copy(scatterT[0:CAP, :], bank(7)[0:CAP, 0:S]).then_inc(sT_ready, 1)
                        build(i + 1, own)
                used(MOE + PER_ITEM - 1, i, PER_ITEM)
                v.tensor_copy(ytok[0:CAP, 512:1024], bank(3)[0:CAP, :]).then_inc(yt_dve, 1)
                for j in range(4):
                    half, tt = j // 2, j % 2
                    dve.wait_ge(scattered, i * 4 + (j + 1))
                    piece = h[:, tt, half * 512:(half + 1) * 512]
                    v.tensor_tensor(piece, piece, bank(4 + 2 * tt + half), ALU.add).then_inc(added[tt], 1)
                lo(MOE + PER_ITEM + 2, i, PER_ITEM)

            dve.wait_ge(gain_in[1], 16 * 3)
            for tt in range(TT):
                dve.wait_ge(rstd_ready[4], tt + 1)
                v.scalar_tensor_tensor(out=hn[:, tt, :], in0=h[:, tt, :], scalar=rstd[:, tt:tt + 1], in1=gain[:, 1, :],
                                       op0=ALU.mult, op1=ALU.mult).then_inc(normed, 1)

        @block.gpsimd
        def _(pool):
            nc.gpsimd.memset(scores_hg, 0.0).then_inc(zeroed, 1)
            with pool.Fori(0, GROUPS) as g:
                for j in range(2 * NBR):
                    buf = (kbuf + qbuf)[j]
                    pool.wait_ge(kq_read, g * 6 + (j + 1))
                    nc.gpsimd.tensor_tensor(buf, buf, rot, ALU.add).then_inc(rope_done, 1)


_INS = ["x", "hgrn_w_in", "hgrn_w_out", "w_kv", "dil_w_q", "dil_w_out", "ffn_w_gate", "ffn_w_up", "ffn_w_down",
        "moe_w_gate", "moe_w_up", "moe_w_down"]


def kernel(**inputs):
    import concourse.bacc as bacc
    from concourse.bass_utils import run_bass_kernel_spmd

    def rows(*a):
        return np.broadcast_to(np.stack([np.asarray(r) for r in a])[None], (P, len(a), D))

    def per_partition(a):
        a = np.asarray(a).reshape(-1, KT, P)
        return np.moveaxis(a, 2, 0).reshape(P, -1)

    router = np.asarray(inputs["moe_w_router"])[0].reshape(KT, P, NEXP)
    parts = {
        "bounds": per_partition(inputs["hgrn_lower_bounds"]),
        "router": np.moveaxis(router, 1, 0).reshape(P, -1),
        "out_norm": np.broadcast_to(np.asarray(inputs["hgrn_out_norm"])[0], (P, P)),
    }
    arrays = {name: np.ascontiguousarray(inputs[name]) for name in _INS}
    attn_norm, ffn_norm = inputs["attn_norm"], inputs["ffn_norm"]
    arrays["gains"] = np.ascontiguousarray(rows(attn_norm[0], ffn_norm[0], attn_norm[1], inputs["kv_norm"],
                                                ffn_norm[1], inputs["final_norm"]))
    arrays["consts"] = constants()
    arrays["params"] = np.ascontiguousarray(np.concatenate([parts[n] for n in PARAMS], 1))
    nc = bacc.Bacc("TRN2", target_bir_lowering=False, num_devices=1)
    aps = {n: nc.dram_tensor(f"in_{n}", a.shape, mybir.dt.from_np(a.dtype), kind="ExternalInput").ap()
           for n, a in arrays.items()}
    out = nc.dram_tensor("out", (1, S, D), F32, kind="ExternalOutput").ap()
    trunk_kernel(nc, aps, out)
    r = run_bass_kernel_spmd(nc, [{f"in_{n}": a for n, a in arrays.items()}], core_ids=[0])
    return r.results[0]["out"]
```
